# Optimizing a Trainium2 kernel written in Bass

```python
import math
import jax
import jax.numpy as jnp
from jax import lax
import numpy as np
import jax, jax.numpy as jnp

D_MODEL = 1024
BATCH = 1
SEQ = 256
DEPTH = 2

N_A_LAYERS = DEPTH // 2
N_B_LAYERS = DEPTH - N_A_LAYERS
EPS = 1e-6
NEG_INF = -1e30

GDN_QK_HEADS = 8
GDN_V_HEADS = 16
GDN_HEAD_DIM = 128
GDN_QK_DIM = GDN_QK_HEADS * GDN_HEAD_DIM
GDN_V_DIM = GDN_V_HEADS * GDN_HEAD_DIM
GDN_CONV_DIM = 2 * GDN_QK_DIM + GDN_V_DIM
GDN_IN_DIM = GDN_CONV_DIM + GDN_V_DIM + 2 * GDN_V_HEADS
GDN_CONV_WIDTH = 4
GDN_CHUNK = 64

SWA_Q_HEADS = 16
SWA_KV_HEADS = 4
SWA_GROUP = SWA_Q_HEADS // SWA_KV_HEADS
SWA_HEAD_DIM = 64
SWA_WINDOW = 128
SWA_BLOCK = 128

REL_BUCKETS = 32
REL_MAX_DISTANCE = 128

D_FF = 2816
FFN_CONV_WIDTH = 3


def rmsnorm(x, w):
    xf = x.astype(jnp.float32)
    y = xf * lax.rsqrt(jnp.mean(xf * xf, axis=-1, keepdims=True) + EPS)
    return (y * w.astype(jnp.float32)).astype(x.dtype)

def l2norm(x):
    return x * lax.rsqrt(jnp.sum(x * x, axis=-1, keepdims=True) + EPS)

def causal_dwconv(x, w, b=None):
    width = w.shape[0]
    t = x.shape[1]
    xp = jnp.pad(x, ((0, 0), (width - 1, 0), (0, 0)))
    y = sum(xp[:, j:j + t] * w[j] for j in range(width))
    return y if b is None else y + b

def chunked_gated_delta_rule(q, k, v, g, beta):
    bsz, t, h, dk = q.shape
    dv = v.shape[-1]
    c = GDN_CHUNK
    n = t // c
    f32 = jnp.float32
    q = q.astype(f32).reshape(bsz, n, c, h, dk).transpose(0, 1, 3, 2, 4)
    k = k.astype(f32).reshape(bsz, n, c, h, dk).transpose(0, 1, 3, 2, 4)
    v = v.astype(f32).reshape(bsz, n, c, h, dv).transpose(0, 1, 3, 2, 4)
    g = g.astype(f32).reshape(bsz, n, c, h).transpose(0, 1, 3, 2)
    beta = beta.astype(f32).reshape(bsz, n, c, h).transpose(0, 1, 3, 2)

    gc = jnp.cumsum(g, axis=-1)
    tril = jnp.tril(jnp.ones((c, c), dtype=bool))
    strict = jnp.tril(jnp.ones((c, c), dtype=bool), -1)
    diff = gc[..., :, None] - gc[..., None, :]
    decay = jnp.where(tril, jnp.exp(jnp.where(tril, diff, 0.0)), 0.0)

    k_beta = k * beta[..., None]
    v_beta = v * beta[..., None]
    m = jnp.where(strict, jnp.einsum('bnhcd,bnhsd->bnhcs', k_beta, k) * decay, 0.0)
    eye = jnp.broadcast_to(jnp.eye(c, dtype=f32), m.shape)
    t_mat = lax.linalg.triangular_solve(m + eye, eye, left_side=True, lower=True,
                                        unit_diagonal=True)
    u = jnp.einsum('bnhcs,bnhse->bnhce', t_mat, v_beta)
    w = jnp.einsum('bnhcs,bnhsd->bnhcd', t_mat, k_beta * jnp.exp(gc)[..., None])
    a_intra = jnp.einsum('bnhcd,bnhsd->bnhcs', q, k) * decay
    q_dec = q * jnp.exp(gc)[..., None]
    k_dec = k * jnp.exp(gc[..., -1:] - gc)[..., None]
    g_last = jnp.exp(gc[..., -1])

    def step(state, inp):
        w_i, u_i, qd_i, kd_i, a_i, gl_i = inp
        v_new = u_i - jnp.einsum('bhcd,bhde->bhce', w_i, state)
        o_i = (jnp.einsum('bhcd,bhde->bhce', qd_i, state)
               + jnp.einsum('bhcs,bhse->bhce', a_i, v_new))
        state = state * gl_i[..., None, None] + jnp.einsum('bhcd,bhce->bhde', kd_i, v_new)
        return state, o_i

    xs = tuple(jnp.moveaxis(z, 1, 0) for z in (w, u, q_dec, k_dec, a_intra, g_last))
    s0 = jnp.zeros((bsz, h, dk, dv), f32)
    _, o = lax.scan(step, s0, xs)
    return o.transpose(1, 0, 3, 2, 4).reshape(bsz, t, h, dv)

def gated_deltanet(hn, w_in, conv_w, a_log, dt_bias, out_norm_w, w_out):
    bsz, t, _ = hn.shape
    proj = hn @ w_in
    qkv, z, b, a = jnp.split(
        proj, [GDN_CONV_DIM, GDN_CONV_DIM + GDN_V_DIM, GDN_CONV_DIM + GDN_V_DIM + GDN_V_HEADS],
        axis=-1)
    qkv = jax.nn.silu(causal_dwconv(qkv, conv_w))
    q, k, v = jnp.split(qkv, [GDN_QK_DIM, 2 * GDN_QK_DIM], axis=-1)
    q = l2norm(q.reshape(bsz, t, GDN_QK_HEADS, GDN_HEAD_DIM)) * (GDN_HEAD_DIM ** -0.5)
    k = l2norm(k.reshape(bsz, t, GDN_QK_HEADS, GDN_HEAD_DIM))
    v = v.reshape(bsz, t, GDN_V_HEADS, GDN_HEAD_DIM)
    rep = GDN_V_HEADS // GDN_QK_HEADS
    q = jnp.repeat(q, rep, axis=2)
    k = jnp.repeat(k, rep, axis=2)
    beta = jax.nn.sigmoid(b.astype(jnp.float32))
    g = -jnp.exp(a_log.astype(jnp.float32)) * jax.nn.softplus(
        a.astype(jnp.float32) + dt_bias.astype(jnp.float32))
    o = chunked_gated_delta_rule(q, k, v, g, beta)
    z = z.reshape(bsz, t, GDN_V_HEADS, GDN_HEAD_DIM).astype(jnp.float32)
    o = rmsnorm(o, out_norm_w) * jax.nn.silu(z)
    return o.reshape(bsz, t, GDN_V_DIM).astype(hn.dtype) @ w_out

def shared_kv(h, kv_norm_w, w_kv):
    bsz, t, _ = h.shape
    kv = rmsnorm(h, kv_norm_w) @ w_kv
    k, v = jnp.split(kv, 2, axis=-1)
    shape = (bsz, t, SWA_KV_HEADS, SWA_HEAD_DIM)
    return k.reshape(shape), v.reshape(shape)

def t5_bucket(dist):
    n = jnp.maximum(dist, 0)
    max_exact = REL_BUCKETS // 2
    nf = jnp.maximum(n, 1).astype(jnp.float32)
    large = max_exact + (jnp.log(nf / max_exact) / math.log(REL_MAX_DISTANCE / max_exact)
                         * (REL_BUCKETS - max_exact)).astype(jnp.int32)
    large = jnp.minimum(large, REL_BUCKETS - 1)
    return jnp.where(n < max_exact, n, large)

def band_bias_and_mask(rel_table, nb):
    qi = jnp.arange(SWA_BLOCK)[:, None]
    ki = jnp.arange(2 * SWA_BLOCK)[None, :]
    dist = qi + SWA_BLOCK - ki
    bias = rel_table.astype(jnp.float32)[t5_bucket(dist)]
    bias = jnp.transpose(bias, (2, 0, 1)).reshape(
        SWA_KV_HEADS, SWA_GROUP, SWA_BLOCK, 2 * SWA_BLOCK)
    in_window = (dist >= 0) & (dist < SWA_WINDOW)
    key_pos = jnp.arange(nb)[:, None, None] * SWA_BLOCK + ki[None] - SWA_BLOCK
    mask = in_window[None] & (key_pos >= 0)
    return bias, mask

def sliding_window_sink_attention(hn, k, v, w_q, sinks, w_o, bias, mask):
    bsz, t, _ = hn.shape
    nb = t // SWA_BLOCK
    q = (hn @ w_q).reshape(bsz, nb, SWA_BLOCK, SWA_KV_HEADS, SWA_GROUP, SWA_HEAD_DIM)
    q = q * (SWA_HEAD_DIM ** -0.5)

    def band(z):
        prev = jnp.concatenate([jnp.zeros_like(z[:, :SWA_BLOCK]), z[:, :-SWA_BLOCK]], axis=1)
        shape = (bsz, nb, SWA_BLOCK, SWA_KV_HEADS, SWA_HEAD_DIM)
        return jnp.concatenate([prev.reshape(shape), z.reshape(shape)], axis=2)

    kb, vb = band(k), band(v)
    s = jnp.einsum('bnqhgd,bnkhd->bnhgqk', q, kb).astype(jnp.float32) + bias
    s = jnp.where(mask[None, :, None, None], s, NEG_INF)
    sink = sinks.astype(jnp.float32).reshape(SWA_KV_HEADS, SWA_GROUP)[:, :, None]
    m = jnp.maximum(jnp.max(s, axis=-1), sink)
    p = jnp.exp(s - m[..., None])
    denom = jnp.sum(p, axis=-1) + jnp.exp(sink - m)
    probs = (p / denom[..., None]).astype(vb.dtype)
    o = jnp.einsum('bnhgqk,bnkhd->bnqhgd', probs, vb)
    return o.reshape(bsz, t, SWA_Q_HEADS * SWA_HEAD_DIM) @ w_o

def conv_gated_mlp(hn, w_up, conv_w, conv_b, w_down):
    u = causal_dwconv(hn @ w_up, conv_w, conv_b)
    gate, val = jnp.split(u, 2, axis=-1)
    return (jax.nn.silu(gate) * val) @ w_down

def first_inputs(seed: int = 0) -> dict:
    key = jax.random.key(seed)
    ks = jax.random.split(key, 24)
    f32 = jnp.float32

    def nrm(k, shape, scale):
        return jax.random.normal(k, shape, f32) * scale

    def gain(k, shape):
        return 1.0 + 0.02 * jax.random.normal(k, shape, f32)

    dt = jnp.exp(jax.random.uniform(ks[5], (N_A_LAYERS, GDN_V_HEADS), f32,
                                    minval=math.log(1e-3), maxval=math.log(1e-1)))
    return {
        'x': nrm(ks[0], (BATCH, SEQ, D_MODEL), 1.0),
        'a_norm_w': gain(ks[1], (N_A_LAYERS, D_MODEL)),
        'a_w_in': nrm(ks[2], (N_A_LAYERS, D_MODEL, GDN_IN_DIM), D_MODEL ** -0.5),
        'a_conv_w': nrm(ks[3], (N_A_LAYERS, GDN_CONV_WIDTH, GDN_CONV_DIM), GDN_CONV_WIDTH ** -0.5),
        'a_a_log': jnp.log(jax.random.uniform(ks[4], (N_A_LAYERS, GDN_V_HEADS), f32,
                                              minval=1.0, maxval=16.0)),
        'a_dt_bias': dt + jnp.log(-jnp.expm1(-dt)),
        'a_out_norm_w': gain(ks[6], (N_A_LAYERS, GDN_HEAD_DIM)),
        'a_w_out': nrm(ks[7], (N_A_LAYERS, GDN_V_DIM, D_MODEL), GDN_V_DIM ** -0.5),
        'kv_norm_w': gain(ks[8], (D_MODEL,)),
        'w_kv': nrm(ks[9], (D_MODEL, 2 * SWA_KV_HEADS * SWA_HEAD_DIM), D_MODEL ** -0.5),
        'b_norm_w': gain(ks[10], (N_B_LAYERS, D_MODEL)),
        'b_w_q': nrm(ks[11], (N_B_LAYERS, D_MODEL, SWA_Q_HEADS * SWA_HEAD_DIM), D_MODEL ** -0.5),
        'b_sinks': nrm(ks[12], (N_B_LAYERS, SWA_Q_HEADS), 0.5),
        'b_w_o': nrm(ks[13], (N_B_LAYERS, SWA_Q_HEADS * SWA_HEAD_DIM, D_MODEL),
                     (SWA_Q_HEADS * SWA_HEAD_DIM) ** -0.5),
        'rel_bias_table': nrm(ks[14], (REL_BUCKETS, SWA_Q_HEADS), 0.5),
        'ffn_norm_w': gain(ks[15], (DEPTH, D_MODEL)),
        'ffn_w_up': nrm(ks[16], (DEPTH, D_MODEL, 2 * D_FF), D_MODEL ** -0.5),
        'ffn_conv_w': nrm(ks[17], (DEPTH, FFN_CONV_WIDTH, 2 * D_FF), FFN_CONV_WIDTH ** -0.5),
        'ffn_conv_b': nrm(ks[18], (DEPTH, 2 * D_FF), 0.02),
        'ffn_w_down': nrm(ks[19], (DEPTH, D_FF, D_MODEL), D_FF ** -0.5),
        'final_norm_w': gain(ks[20], (D_MODEL,)),
    }

def first_block(x, a_norm_w, a_w_in, a_conv_w, a_a_log, a_dt_bias, a_out_norm_w, a_w_out,
              kv_norm_w, w_kv, b_norm_w, b_w_q, b_sinks, b_w_o, rel_bias_table,
              ffn_norm_w, ffn_w_up, ffn_conv_w, ffn_conv_b, ffn_w_down, final_norm_w):
    nb = x.shape[1] // SWA_BLOCK
    bias, mask = band_bias_and_mask(rel_bias_table, nb)
    h = x
    k_sh = None
    v_sh = None
    for layer in range(DEPTH):
        if layer < N_A_LAYERS:
            i = layer
            h = h + gated_deltanet(rmsnorm(h, a_norm_w[i]), a_w_in[i], a_conv_w[i], a_a_log[i],
                                   a_dt_bias[i], a_out_norm_w[i], a_w_out[i])
        else:
            j = layer - N_A_LAYERS
            if j == 0:
                k_sh, v_sh = shared_kv(h, kv_norm_w, w_kv)
            h = h + sliding_window_sink_attention(rmsnorm(h, b_norm_w[j]), k_sh, v_sh, b_w_q[j],
                                                  b_sinks[j], b_w_o[j], bias, mask)
        h = h + conv_gated_mlp(rmsnorm(h, ffn_norm_w[layer]), ffn_w_up[layer], ffn_conv_w[layer],
                               ffn_conv_b[layer], ffn_w_down[layer])
    return rmsnorm(h, final_norm_w)


DEPTH_2 = 1

CHUNK = 64
Q_BLOCK = 128

GLA_HEADS = 4
GLA_DK = 128
GLA_DV = 256
GLA_LOWRANK = 16
GLA_GATE_TEMP = 16.0

MLA_HEADS = 8
MLA_Q_LORA = 384
MLA_KV_LORA = 256
MLA_NOPE = 128
MLA_ROPE = 64
MLA_V = 128
ROPE_THETA = 10000.0

D_FF_2 = ((8 * D_MODEL // 3 + 255) // 256) * 256

NORM_EPS = 1e-6

IN_SPLITS = (
    GLA_HEADS * GLA_DK,
    GLA_HEADS * GLA_DK,
    GLA_HEADS * GLA_DV,
    GLA_HEADS * GLA_DV,
    GLA_LOWRANK,
    MLA_Q_LORA,
    MLA_KV_LORA,
    MLA_ROPE,
)
D_IN = sum(IN_SPLITS)
GLA_WIDTH = GLA_HEADS * GLA_DV
MLA_WIDTH = MLA_HEADS * MLA_V


def rms_norm(x, g):
    xf = x.astype(jnp.float32)
    y = xf * lax.rsqrt(jnp.mean(xf * xf, axis=-1, keepdims=True) + NORM_EPS)
    return (y * g.astype(jnp.float32)).astype(x.dtype)

def rope_tables(positions):
    inv_freq = 1.0 / (ROPE_THETA ** (jnp.arange(0, MLA_ROPE, 2, dtype=jnp.float32) / MLA_ROPE))
    ang = positions.astype(jnp.float32)[..., None] * inv_freq
    return jnp.cos(ang), jnp.sin(ang)

def apply_rope(x, cos, sin):
    half = x.shape[-1] // 2
    x1 = x[..., :half].astype(jnp.float32)
    x2 = x[..., half:].astype(jnp.float32)
    out = jnp.concatenate([x1 * cos - x2 * sin, x2 * cos + x1 * sin], axis=-1)
    return out.astype(x.dtype)

def gla_branch(h_q, h_k, h_v, h_g, h_a, w_a2, b_a2, gla_norm):
    B, S, _ = h_q.shape
    n_chunks = S // CHUNK
    f32 = jnp.float32
    q = h_q.reshape(B, S, GLA_HEADS, GLA_DK).astype(f32) * (GLA_DK ** -0.5)
    k = h_k.reshape(B, S, GLA_HEADS, GLA_DK).astype(f32)
    v = h_v.reshape(B, S, GLA_HEADS, GLA_DV).astype(f32)
    log_a = jax.nn.log_sigmoid((h_a @ w_a2 + b_a2).astype(f32)) / GLA_GATE_TEMP
    log_a = log_a.reshape(B, S, GLA_HEADS, GLA_DK)

    def to_chunks(t):
        return t.reshape(B, n_chunks, CHUNK, GLA_HEADS, t.shape[-1]).transpose(1, 0, 3, 2, 4)

    q, k, v, log_a = to_chunks(q), to_chunks(k), to_chunks(v), to_chunks(log_a)
    b = jnp.cumsum(log_a, axis=3)
    b_end = b[:, :, :, -1:, :]
    k_dec = k * jnp.exp(b_end - b)
    chunk_decay = jnp.exp(b_end[:, :, :, 0, :])

    def step(state, inp):
        qc, kc, vc, dc = inp
        state = dc[..., None] * state + jnp.einsum('bhck,bhcv->bhkv', kc, vc)
        out = jnp.einsum('bhck,bhkv->bhcv', qc, state)
        return state, out

    state0 = jnp.zeros((B, GLA_HEADS, GLA_DK, GLA_DV), f32)
    _, o = lax.scan(step, state0, (q, k_dec, v, chunk_decay))
    o = o.transpose(1, 0, 3, 2, 4).reshape(B, S, GLA_HEADS, GLA_DV)
    o = rms_norm(o, gla_norm)
    g = h_g.reshape(B, S, GLA_HEADS, GLA_DV).astype(f32)
    o = o * jax.nn.silu(g)
    return o.reshape(B, S, GLA_WIDTH).astype(h_q.dtype)

def mla_branch(c_q, c_kv, k_pe, cos, sin, q_norm, w_uq, kv_norm, w_ukv):
    B, S, _ = c_q.shape
    q = (rms_norm(c_q, q_norm) @ w_uq).reshape(B, S, MLA_HEADS, MLA_NOPE + MLA_ROPE)
    q_nope = q[..., :MLA_NOPE]
    q_pe = apply_rope(q[..., MLA_NOPE:], cos[:, :, None, :], sin[:, :, None, :])
    kv = (rms_norm(c_kv, kv_norm) @ w_ukv).reshape(B, S, MLA_HEADS, MLA_NOPE + MLA_V)
    k_nope = kv[..., :MLA_NOPE]
    v = kv[..., MLA_NOPE:]
    k_pe = apply_rope(k_pe, cos, sin)
    scale = (MLA_NOPE + MLA_ROPE) ** -0.5
    n_blocks = S // Q_BLOCK

    def blocks(t):
        return t.reshape(B, n_blocks, Q_BLOCK, MLA_HEADS, t.shape[-1]).transpose(1, 0, 2, 3, 4)

    key_chunk = jnp.arange(S) // CHUNK

    def attend(args):
        qn_b, qp_b, blk = args
        s = (jnp.einsum('bqhd,bkhd->bhqk', qn_b, k_nope)
             + jnp.einsum('bqhr,bkr->bhqk', qp_b, k_pe)).astype(jnp.float32) * scale
        q_chunk = (blk * Q_BLOCK + jnp.arange(Q_BLOCK)) // CHUNK
        mask = key_chunk[None, :] <= q_chunk[:, None]
        s = jnp.where(mask[None, None], s, -jnp.inf)
        p = jax.nn.softmax(s, axis=-1).astype(v.dtype)
        return jnp.einsum('bhqk,bkhd->bqhd', p, v)

    o = lax.map(attend, (blocks(q_nope), blocks(q_pe), jnp.arange(n_blocks)))
    return o.transpose(1, 0, 2, 3, 4).reshape(B, S, MLA_WIDTH)

def second_inputs(seed: int = 0) -> dict:
    key = jax.random.key(seed)
    ks = jax.random.split(key, 24)
    f32 = jnp.float32

    def w(k, shape, fan_in):
        return jax.random.normal(k, shape, f32) * (fan_in ** -0.5)

    def gain(k, dim):
        return 1.0 + 0.02 * jax.random.normal(k, (DEPTH_2, dim), f32)

    x = jax.random.normal(ks[0], (BATCH, SEQ, D_MODEL), f32)
    offsets = jax.random.randint(ks[1], (BATCH, 1), 0, 4096, dtype=jnp.int32)
    positions = offsets + jnp.arange(SEQ, dtype=jnp.int32)[None, :]
    return {
        "x": x,
        "positions": positions,
        "pre_mix_norm": gain(ks[2], D_MODEL),
        "w_in": w(ks[3], (DEPTH_2, D_MODEL, D_IN), D_MODEL),
        "w_a2": w(ks[4], (DEPTH_2, GLA_LOWRANK, GLA_HEADS * GLA_DK), GLA_LOWRANK),
        "b_a2": 0.1 * jax.random.normal(ks[5], (DEPTH_2, GLA_HEADS * GLA_DK), f32),
        "gla_norm": gain(ks[6], GLA_DV),
        "w_o_gla": w(ks[7], (DEPTH_2, GLA_WIDTH, D_MODEL), GLA_WIDTH),
        "q_norm": gain(ks[8], MLA_Q_LORA),
        "w_uq": w(ks[9], (DEPTH_2, MLA_Q_LORA, MLA_HEADS * (MLA_NOPE + MLA_ROPE)), MLA_Q_LORA),
        "kv_norm": gain(ks[10], MLA_KV_LORA),
        "w_ukv": w(ks[11], (DEPTH_2, MLA_KV_LORA, MLA_HEADS * (MLA_NOPE + MLA_V)), MLA_KV_LORA),
        "w_o_mla": w(ks[12], (DEPTH_2, MLA_WIDTH, D_MODEL), MLA_WIDTH),
        "w_gate": w(ks[13], (DEPTH_2, D_MODEL, 2 * D_MODEL), D_MODEL),
        "b_gate": 0.02 * jax.random.normal(ks[14], (DEPTH_2, 2 * D_MODEL), f32),
        "w_out": w(ks[15], (DEPTH_2, D_MODEL, D_MODEL), D_MODEL),
        "post_mix_norm": gain(ks[16], D_MODEL),
        "pre_ffn_norm": gain(ks[17], D_MODEL),
        "w_ffn_gate": w(ks[18], (DEPTH_2, D_MODEL, D_FF_2), D_MODEL),
        "w_ffn_up": w(ks[19], (DEPTH_2, D_MODEL, D_FF_2), D_MODEL),
        "w_ffn_down": w(ks[20], (DEPTH_2, D_FF_2, D_MODEL), D_FF_2),
        "post_ffn_norm": gain(ks[21], D_MODEL),
    }

def second_block(x, positions, pre_mix_norm, w_in, w_a2, b_a2, gla_norm, w_o_gla,
              q_norm, w_uq, kv_norm, w_ukv, w_o_mla, w_gate, b_gate, w_out,
              post_mix_norm, pre_ffn_norm, w_ffn_gate, w_ffn_up, w_ffn_down,
              post_ffn_norm):
    cos, sin = rope_tables(positions)
    split_points = list(np.cumsum(IN_SPLITS)[:-1])
    for l in range(DEPTH_2):
        h = rms_norm(x, pre_mix_norm[l])
        proj = h @ w_in[l]
        h_q, h_k, h_v, h_g, h_a, c_q, c_kv, k_pe = jnp.split(proj, split_points, axis=-1)
        y_a = gla_branch(h_q, h_k, h_v, h_g, h_a, w_a2[l], b_a2[l], gla_norm[l]) @ w_o_gla[l]
        y_b = mla_branch(c_q, c_kv, k_pe, cos, sin, q_norm[l], w_uq[l], kv_norm[l], w_ukv[l]) @ w_o_mla[l]
        gates = jax.nn.sigmoid(h @ w_gate[l] + b_gate[l])
        g_a, g_b = jnp.split(gates, 2, axis=-1)
        mixed = (g_a * y_a + g_b * y_b) @ w_out[l]
        x = x + rms_norm(mixed, post_mix_norm[l])
        h = rms_norm(x, pre_ffn_norm[l])
        f = (jax.nn.silu(h @ w_ffn_gate[l]) * (h @ w_ffn_up[l])) @ w_ffn_down[l]
        x = x + rms_norm(f, post_ffn_norm[l])
    return x


def setup_inputs(seed=0):
    out = dict(first_inputs(seed))
    for name, value in second_inputs(seed + 1).items():
        if name != "x":
            out[name + "_2"] = value
    return out


def reference(
    x, a_norm_w, a_w_in, a_conv_w, a_a_log, a_dt_bias, a_out_norm_w, a_w_out, kv_norm_w, w_kv,
    b_norm_w, b_w_q, b_sinks, b_w_o, rel_bias_table, ffn_norm_w, ffn_w_up, ffn_conv_w,
    ffn_conv_b, ffn_w_down, final_norm_w, positions_2, pre_mix_norm_2, w_in_2, w_a2_2, b_a2_2,
    gla_norm_2, w_o_gla_2, q_norm_2, w_uq_2, kv_norm_2, w_ukv_2, w_o_mla_2, w_gate_2, b_gate_2,
    w_out_2, post_mix_norm_2, pre_ffn_norm_2, w_ffn_gate_2, w_ffn_up_2, w_ffn_down_2,
    post_ffn_norm_2,
):
    x = first_block(
        x, a_norm_w, a_w_in, a_conv_w, a_a_log, a_dt_bias, a_out_norm_w, a_w_out, kv_norm_w,
        w_kv, b_norm_w, b_w_q, b_sinks, b_w_o, rel_bias_table, ffn_norm_w, ffn_w_up, ffn_conv_w,
        ffn_conv_b, ffn_w_down, final_norm_w,
    )
    return second_block(
        x, positions_2, pre_mix_norm_2, w_in_2, w_a2_2, b_a2_2, gla_norm_2, w_o_gla_2, q_norm_2,
        w_uq_2, kv_norm_2, w_ukv_2, w_o_mla_2, w_gate_2, b_gate_2, w_out_2, post_mix_norm_2,
        pre_ffn_norm_2, w_ffn_gate_2, w_ffn_up_2, w_ffn_down_2, post_ffn_norm_2,
    )


_drawn_inputs = setup_inputs


def setup_inputs(seed=0):
    import zlib

    import numpy as np

    out = dict(_drawn_inputs(seed))
    spreads = {}
    factors = {'kv_norm_w': 6.245,
     'b_norm_w': 8.0,
     'b_sinks': 15.092,
     'gla_norm_2': 27.816,
     'q_norm_2': 8.0,
     'kv_norm_2': 8.0,
     'b_gate_2': 8.0,
     'post_mix_norm_2': 3.307,
     'pre_ffn_norm_2': 3.408,
     'post_ffn_norm_2': 49.477,
     'b_a2_2': 3.87}
    for name, (base, spread) in spreads.items():
        noise = np.random.default_rng([zlib.crc32(name.encode()), seed]).standard_normal(out[name].shape)
        drawn = base * np.exp(spread * noise) if base else spread * noise
        out[name] = jnp.asarray(drawn.astype(out[name].dtype))
    for name, factor in factors.items():
        out[name] = (out[name] * factor).astype(out[name].dtype)
    return out
```

```python
from contextlib import ExitStack

import numpy as np

import concourse.bass as bass
from concourse import mybir

F32 = mybir.dt.float32
F32R = mybir.dt.float32r
I32 = mybir.dt.int32
ALU = mybir.AluOpType
ACT = mybir.ActivationFunctionType
AX = mybir.AxisListType

P = 128
SEQ, NT = 256, 2
D, KD = 1024, 8
UNIT = 1024
RING = 6
EPS = 1e-6
BIG = 1e30

VH = 16
QKH = 8
HD = 128
FF, NF = 2816, 22
AH, AHD = 16, 64
LEVELS = 7
GH, GDV = 4, 256
MH = 8
QL, KVL = 384, 256
BANDX = 383

PLAN = [("qkv", 32), ("z", 16), ("wout", 16), ("ffn0", 3 * NF), ("kv", 4), ("wq", 8), ("wo", 8),
        ("ffn1", 3 * NF), ("cq", 4), ("ckv", 2), ("x", 1), ("gq", 4), ("gk", 4), ("gv", 8),
        ("gg", 8), ("gates", 16), ("uq", 6), ("kn", 2), ("vm", 2), ("ogla", 8), ("omla", 8),
        ("w2", 8), ("ffn2", 3 * NF)]
BASE, _n = {}, 0
for _name, _count in PLAN:
    BASE[_name] = _n
    _n += _count
UNITS = _n

COLS = [("a_norm", 8), ("ffn0_norm", 8), ("kv_norm", 8), ("b_norm", 8), ("ffn1_norm", 8),
        ("pre_mix", 8), ("pre_ffn", 8), ("out_norm", 1), ("gla_norm", 2), ("q_norm", 3),
        ("kv2_norm", 2), ("conv_a", 32 * 4), ("conv0", 44 * 3), ("bias0", 44), ("conv1", 44 * 3),
        ("bias1", 44), ("left", LEVELS), ("inv_freq", 1), ("rope_sign", 1), ("chunk_of", 2)]
COL, _n = {}, 0
for _name, _count in COLS:
    COL[_name] = _n
    _n += _count
NCOLS = _n

TABS = [("ident", 128), ("ones", 128), ("tri", 128), ("future", 128), ("levels", LEVELS * 64),
        ("later", 128), ("chunk_mask", 384), ("swap", 128), ("dup", 128), ("dup_swap", 128),
        ("buckets", 384)]
TAB, _n = {}, 0
for _name, _count in TABS:
    TAB[_name] = _n
    _n += _count
NTABS = _n


class Named(dict):

    def __getattr__(self, name):
        return self[name]


def unit(k, i=0):
    return Named(u=k + RING * i, q=k // RING + i, s=k % RING,
                           first=isinstance(i, int) and k + RING * i < RING)


def build(nc, x, stream, w_ba, cols, tabs, rows, w_a2, rel_table, positions, out, band_scratch):
    with ExitStack() as ctx:
        def sb(name, shape, dt=F32):
            return ctx.enter_context(nc.sbuf_tensor(name, shape, dt))

        def sem(name):
            return ctx.enter_context(nc.semaphore(name))

        def sems(stage, names):
            return Named(**{n: sem(f"{stage}_{n}") for n in names.split()})

        raw = sb("raw", [P, RING, UNIT])
        whi = sb("whi", [P, RING, UNIT], F32R)
        wlo = sb("wlo", [P, RING, UNIT], F32R)
        xhi = sb("xhi", [P, 16, SEQ], F32R)
        xlo = sb("xlo", [P, 16, SEQ], F32R)
        fhi = sb("fhi", [P, 2, SEQ], F32R)
        flo = sb("flo", [P, 2, SEQ], F32R)
        resid = sb("resid", [P, NT, D])
        scr = sb("scr", [P, NT, D])
        col = sb("col", [P, NCOLS])
        tab = sb("tab", [P, NTABS])
        cosT = sb("cosT", [P, SEQ])
        sinT = sb("sinT", [P, SEQ])
        small = sb("small", [P, 48])
        stat = sb("stat", [P, 64])
        AREA = 19100
        area = sb("area", [P, AREA])
        wba_hi = sb("wba_hi", [P, KD * 32], F32R)
        wba_lo = sb("wba_lo", [P, KD * 32], F32R)

        def carve(offset, *shape):
            n = int(np.prod(shape))
            assert offset + n <= AREA, (offset, n)
            v = area[:, offset:offset + n]
            if len(shape) == 2:
                v = v.rearrange("p (a b) -> p a b", a=shape[0])
            if len(shape) == 3:
                v = v.rearrange("p (a b c) -> p a b c", a=shape[0], b=shape[1])
            return v, offset + n

        ps = [ctx.enter_context(nc.psum_tensor(f"bank{b}", [P, 512], F32)) for b in range(8)]

        def tabv(name):
            n = dict(TABS)[name]
            return tab[:, TAB[name]:TAB[name] + n]

        def colv(name, i=0, step=1):
            c = COL[name] + i
            return col[:, c:c + 1] if isinstance(c, int) else col[:, bass.ds(c, 1)]

        ident, ones, tri = tabv("ident"), tabv("ones"), tabv("tri")

        landed = [sem(f"landed{s}") for s in range(RING)]
        hi_ready, lo_ready, unit_done = sem("hi_ready"), sem("lo_ready"), sem("unit_done")

        def load_unit(sp, n):
            if not n.first:
                sp.wait_ge(lo_ready, n.u - RING + 1)
            src = stream[n.u] if isinstance(n.u, int) else stream[bass.ds(n.u, 1)].rearrange("a p c -> p (a c)")
            sp.dma_start(raw[:, n.s, :], src).then_inc(landed[n.s], 16)

        def round_unit(act, n):
            act.wait_ge(landed[n.s], 16 * n.q + 16)
            if not n.first:
                act.wait_ge(unit_done, n.u - RING + 1)
            act.activation(whi[:, n.s, :], raw[:, n.s, :], ACT.Copy).then_inc(hi_ready, 1)

        def rest_of_unit(pool, n):
            pool.wait_ge(hi_ready, n.u + 1)
            pool.tensor_tensor(wlo[:, n.s, :], raw[:, n.s, :], whi[:, n.s, :].bitcast(F32),
                               ALU.subtract).then_inc(lo_ready, 1)

        def refill(act, n):
            k = n if isinstance(n, Named) else unit(n)
            if isinstance(k.u, int) and k.u + RING >= UNITS:
                return
            round_unit(act, Named(u=k.u + RING, q=k.q + 1, s=k.s, first=False))

        def three(out_ap, a_hi, a_lo, b_hi, b_lo, start, stop):
            nc.tensor.matmul(out_ap, a_hi, b_hi, start=start, stop=False)
            nc.tensor.matmul(out_ap, a_hi, b_lo, start=False, stop=False)
            return nc.tensor.matmul(out_ap, a_lo, b_hi, start=False, stop=stop)

        def weights_still(pe, n, outs, kts, xs):
            pe.wait_ge(lo_ready, n.u + 1)
            i = 0
            for o in outs:
                for k in range(kts):
                    w = slice(i * P, i * P + P)
                    mm = three(o, whi[:, n.s, w], wlo[:, n.s, w], xhi[:, xs + k, :], xlo[:, xs + k, :],
                               k == 0, k == kts - 1)
                    i += 1
            mm.then_inc(unit_done, 1)

        def tokens_still(pe, n, banks, slots, width, ah, al, first, last):
            pe.wait_ge(lo_ready, n.u + 1)
            halves = len(banks[0])
            for t in range(NT):
                tok = slice(t * P, t * P + P)
                for h in range(halves):
                    for i, k in enumerate(slots):
                        w0 = (i * halves + h) * width
                        w = slice(w0, w0 + width)
                        mm = three(banks[t][h], ah[:, k, tok], al[:, k, tok], whi[:, n.s, w],
                                   wlo[:, n.s, w], first and i == 0, last and i == len(slots) - 1)
            mm.then_inc(unit_done, 1)

        def chain(eng, name):
            s, n = sem(name), [0]

            def link(ins):
                n[0] += 1
                ins.then_inc(s, 1)
                eng.wait_ge(s, n[0])
            return link

        dve_link = chain(nc.vector, "dve_chain")
        act_link = chain(nc.scalar, "act_chain")
        root_tmp = sb("root_tmp", [P, 32])

        def inverse_root(dve, y, w, eps, tmp):
            dve_link(dve.tensor_scalar(w, w, eps, None, ALU.add))
            dve_link(dve.tensor_scalar(tmp.bitcast(I32), w.bitcast(I32), 1, None, ALU.logical_shift_right))
            dve_link(dve.tensor_scalar(y.bitcast(I32), tmp.bitcast(I32), -1.0, float(0x5F3759DF), ALU.mult, ALU.add))
            for _ in range(3):
                dve_link(dve.tensor_tensor(tmp, y, w, ALU.mult))
                dve_link(dve.scalar_tensor_tensor(tmp, tmp, -0.5, y, ALU.mult, ALU.mult))
                dve_link(dve.scalar_tensor_tensor(y, tmp, 1.5, y, ALU.add, ALU.mult))

        TURNS = {"a": [("a_norm", 0)], "ffn0": [("ffn0_norm", 0)], "b": [("kv_norm", 0), ("b_norm", 8)],
                 "attn": [(None, 0)], "ffn1": [("ffn1_norm", 0)], "mix": [("pre_mix", 0)],
                 "gla": [("gla_norm", 0)], "mla": [(None, 8)], "mixed": [(None, 0)],
                 "ffn2": [("pre_ffn", 0)]}
        TR = sems("turn", "ready turned hi lo")
        TB, _i, _c = {}, 0, 0
        for _k, _v in TURNS.items():
            _c += 8 * len(_v)
            TB[_k] = Named(ready=2 * _i, turned=4 * _i, split=_c - 8 * len(_v), done=_c)
            _i += 1

        def weight_of(name, k):
            return 1.0 if name is None else colv(name, k % 2 if name == "gla_norm" else k)

        def turn_pe(pe, key, src):
            for pair in range(4):
                for t in range(NT):
                    if pair == 0:
                        pe.wait_ge(TR.ready, TB[key].ready + t + 1)
                    for k in (2 * pair, 2 * pair + 1):
                        c = k % 2 * SEQ + t * P
                        mm = pe.transpose(ps[4 + pair][:, c:c + P], src[:, t, k * P:k * P + P], ident)
                mm.then_inc(TR.turned, 1)

        def turn_act(act, key):
            for pair in range(4):
                act.wait_ge(TR.turned, TB[key].turned + pair + 1)
                for name, slot in TURNS[key]:
                    for k in (2 * pair, 2 * pair + 1):
                        act.activation(xhi[:, slot + k, :], ps[4 + pair][:, k % 2 * SEQ:k % 2 * SEQ + SEQ],
                                       ACT.Copy, scale=weight_of(name, k)).then_inc(TR.hi, 1)

        def turn_dve(dve, key):
            for pair in range(4):
                n = len(TURNS[key])
                dve.wait_ge(TR.hi, TB[key].split + 2 * n * (pair + 1))
                for name, slot in TURNS[key]:
                    for k in (2 * pair, 2 * pair + 1):
                        dve.scalar_tensor_tensor(
                            xlo[:, slot + k, :], ps[4 + pair][:, k % 2 * SEQ:k % 2 * SEQ + SEQ],
                            weight_of(name, k), xhi[:, slot + k, :].bitcast(F32), ALU.mult,
                            ALU.subtract).then_inc(TR.lo, 1)

        NORMS = {k: i for i, k in enumerate(["a", "ffn0", "b", "ffn1", "final", "mix", "post_mix",
                                             "ffn2", "post_ffn"])}
        squares, rescaled = sem("squares"), sem("rescaled")

        def norm_act(act, key, ready, value, src=resid):
            st = 4 * NORMS[key]
            for t in range(NT):
                act.wait_ge(ready, value(t))
                act.activation(scr[:, t, :], src[:, t, :], ACT.Square,
                               accum_out=stat[:, st + t:st + t + 1]).then_inc(squares, 1)

        def norm_dve(dve, key, row=None, src=resid):
            i, st = NORMS[key], 4 * NORMS[key]
            dve.wait_ge(squares, NT * (i + 1))
            inverse_root(dve, stat[:, st + 2:st + 4], stat[:, st:st + 2], D * EPS, root_tmp[:, 0:2])
            for t in range(NT):
                r = stat[:, st + 2 + t:st + 3 + t]
                ins = dve.tensor_scalar(scr[:, t, :], src[:, t, :], r, float(D) ** 0.5, ALU.mult, ALU.mult)
                if row is None:
                    ins.then_inc(TR.ready, 1)
                elif key == "final":
                    dve_link(ins)
                    dve.tensor_tensor(resid[:, t, :], scr[:, t, :], row, ALU.mult).then_inc(rescaled, 1)
                else:
                    dve_link(ins)
                    dve_link(dve.tensor_tensor(scr[:, t, :], scr[:, t, :], row, ALU.mult))
                    dve.tensor_tensor(resid[:, t, :], resid[:, t, :], scr[:, t, :], ALU.add).then_inc(rescaled, 1)
        FS = {f: sems(f"ffn{f}", "first tap conv silu act hi lo resid") for f in range(3)}
        ffn_g, _o = carve(AREA - 6 * SEQ, 2, SEQ)
        ffn_v, _o = carve(_o, 2, SEQ)
        ffn_a, _o = carve(_o, 2, SEQ)
        ACC = [[ps[0][:], ps[1][:]], [ps[2][:], ps[3][:]]]

        def ffn_unit(f, j, i, what):
            b = BASE[f"ffn{f}"]
            if what == "down":
                return unit(b + 3 * j + 4 if j < NF - 1 else b + 3 * NF - 1, i)
            half = 0 if what == "gate" else 1
            return unit(b + half if j == 0 else b + 3 * j - 1 + half, i)

        def ffn_pe(pe, f, conv):
            s = FS[f]
            bank_free, per_tile = (s.conv, 2) if conv else (s.act, 1)

            def up(j, i, reused):
                for half, what in enumerate(("gate", "val")):
                    if reused:
                        pe.wait_ge(bank_free, per_tile * (j - 2) + 2 * per_tile * i + (half + 1 if conv else 1))
                    weights_still(pe, ffn_unit(f, j, i, what), [ps[4 + j % 2 * 2 + half][:, 0:SEQ]], KD, 0)

            def down(j, i, first=False, last=False):
                pe.wait_ge(s.lo, j + 2 * i + 1)
                p = j % 2
                tokens_still(pe, ffn_unit(f, j, i, "down"), ACC, [0], 512, fhi[:, p:p + 1, :],
                             flo[:, p:p + 1, :], first, last)

            pe.wait_ge(TR.lo, TB[f"ffn{f}"].done)
            up(0, 0, False)
            up(1, 0, False)
            down(0, 0, first=True)
            with pe.Fori(0, (NF - 2) // 2) as i:
                for j in (2, 3):
                    up(j, i, True)
                    down(j - 1, i)
            down(NF - 1, 0, last=True)

        def ffn_act(act, f, conv):
            s = FS[f]

            def tile_of(j, i, reused):
                tile, p = j + 2 * i, j % 2
                for half, (what, dst) in enumerate((("gate", ffn_g), ("val", ffn_v))):
                    n = ffn_unit(f, j, i, what)
                    src = ps[4 + p * 2 + half][:, 0:SEQ]
                    if conv or half == 0:
                        act.wait_ge(unit_done, n.u + 1)
                        if reused:
                            act.wait_ge(s.lo, tile - 1)
                    if conv:
                        act.activation(dst[:, p, :], src, ACT.Identity, bias=colv(f"bias{f}", tile + half * NF),
                                       scale=colv(f"conv{f}", 88 + tile + half * NF)).then_inc(s.first, 1)
                    elif half == 0:
                        act.activation(dst[:, p, :], src, ACT.Silu).then_inc(s.silu, 1)
                    refill(act, n)
                if conv:
                    act.wait_ge(s.conv, 2 * tile + 1)
                    act.activation(ffn_g[:, p, :], ffn_g[:, p, :], ACT.Silu).then_inc(s.silu, 1)
                act.wait_ge(s.act, tile + 1)
                if reused:
                    act.wait_ge(unit_done, ffn_unit(f, j - 2, i, "down").u + 1)
                act.activation(fhi[:, p, :], ffn_a[:, p, :], ACT.Copy).then_inc(s.hi, 1)

            tile_of(0, 0, False)
            tile_of(1, 0, False)
            refill(act, ffn_unit(f, 0, 0, "down"))
            trips = (NF - 2) // 2 - (f == 2)
            with act.Fori(0, trips) as i:
                for j in (2, 3):
                    tile_of(j, i, True)
                    refill(act, ffn_unit(f, j - 1, i, "down"))
            if f == 2:
                for j in (2, 3):
                    tile_of(j, trips, True)
                    refill(act, ffn_unit(f, j - 1, trips, "down"))
            refill(act, ffn_unit(f, NF - 1, 0, "down"))

        def ffn_dve(dve, f, conv):
            s = FS[f]

            def tile_of(j, i):
                tile, p = j + 2 * i, j % 2
                if conv:
                    for half, dst in enumerate((ffn_g, ffn_v)):
                        src, y = ps[4 + p * 2 + half], dst[:, p, :]
                        nth = 2 * tile + half + 1
                        dve.wait_ge(s.first, nth)
                        dve.scalar_tensor_tensor(y[:, 1:SEQ], src[:, 0:SEQ - 1],
                                                 colv(f"conv{f}", 44 + tile + half * NF), y[:, 1:SEQ],
                                                 ALU.mult, ALU.add).then_inc(s.tap, 1)
                        dve.wait_ge(s.tap, nth)
                        dve.scalar_tensor_tensor(y[:, 2:SEQ], src[:, 0:SEQ - 2],
                                                 colv(f"conv{f}", tile + half * NF), y[:, 2:SEQ],
                                                 ALU.mult, ALU.add).then_inc(s.conv, 1)
                    dve.wait_ge(s.conv, 2 * tile + 2)
                    dve.wait_ge(s.silu, tile + 1)
                    dve.tensor_tensor(ffn_a[:, p, :], ffn_g[:, p, :], ffn_v[:, p, :],
                                      ALU.mult).then_inc(s.act, 1)
                else:
                    dve.wait_ge(s.silu, tile + 1)
                    dve.wait_ge(unit_done, ffn_unit(f, j, i, "val").u + 1)
                    dve.tensor_tensor(ffn_a[:, p, :], ffn_g[:, p, :], ps[5 + p * 2][:, 0:SEQ],
                                      ALU.mult).then_inc(s.act, 1)
                dve.wait_ge(s.hi, tile + 1)
                dve.tensor_tensor(flo[:, p, :], ffn_a[:, p, :], fhi[:, p, :].bitcast(F32),
                                  ALU.subtract).then_inc(s.lo, 1)

            tile_of(0, 0)
            tile_of(1, 0)
            with dve.Fori(0, (NF - 2) // 2) as i:
                tile_of(2, i)
                tile_of(3, i)

        def add_residual(dve, last_unit, done):
            dve.wait_ge(unit_done, last_unit + 1)
            for t in range(NT):
                for h in range(2):
                    r = resid[:, t, h * 512:h * 512 + 512]
                    dve.tensor_tensor(r, r, ACC[t][h], ALU.add).then_inc(done, 1)

        CV = sems("qkv", "first tap conv silu square turned_v copied_v sums turned_k copied_k sums_copied")
        GT = sems("gate", "ba exp absx logs g beta cum cum_copied")
        QK, _o = carve(0, 16, SEQ)
        V, _o = carve(_o, NT, VH * HD)
        Z, _groups = carve(_o, NT, VH * HD)
        cy, _o = carve(_groups, 2, SEQ)
        csq, _o = carve(_o, 2, SEQ)
        cvt, _o = carve(_o, 2, SEQ)
        bufs = []
        _o = _groups
        for _ in range(NT):
            b_ = Named()
            for name in ("M", "A", "T", "TT", "Pm"):
                b_[name], _o = carve(_o, 4, P)
            bufs.append(b_)
        K1, _o = carve(_o, QKH, P)
        gsc = sb("gsc", [P, 17 * 32])

        def gs(i, heads=16):
            return gsc[:, i * 32:i * 32 + 32].rearrange("p (t h) -> p t h", t=NT)

        BETA, G, GC, EGC, NEGC, DEC, RK, NK, BRK, RK2B, RKDEC, ROQ, SSQ, TMP, TMP2, OSS, ORS = range(17)

        def gates_act(act):
            act.wait_ge(GT.ba, 1)
            bav = ps[0][:, 0:64].rearrange("p (t c) -> p t c", t=NT)
            act.activation(gs(BETA), bav[:, :, 0:16], ACT.Exp, scale=-1.0).then_inc(GT.exp, 1)
            act_link(act.activation(small[:, 16:32], small[:, 16:32], ACT.Exp))
            act.wait_ge(GT.absx, 1)
            act_link(act.activation(gs(TMP2), gs(TMP), ACT.Abs))
            act_link(act.activation(gs(TMP2), gs(TMP2), ACT.Exp, scale=-1.0))
            act.activation(gs(TMP2), gs(TMP2), ACT.Ln, bias=ones[:, 0:1]).then_inc(GT.logs, 1)

        def gates_dve(dve):
            dve.wait_ge(GT.ba, 1)
            dve.wait_ge(GT.exp, 1)
            bav = ps[0][:, 0:64].rearrange("p (t c) -> p t c", t=NT)
            dve.tensor_tensor(gs(TMP), bav[:, :, 16:32], small[:, 0:16].unsqueeze(1).broadcast_to([P, NT, 16]),
                              ALU.add).then_inc(GT.absx, 1)
            dve_link(dve.tensor_scalar(gs(BETA), gs(BETA), 1.0, None, ALU.add))
            dve.reciprocal(gs(BETA), gs(BETA)).then_inc(GT.beta, 1)
            dve.wait_ge(GT.logs, 1)
            dve_link(dve.scalar_tensor_tensor(gs(G), gs(TMP), 0.0, gs(TMP2), ALU.max, ALU.add))
            dve.scalar_tensor_tensor(gs(G), gs(G), -1.0,
                                     small[:, 16:32].unsqueeze(1).broadcast_to([P, NT, 16]), ALU.mult,
                                     ALU.mult).then_inc(GT.g, 1)

        def qkv_pe(pe):
            pe.wait_ge(TR.lo, TB["a"].done)
            pe.wait_ge(wba_ready, 1)
            for t in range(NT):
                tok = slice(t * P, t * P + P)
                for k in range(KD):
                    w = slice(k * 32, k * 32 + 32)
                    mm = three(ps[0][:, t * 32:t * 32 + 32], xhi[:, k, tok], xlo[:, k, tok], wba_hi[:, w],
                               wba_lo[:, w], k == 0, k == KD - 1)
            mm.then_inc(GT.ba, 1)
            for b in range(32 + 2):
                if b < 32:
                    if b == 3:
                        pe.wait_ge(GT.absx, 1)
                    if b >= 4:
                        pe.wait_ge(CV.conv, b - 3)
                    weights_still(pe, unit(BASE["qkv"] + b), [ps[(b + 1) % 4][:, 0:SEQ]], KD, 0)
                if b == 6:
                    pe.wait_ge(GT.g, 1)
                    pe.matmul(ps[7][:, 0:32], tri, gsc[:, G * 32:G * 32 + 32], start=True, stop=True)
                    pe.matmul(ps[7][:, 32:64], ones, gsc[:, G * 32:G * 32 + 32], start=True,
                              stop=True).then_inc(GT.cum, 1)
                c = b - 2
                if 0 <= c < 16:
                    pe.wait_ge(CV.square, c + 1)
                    for t in range(NT):
                        mm = pe.matmul(ps[4][:, t * 16 + c:t * 16 + c + 1], csq[:, c % 2, t * P:t * P + P],
                                       ones[:, 0:1], start=True, stop=True)
                    mm.then_inc(CV.sums, 1)
                if 16 <= c < 32:
                    pe.wait_ge(CV.silu, c + 1)
                    if c >= 18:
                        pe.wait_ge(CV.copied_v, c - 17)
                    for t in range(NT):
                        mm = pe.transpose(ps[5 + c % 2][:, t * P:t * P + P], cvt[:, c % 2, t * P:t * P + P],
                                          ident)
                    mm.then_inc(CV.turned_v, 1)
                if c in (17, 19):
                    if c == 17:
                        pe.wait_ge(GT.cum_copied, 1)
                    else:
                        pe.wait_ge(CV.copied_k, 1)
                    for h in range(4):
                        mm = pe.transpose(ps[7][:, h * P:h * P + P], QK[:, (c - 17) * 2 + h, 0:P], ident)
                    mm.then_inc(CV.turned_k, 1)

        def qkv_act(act):
            def finish(b):
                act.wait_ge(CV.conv, b + 1)
                if b < 16:
                    act.activation(QK[:, b, :], cy[:, b % 2, :], ACT.Silu).then_inc(CV.silu, 1)
                    if b >= 2:
                        act.wait_ge(CV.sums, b - 1)
                    act.wait_ge(CV.silu, b + 1)
                    act.activation(csq[:, b % 2, :], QK[:, b, :], ACT.Square).then_inc(CV.square, 1)
                else:
                    if b >= 18:
                        act.wait_ge(CV.turned_v, b - 17)
                    act.activation(cvt[:, b % 2, :], cy[:, b % 2, :], ACT.Silu).then_inc(CV.silu, 1)

            for b in range(32):
                act.wait_ge(unit_done, BASE["qkv"] + b + 1)
                if b >= 2:
                    act.wait_ge(CV.silu, b - 1)
                act.activation(cy[:, b % 2, :], ps[(b + 1) % 4][:, 0:SEQ], ACT.Copy,
                               scale=colv("conv_a", 96 + b)).then_inc(CV.first, 1)
                refill(act, BASE["qkv"] + b)
                if b >= 1:
                    finish(b - 1)
            finish(31)

        def qkv_dve(dve):
            def copy_v(b):
                dve.wait_ge(CV.turned_v, b - 15)
                dve.tensor_copy(V[:, :, (b - 16) * P:(b - 15) * P],
                                ps[5 + b % 2][:, 0:SEQ].rearrange("p (t c) -> p t c", t=NT)).then_inc(CV.copied_v, 1)

            for b in range(32):
                src, y = ps[(b + 1) % 4], cy[:, b % 2, :]
                dve.wait_ge(CV.first, b + 1)
                for tap in (1, 2, 3):
                    ins = dve.scalar_tensor_tensor(y[:, tap:SEQ], src[:, 0:SEQ - tap],
                                                   colv("conv_a", (3 - tap) * 32 + b), y[:, tap:SEQ],
                                                   ALU.mult, ALU.add)
                    if tap < 3:
                        dve_link(ins)
                ins.then_inc(CV.conv, 1)
                if b == 9:
                    dve.wait_ge(GT.cum, 1)
                    dve_link(dve.tensor_copy(gsc[:, GC * 32:GC * 32 + 32], ps[7][:, 0:32]))
                    dve.tensor_tensor(gsc[:, DEC * 32:DEC * 32 + 32], ps[7][:, 32:64],
                                      gsc[:, GC * 32:GC * 32 + 32], ALU.subtract).then_inc(GT.cum_copied, 1)
                if b == 19:
                    dve.wait_ge(CV.sums, 16)
                    dve.tensor_scalar(gsc[:, SSQ * 32:SSQ * 32 + 32], ps[4][:, 0:32], 0.0, None,
                                      ALU.add).then_inc(CV.sums_copied, 1)
                if b >= 19:
                    copy_v(b - 3)
                if b in (21, 24):
                    dve.wait_ge(CV.turned_k, 1 + (b == 24))
                    h = 4 * (b == 24)
                    dve.tensor_copy(K1[:, h:h + 4, :], ps[7][:].rearrange("p (h c) -> p h c", h=4)).then_inc(CV.copied_k, 1)
            for b in (29, 30, 31):
                copy_v(b)
        DN = sems("delta", "setup diff decay mat init prod masked both updated r1 vn1p vn1 o1p s1p s1 kqs r2 "
                  "vn2p vn2 o2p o squares sumsq gated exps scal z_copied z_silu turned hi lo resid "
                  "normed")
        BA, BB, BC = (ps[2], ps[5]), (ps[3], ps[6]), (ps[4], ps[7])

        def by_head(i, t, g):
            c = i * 32 + t * 16 + 4 * g
            return gsc[:, c:c + 4].unsqueeze(2).broadcast_to([P, 4, P])

        def scalar(i, t, h):
            c = i * 32 + t * 16 + h
            return gsc[:, c:c + 1]

        def heads(bank, n=P):
            return bank[:, 0:4 * n].rearrange("p (h c) -> p h c", h=4)

        def blocks(flat, s, half):
            return flat.rearrange("p (n two s) -> p n two s", two=2, s=s)[:, :, half, :]

        def flat(buf):
            return buf.rearrange("p h c -> p (h c)")

        def group_cols(x, t, g):
            return x[:, t, g * 512:g * 512 + 512].rearrange("p (h c) -> p h c", h=4)

        def delta_pe(pe):
            def z_units(c, ks):
                for k in ks:
                    if k == 0:
                        if c == 0:
                            pe.wait_ge(CV.conv, 32)
                        else:
                            pe.wait_ge(DN.z_copied, 2 * c)
                    tokens_still(pe, unit(BASE["z"] + 4 * c + k), [[ps[0][:]], [ps[1][:]]],
                                 [2 * k, 2 * k + 1], 512, xhi, xlo, k == 0, k == 3)

            def setup(g, t):
                tok = slice(t * P, t * P + P)
                for kq in range(2):
                    k, q = QK[:, 2 * g + kq, tok], QK[:, 8 + 2 * g + kq, tok]
                    pe.matmul(BA[t][:, kq * 256:kq * 256 + P], k, k, start=True, stop=True)
                    pe.matmul(BA[t][:, kq * 256 + P:kq * 256 + 256], k, q, start=True, stop=True)
                for h in range(4):
                    mm = pe.matmul(BB[t][:, h * P:h * P + P],
                                   scalar(G, t, 4 * g + h).broadcast_to([P, P]), tri, start=True, stop=True)
                mm.then_inc(DN.setup, 1)

            pe.wait_ge(CV.copied_v, 16)
            pe.wait_ge(CV.copied_k, 2)
            for g in range(4):
                if g:
                    pe.wait_ge(DN.o, 2 * g)
                for t in range(NT):
                    setup(g, t)
                z_units(g, (0, 1, 2, 3))
                for lv in range(LEVELS):
                    s, last = 1 << lv, lv == LEVELS - 1
                    for t in range(NT):
                        b = bufs[t]
                        if lv == 0:
                            pe.wait_ge(DN.init, 2 * (2 * g + t) + 2)
                        else:
                            pe.wait_ge(DN.updated, (g * LEVELS + lv - 1) * 2 + t + 1)
                        for h in range(4):
                            mm = pe.matmul(BA[t][:, h * 64:h * 64 + 64].rearrange("p (n s) -> p n s", s=s),
                                           b.M[:, h, :], blocks(b.T[:, h, :], s, 0), start=True, stop=True)
                        mm.then_inc(DN.prod, 1)
                    for t in range(NT):
                        b = bufs[t]
                        pe.wait_ge(DN.masked, (g * LEVELS + lv) * 2 + t + 1)
                        for h in range(4):
                            if not last:
                                pe.matmul(BB[t][:, h * 64:h * 64 + 64].rearrange("p (n s) -> p n s", s=s),
                                          b.TT[:, h, :], blocks(b.Pm[:, h, :], s, 0), start=True, stop=True)
                            mm = pe.matmul(BC[t][:, h * 64:h * 64 + 64].rearrange("p (n s) -> p n s", s=s),
                                           b.Pm[:, h, :], blocks(b.TT[:, h, :], s, 1), start=True, stop=True)
                        mm.then_inc(DN.both, 1)
                b0, b1 = bufs
                pe.wait_ge(DN.updated, 2 * LEVELS * (g + 1))
                pe.wait_ge(DN.r1, g + 1)
                for h in range(4):
                    mm = pe.matmul(BA[0][:, h * P:h * P + P], b0.TT[:, h, :], b0.M[:, h, :], start=True, stop=True)
                mm.then_inc(DN.vn1p, 1)
                pe.wait_ge(DN.vn1, g + 1)
                for kq in range(2):
                    mm = pe.matmul(BB[0][:, kq * 256:kq * 256 + 256], K1[:, 2 * g + kq, :],
                                   b0.T[:, 2 * kq:2 * kq + 2, :], start=True, stop=True)
                mm.then_inc(DN.s1p, 1)
                for h in range(4):
                    mm = pe.matmul(BC[0][:, h * P:h * P + P], b0.A[:, h, :], b0.Pm[:, h, :], start=True, stop=True)
                mm.then_inc(DN.o1p, 1)
                pe.wait_ge(DN.s1, g + 1)
                for bank, which in ((BA[1], 0), (BB[1], 8)):
                    for kq in range(2):
                        mm = pe.matmul(bank[:, kq * 256:kq * 256 + 256], QK[:, which + 2 * g + kq, P:SEQ],
                                       b1.T[:, 2 * kq:2 * kq + 2, :], start=True, stop=True)
                mm.then_inc(DN.kqs, 1)
                pe.wait_ge(DN.r2, g + 1)
                for h in range(4):
                    mm = pe.matmul(BC[1][:, h * P:h * P + P], b1.TT[:, h, :], b1.M[:, h, :], start=True, stop=True)
                mm.then_inc(DN.vn2p, 1)
                pe.wait_ge(DN.vn2, g + 1)
                for h in range(4):
                    mm = pe.matmul(BA[0][:, h * P:h * P + P], b1.A[:, h, :], b0.T[:, h, :], start=True, stop=True)
                mm.then_inc(DN.o2p, 1)

            pe.wait_ge(DN.o, 8)
            pe.wait_ge(DN.z_copied, 8)

            def turn(pair):
                pe.wait_ge(DN.gated, (pair // 2 + 1) * 2)
                if pair >= 4:
                    pe.wait_ge(DN.lo, pair - 3)
                for k in (2 * pair, 2 * pair + 1):
                    for t in range(NT):
                        c = k % 2 * SEQ + t * P
                        mm = pe.transpose(ps[4 + pair % 4][:, c:c + P], V[:, t, k * P:k * P + P], ident)
                mm.then_inc(DN.turned, 1)

            turn(0)
            turn(1)
            for pair in range(8):
                if pair < 6:
                    turn(pair + 2)
                pe.wait_ge(DN.lo, pair + 1)
                for k in (2 * pair, 2 * pair + 1):
                    tokens_still(pe, unit(BASE["wout"] + k), ACC, [k], 512, xhi, xlo, k == 0, k == 15)

        def delta_act(act):
            act.wait_ge(GT.cum_copied, 1)
            act.activation(gsc[:, EGC * 32:EGC * 32 + 32], gsc[:, GC * 32:GC * 32 + 32], ACT.Exp).then_inc(DN.exps, 1)
            act.activation(gsc[:, DEC * 32:DEC * 32 + 32], gsc[:, DEC * 32:DEC * 32 + 32], ACT.Exp).then_inc(DN.exps, 1)
            for g in range(4):
                for t in range(NT):
                    act.wait_ge(DN.diff, 2 * g + t + 1)
                    act.activation(flat(bufs[t].T), flat(bufs[t].T), ACT.Exp).then_inc(DN.decay, 1)
                for t in range(NT):
                    act.wait_ge(DN.mat, 2 * g + t + 1)
                    for buf in (bufs[t].T, bufs[t].TT):
                        act.activation(buf, ident.unsqueeze(1).broadcast_to([P, 4, P]), ACT.Copy).then_inc(DN.init, 1)
                for k in range(4):
                    refill(act, BASE["z"] + 4 * g + k)
                for t in range(NT):
                    act.activation(Z[:, t, g * 512:g * 512 + 512], ps[t][:], ACT.Copy).then_inc(DN.z_copied, 1)
                if g == 3:
                    act.wait_ge(DN.z_copied, 8)
                    for t in range(NT):
                        act.activation(Z[:, t, :], Z[:, t, :], ACT.Silu).then_inc(DN.z_silu, 1)
                act.wait_ge(DN.s1p, g + 1)
                act.activation(flat(bufs[1].T), BB[0][:], ACT.Copy).then_inc(DN.s1, 1)
                for t in range(NT):
                    act.wait_ge(DN.o, 2 * g + t + 1)
                    if g:
                        act.wait_ge(DN.sumsq, 2 * g - 1 + t)
                    act.activation(scr[:, t, 0:512], V[:, t, g * 512:g * 512 + 512], ACT.Square).then_inc(DN.squares, 1)
            for pair in range(8):
                act.wait_ge(DN.turned, pair + 1)
                act.activation(xhi[:, 2 * pair:2 * pair + 2, :].rearrange("p a b -> p (a b)"),
                               ps[4 + pair % 4][:], ACT.Copy, scale=colv("out_norm")).then_inc(DN.hi, 1)
                if pair >= 2:
                    refill(act, BASE["wout"] + 2 * pair - 4)
                    refill(act, BASE["wout"] + 2 * pair - 3)
            for k in range(12, 16):
                refill(act, BASE["wout"] + k)

        def delta_dve(dve):
            dve.memset(bufs[0].Pm, 0.0).then_inc(DN.scal, 1)
            dve.memset(bufs[1].Pm, 0.0).then_inc(DN.scal, 1)
            w, rk, nk = (gsc[:, i * 32:i * 32 + 32] for i in (SSQ, RK, NK))
            dve.wait_ge(CV.sums_copied, 1)
            inverse_root(dve, rk, w, EPS, root_tmp[:])
            dve_link(dve.tensor_tensor(nk, w, rk, ALU.mult))
            dve.wait_ge(DN.exps, 2)

            def pairs(i):
                return gs(i).rearrange("p t (h r) -> p t h r", r=2)

            def shared(i, q=0):
                return gs(i)[:, :, 8 * q:8 * q + 8].unsqueeze(3).broadcast_to([P, NT, 8, 2])

            dve_link(dve.tensor_tensor(pairs(BRK), pairs(BETA), shared(RK), ALU.mult))
            dve_link(dve.tensor_tensor(pairs(RK2B), pairs(BRK), shared(RK), ALU.mult))
            dve_link(dve.tensor_tensor(pairs(RKDEC), pairs(DEC), shared(RK), ALU.mult))
            dve_link(dve.tensor_scalar(gs(NEGC), gs(EGC), -1.0, None, ALU.mult))
            dve_link(dve.tensor_copy(pairs(TMP), shared(NK)))
            dve_link(dve.tensor_copy(pairs(ROQ), shared(RK, 1)))
            dve_link(dve.tensor_scalar(gs(ROQ), gs(ROQ), float(HD) ** -0.5, None, ALU.mult))

            def norm_out(g):
                for t in range(NT):
                    dve.wait_ge(DN.squares, 2 * g + t + 1)
                    c = OSS * 32 + t * 16 + 4 * g
                    dve.tensor_reduce(gsc[:, c:c + 4], scr[:, t, 0:512].rearrange("p (h c) -> p h c", h=4),
                                      AX.X, ALU.add).then_inc(DN.sumsq, 1)
                dve.wait_ge(DN.sumsq, 2 * g + 2)
                sums = gs(OSS)[:, :, 4 * g:4 * g + 4]
                inverse_root(dve, gs(ORS)[:, :, 4 * g:4 * g + 4], sums, HD * EPS,
                             root_tmp[:, 0:8].rearrange("p (t h) -> p t h", t=NT))
                for t in range(NT):
                    v = group_cols(V, t, g)
                    dve.tensor_tensor(v, v, by_head(ORS, t, g), ALU.mult).then_inc(DN.normed, 1)

            for g in range(4):
                for t in range(NT):
                    dve.wait_ge(DN.setup, 2 * g + t + 1)
                    for h in range(4):
                        ins = dve.scalar_tensor_tensor(bufs[t].T[:, h, :], BB[t][:, h * P:h * P + P],
                                                       scalar(GC, t, 4 * g + h), tabv("future"),
                                                       ALU.subtract, ALU.min)
                    ins.then_inc(DN.diff, 1)
                for t in range(NT):
                    dve.wait_ge(DN.decay, 2 * g + t + 1)
                    for h in range(4):
                        hh, c = 4 * g + h, h // 2 * 256
                        dve.scalar_tensor_tensor(bufs[t].M[:, h, :], BA[t][:, c:c + P], scalar(RK2B, t, hh),
                                                 bufs[t].T[:, h, :], ALU.mult, ALU.mult)
                        ins = dve.scalar_tensor_tensor(bufs[t].A[:, h, :], BA[t][:, c + P:c + 256],
                                                       scalar(RK, t, hh // 2), bufs[t].T[:, h, :],
                                                       ALU.mult, ALU.mult)
                    ins.then_inc(DN.mat, 1)
                if g:
                    norm_out(g - 1)
                for lv in range(LEVELS):
                    s, last = 1 << lv, lv == LEVELS - 1
                    for t in range(NT):
                        b = bufs[t]
                        dve.wait_ge(DN.prod, (g * LEVELS + lv) * 2 + t + 1)
                        m = tabv("levels")[:, lv * 64:lv * 64 + 64].rearrange("p (n s) -> p n s", s=s)
                        dst = b.Pm.rearrange("p h (n two s) -> p h n two s", two=2, s=s)[:, :, :, 0, :]
                        src = BA[t][:, 0:256].rearrange("p (h n s) -> p h n s", h=4, s=s)
                        dve.tensor_tensor(dst, src, m.unsqueeze(1).broadcast_to([P, 4, 64 // s, s]),
                                          ALU.mult).then_inc(DN.masked, 1)
                    for t in range(NT):
                        b = bufs[t]
                        dve.wait_ge(DN.both, (g * LEVELS + lv) * 2 + t + 1)
                        if not last:
                            left = blocks(flat(b.T), s, 0)
                            dve.tensor_tensor(left, left, BB[t][:, 0:256].rearrange("p (n s) -> p n s", s=s),
                                              ALU.subtract)
                        right = blocks(flat(b.TT), s, 1)
                        dve.scalar_tensor_tensor(right, BC[t][:, 0:256].rearrange("p (n s) -> p n s", s=s),
                                                 colv("left", lv), right, ALU.mult, ALU.add).then_inc(DN.updated, 1)
                b0, b1 = bufs
                dve.tensor_tensor(b0.M, group_cols(V, 0, g), by_head(TMP, 0, g), ALU.mult).then_inc(DN.r1, 1)
                dve_link(dve.tensor_tensor(b1.M, group_cols(V, 1, g), by_head(TMP, 1, g), ALU.mult))
                dve.wait_ge(DN.vn1p, g + 1)
                dve_link(dve.tensor_tensor(b0.Pm, heads(BA[0]), by_head(BRK, 0, g), ALU.mult))
                dve.tensor_tensor(b0.T, b0.Pm, by_head(RKDEC, 0, g), ALU.mult).then_inc(DN.vn1, 1)
                dve.wait_ge(DN.kqs, g + 1)
                dve_link(dve.tensor_tensor(b1.Pm, heads(BA[1]), by_head(NEGC, 1, g), ALU.mult))
                dve.tensor_tensor(b1.M, b1.M, b1.Pm, ALU.add).then_inc(DN.r2, 1)
                dve.wait_ge(DN.r2, g + 1)
                dve_link(dve.tensor_tensor(b1.Pm, heads(BB[1]), by_head(EGC, 1, g), ALU.mult))
                dve.wait_ge(DN.o1p, g + 1)
                dve.tensor_tensor(group_cols(V, 0, g), heads(BC[0]), by_head(ROQ, 0, g), ALU.mult).then_inc(DN.o, 1)
                dve.wait_ge(DN.vn2p, g + 1)
                dve.tensor_tensor(b0.T, heads(BC[1]), by_head(BRK, 1, g), ALU.mult).then_inc(DN.vn2, 1)
                dve.wait_ge(DN.o2p, g + 1)
                dve_link(dve.tensor_tensor(b1.Pm, heads(BA[0]), b1.Pm, ALU.add))
                dve.tensor_tensor(group_cols(V, 1, g), b1.Pm, by_head(ROQ, 1, g), ALU.mult).then_inc(DN.o, 1)
            norm_out(3)
            dve.wait_ge(DN.z_silu, 2)
            dve.wait_ge(DN.normed, 8)
            for g in range(4):
                for t in range(NT):
                    v = group_cols(V, t, g)
                    dve.tensor_tensor(v, v, group_cols(Z, t, g), ALU.mult).then_inc(DN.gated, 1)
            for pair in range(8):
                dve.wait_ge(DN.hi, pair + 1)
                dve.scalar_tensor_tensor(xlo[:, 2 * pair:2 * pair + 2, :].rearrange("p a b -> p (a b)"),
                                         ps[4 + pair % 4][:], colv("out_norm"),
                                         xhi[:, 2 * pair:2 * pair + 2, :].rearrange("p a b -> p (a b)").bitcast(F32),
                                         ALU.mult, ALU.subtract).then_inc(DN.lo, 1)
            add_residual(dve, BASE["wout"] + 15, DN.resid)
        AT = sems("attn", "scores maxed exps turned copied outs sunk total inverse")
        bias_, _o = carve(0, AH, SEQ)
        QT, _o = carve(_o, 8, SEQ)
        KT, _o = carve(_o, 2, SEQ)
        VN, _o = carve(_o, NT, SEQ)
        swa = Named(heads=AH, width=AHD, base=0, AO=carve(8192, NT, D)[0])
        swa["S"], _o = carve(12288, 3, 384)
        swa["PT"], _o = carve(_o, 2, 384)
        row_b_a2, _o = carve(15872, 512)
        row_final, _o = carve(_o, D)
        PARTS = (slice(0, P), slice(P, 384))
        att_stat = sb("att_stat", [P, 4 * 32])

        def att(i, n):
            return att_stat[:, i * 32:i * 32 + 2 * n].rearrange("p (h t) -> p h t", t=NT)

        def attention_pe(pe, a, scores, v):
            n, b = a.heads, a.base
            for j in range(n + 2):
                if j < n:
                    if j >= 2:
                        pe.wait_ge(AT.maxed, b + j - 1)
                    scores(j, ps[4 + j % 2]).then_inc(AT.scores, 1)
                h = j - 1
                if 0 <= h < n:
                    pe.wait_ge(AT.exps, b + h + 1)
                    if h >= 2:
                        pe.wait_ge(AT.copied, b + h - 1)
                    for c in range(3):
                        mm = pe.transpose(ps[6 + h % 2][:, c * P:c * P + P], a.S[:, h % 3, c * P:c * P + P], ident)
                    mm.then_inc(AT.turned, 1)
                h = j - 2
                if h >= 0:
                    pe.wait_ge(AT.copied, b + h + 1)
                    pt, c = a.PT[:, h % 2, :], h * a.width
                    o = [ACC[t][c // 512][:, c % 512:c % 512 + a.width] for t in range(NT)]
                    pe.matmul(o[0], pt[:, 0:P], v(h, 0), start=True, stop=True)
                    pe.matmul(o[1], pt[:, P:SEQ], v(h, 0), start=True, stop=False)
                    pe.matmul(o[1], pt[:, SEQ:384], v(h, 1), start=False, stop=True).then_inc(AT.outs, 1)

        def attention_act(act, a):
            n, b = a.heads, a.base
            for j in range(n + 1):
                if j < n:
                    act.wait_ge(AT.maxed, b + j + 1)
                    for t in range(NT):
                        ins = act.activation(a.S[:, j % 3, PARTS[t]], a.S[:, j % 3, PARTS[t]], ACT.Exp,
                                             bias=att(0, n)[:, j, t:t + 1], accum_out=att(1, n)[:, j, t:t + 1])
                    ins.then_inc(AT.exps, 1)
                h = j - 1
                if h >= 0:
                    act.wait_ge(AT.turned, b + h + 1)
                    if h >= 2:
                        act.wait_ge(AT.outs, b + h - 1)
                    act.activation(a.PT[:, h % 2, :], ps[6 + h % 2][:, 0:384], ACT.Copy).then_inc(AT.copied, 1)

        def attention_dve(dve, a, bias, least):
            n, b = a.heads, a.base
            for j in range(n):
                dve.wait_ge(AT.scores, b + j + 1)
                if j >= 3:
                    dve.wait_ge(AT.turned, b + j - 2)
                for t in range(NT):
                    ins = dve.tensor_tensor_reduce(a.S[:, j % 3, PARTS[t]], ps[4 + j % 2][:, PARTS[t]], bias(j, t),
                                                   1.0, least(j), ALU.add, ALU.max,
                                                   accum_out=att(2, n)[:, j, t:t + 1])
                dve_link(ins)
                dve.tensor_scalar(att(0, n)[:, j, :], att(2, n)[:, j, :], -1.0, None, ALU.mult).then_inc(AT.maxed, 1)

        def attention_finish(dve, a, extra):
            n, b = a.heads, a.base
            dve.wait_ge(AT.exps, b + n)
            extra()
            dve_link(dve.reciprocal(att(3, n), att(1, n)))
            dve.wait_ge(AT.outs, b + n)
            for t in range(NT):
                for half in range(2):
                    hs = n // 2
                    ins = dve.tensor_tensor(
                        a.AO[:, t, half * 512:half * 512 + 512].rearrange("p (h c) -> p h c", h=hs),
                        ACC[t][half].rearrange("p (h c) -> p h c", h=hs),
                        att(3, n)[:, half * hs:half * hs + hs, t:t + 1].broadcast_to([P, hs, a.width]), ALU.mult)
                ins.then_inc(TR.ready, 1)

        SW = sems("swa", "bias row_final row_b copied resid")

        def swa_load(act):
            act.wait_ge(IN.band_out, 16)
            skewed = bass.AP(tensor=band_scratch.tensor, offset=band_scratch.offset + P - 1,
                             ap=[[BANDX, P], [P * 384, AH], [1, SEQ]])
            act.dma_start(bias_, skewed).then_inc(SW.bias, 16)
            act.dma_start(row_final, rows["final"].broadcast_to([P, D])).then_inc(SW.row_final, 16)
            act.dma_start(row_b_a2, rows["b_a2"].broadcast_to([P, 512])).then_inc(SW.row_b, 16)

        def swa_pe(pe):
            pe.wait_ge(TR.lo, TB["b"].done)
            for b in range(2):
                weights_still(pe, unit(BASE["kv"] + b), [ps[b][:, 0:SEQ]], KD, 0)
            for k in range(2):
                tokens_still(pe, unit(BASE["kv"] + 2 + k), [[ps[4][:, 0:SEQ]], [ps[5][:, 0:SEQ]]],
                             [4 * k + i for i in range(4)], SEQ, xhi, xlo, k == 0, k == 1)
            for b in range(8):
                if b >= 2:
                    pe.wait_ge(SW.copied, b + 1 if b >= 4 else b - 1)
                weights_still(pe, unit(BASE["wq"] + b), [ps[(2 + b) % 4][:, 0:SEQ]], KD, 8)

            def scores(j, bank):
                half = slice(j % 2 * AHD, j % 2 * AHD + AHD)
                q, k = QT[half, j // 2, :], KT[half, j // 8, :]
                pe.matmul(bank[:, 0:P], q[:, 0:P], k[:, 0:P], start=True, stop=True)
                return pe.matmul(bank[:, P:384], q[:, P:SEQ], k, start=True, stop=True)

            def v(j, t):
                g = j // 8 * 2 + j % 2
                return VN[:, t, g * AHD:g * AHD + AHD]

            pe.wait_ge(SW.copied, 12)
            attention_pe(pe, swa, scores, v)
            turn_pe(pe, "attn", swa.AO)
            for k in range(KD):
                pe.wait_ge(TR.lo, TB["attn"].split + k + 1)
                tokens_still(pe, unit(BASE["wo"] + k), ACC, [k], 512, xhi, xlo, k == 0, k == KD - 1)

        def swa_act(act):
            def copy(last, dst, bank, scale=1.0):
                act.wait_ge(unit_done, last + 1)
                act.activation(dst, ps[bank][:, 0:SEQ], ACT.Copy, scale=scale).then_inc(SW.copied, 1)

            for b in range(2):
                copy(BASE["kv"] + b, KT[:, b, :], b)
                refill(act, BASE["kv"] + b)
            refill(act, BASE["kv"] + 2)
            for t in range(NT):
                copy(BASE["kv"] + 3, VN[:, t, :], 4 + t)
            refill(act, BASE["kv"] + 3)
            for b in range(8):
                copy(BASE["wq"] + b, QT[:, b, :], (2 + b) % 4, AHD ** -0.5)
                refill(act, BASE["wq"] + b)
            attention_act(act, swa)
            act.wait_ge(AT.sunk, 1)
            act.activation(att(2, AH), att(2, AH), ACT.Exp).then_inc(AT.total, 1)
            turn_act(act, "attn")
            for k in range(KD):
                refill(act, BASE["wo"] + k)

        def swa_dve(dve):
            sinks = small[:, 32:48]
            dve.wait_ge(SW.bias, 16)
            attention_dve(dve, swa, lambda j, t: bias_[:, j, (P, 0)[t]:SEQ], lambda j: sinks[:, j:j + 1])

            def sink_terms():
                dve.tensor_tensor(att(2, AH), att(0, AH), sinks.unsqueeze(2).broadcast_to([P, AH, NT]),
                                  ALU.add).then_inc(AT.sunk, 1)
                dve.wait_ge(AT.total, 1)
                dve_link(dve.tensor_tensor(att(1, AH), att(1, AH), att(2, AH), ALU.add))

            attention_finish(dve, swa, sink_terms)
            turn_dve(dve, "attn")
            add_residual(dve, BASE["wo"] + KD - 1, SW.resid)
        MX = sems("mix", "w_a2 row_gate row_post row_ffn copied la_made la_x la_ln la suffix decays kdec "
                  "c_squares c_ready c_turned c_hi c_lo gates_in sigmoid kv state o o_squares up_copied "
                  "rope_made roped ya_used w2_copied")
        GV, _o = carve(0, NT, D)
        GK, _o = carve(_o, NT, 512)
        GQT, _o = carve(_o, GH, SEQ)
        LA, _s1 = carve(_o, NT, 512)
        ST, _o = carve(_o, 2, GH * GDV)
        GG, _o = carve(_o, NT, D)
        GA, _o = carve(_o, NT, D)
        GB, _o = carve(_o, NT, D)
        OG, _t = carve(_o, NT, D)
        LT, _t = carve(_o, NT, 512)
        LX, _t = carve(_t, NT, 512)
        CQ, _o = carve(_t, NT, QL)
        CKV, _o = carve(_o, NT, KVL)
        XB, _o = carve(_o, SEQ)
        QN, _t = carve(0, MH, SEQ)
        KN, _t = carve(_t, MH, SEQ)
        VM, _t = carve(_t, NT, D)
        row_post, _t = carve(14336, D)
        row_ffn, _t = carve(_t, D)
        QP, _t = carve(16384, 4, SEQ)
        W_A2, _t = carve(17408, 512)
        KP, _t = carve(17920, SEQ)
        MIXED = carve(0, NT, D)[0]
        mla = Named(heads=MH, width=P, base=AH, S=swa.S, PT=swa.PT, AO=carve(6144, NT, D)[0])
        DC = att_stat[:, 0:16]
        OSQ, CSQ = att_stat[:, 32:48], att_stat[:, 64:72]
        CHUNKS = ("gk0", "gv0", "gv1", "gg0", "gg1", "gates0", "gates1", "gates2", "gates3")

        def block2_pe(pe):
            turn_pe(pe, "mix", scr)
            pe.wait_ge(TR.lo, TB["mix"].done)
            for k in range(4):
                tokens_still(pe, unit(BASE["cq"] + k), [[ps[t][:, 0:QL]] for t in range(NT)], [2 * k, 2 * k + 1],
                             QL, xhi, xlo, k == 0, k == 3)
            for k in range(2):
                tokens_still(pe, unit(BASE["ckv"] + k), [[ps[2 + t][:, 0:KVL]] for t in range(NT)],
                             [4 * k + i for i in range(4)], KVL, xhi, xlo, k == 0, k == 1)
            weights_still(pe, unit(BASE["x"]), [ps[4][:, 0:SEQ]], KD, 0)
            for h in range(GH):
                if h == 3:
                    pe.wait_ge(MX.copied, 5)
                weights_still(pe, unit(BASE["gq"] + h), [ps[(5, 6, 7, 4)[h]][:, 0:SEQ]], KD, 0)
            pe.wait_ge(MX.w_a2, 16)
            pe.wait_ge(MX.copied, 7)
            for t in range(NT):
                mm = pe.matmul(ps[5 + t][:], XB[0:16, t * P:t * P + P], W_A2[0:16, :], start=True, stop=True)
            mm.then_inc(MX.la_made, 1)
            for c, name in enumerate(CHUNKS):
                pair = c % 2 * 2
                if c <= 6:
                    pe.wait_ge(MX.copied, (2, 4, 11, 13, 15, 17, 19)[c])
                else:
                    pe.wait_ge(MX.gates_in, 2 * (c - 6))
                for k in range(4):
                    tokens_still(pe, unit(BASE[name[:-1]] + int(name[-1]) * 4 + k), [[ps[pair][:]], [ps[pair + 1][:]]],
                                 [2 * k, 2 * k + 1], 512, xhi, xlo, k == 0, k == 3)
                if c == 0:
                    pe.wait_ge(MX.la, 1)
                    pe.wait_ge(MX.copied, 8)
                    for t in range(NT):
                        pe.matmul(ps[5 + t][:], tabv("later"), LA[:, t, :], start=True, stop=True)
                        for h in range(GH):
                            i = (t * GH + h) * 2
                            mm = pe.matmul(ps[7][:, i:i + 2], LA[:, t, h * P:h * P + P],
                                           col[:, COL["chunk_of"]:COL["chunk_of"] + 2], start=True, stop=True)
                    mm.then_inc(MX.suffix, 1)
                if c == 3:
                    pe.wait_ge(MX.c_ready, 1)
                    pe.wait_ge(MX.decays, 2)
                    pe.wait_ge(MX.copied, 9)
                    for bank, src, ks in ((4, CQ, (0, 1)), (5, CQ, (2,)), (6, CKV, (0, 1))):
                        for i, k in enumerate(ks):
                            for t in range(NT):
                                mm = pe.transpose(ps[bank][:, i * SEQ + t * P:i * SEQ + t * P + P],
                                                  src[:, t, k * P:k * P + P], ident)
                        mm.then_inc(MX.c_turned, 1)

            pe.wait_ge(MX.c_lo, 5)
            pe.wait_ge(MX.kdec, 1)
            pe.wait_ge(MX.gates_in, 8)
            for c in range(2 * NT + 1):
                if c < 2 * NT:
                    t, half = c // 2, slice(c % 2 * 64, c % 2 * 64 + 64)
                    if c >= 2:
                        pe.wait_ge(MX.state, c - 1)
                    for h in range(GH):
                        mm = pe.matmul(ps[4 + c % 2 * 2 + h // 2][:, h % 2 * GDV:h % 2 * GDV + GDV],
                                       GK[half, t, h * P:h * P + P], GV[half, t, h * GDV:h * GDV + GDV],
                                       start=True, stop=True)
                    mm.then_inc(MX.kv, 1)
                c -= 1
                if c >= 0:
                    t, half = c // 2, slice(c % 2 * 64, c % 2 * 64 + 64)
                    pe.wait_ge(MX.state, c + 1)
                    for h in range(GH):
                        mm = pe.matmul(ACC[t][h // 2][half, h % 2 * GDV:h % 2 * GDV + GDV],
                                       GQT[:, h, c * 64:c * 64 + 64], ST[:, c % 2, h * GDV:h * GDV + GDV],
                                       start=True, stop=True)
                    mm.then_inc(MX.o, 1)

            for i in range(6):
                if i >= 4:
                    pe.wait_ge(MX.up_copied, i - 3)
                b = ps[4 + i % 4]
                weights_still(pe, unit(BASE["uq"] + i), [b[:, 0:SEQ], b[:, SEQ:512]], 3, 8)
            for i in range(2):
                pe.wait_ge(MX.up_copied, 4 + 2 * i)
                banks = (ps[6], ps[7]) if i == 0 else (ps[4], ps[5])
                weights_still(pe, unit(BASE["kn"] + i), [b[:, c:c + SEQ] for b in banks for c in (0, SEQ)], 2, 11)
            pe.wait_ge(TR.ready, TB["gla"].ready + 2)
            for i in range(2):
                tokens_still(pe, unit(BASE["vm"] + i), ACC, [11 + i], 512, xhi, xlo, i == 0, i == 1)
            pe.wait_ge(MX.up_copied, 10)
            for i in range(2):
                pe.matmul(ps[4 + i][:], tabv("swap"), QP[:, 2 * i:2 * i + 2, :], start=True, stop=True)
            pe.matmul(ps[6][:, 0:SEQ], tabv("dup")[64:P, :], XB[64:P, :], start=True, stop=True)
            pe.matmul(ps[6][:, SEQ:512], tabv("dup_swap")[64:P, :], XB[64:P, :], start=True,
                      stop=True).then_inc(MX.rope_made, 1)
            pe.wait_ge(MX.roped, 1)
            turn_pe(pe, "gla", OG)
            pe.wait_ge(MX.up_copied, 14)
            for k in range(KD):
                pe.wait_ge(TR.lo, TB["gla"].split + k + 1)
                tokens_still(pe, unit(BASE["ogla"] + k), ACC, [k], 512, xhi, xlo, k == 0, k == KD - 1)

            def scores(h, bank):
                half = slice(h % 2 * 64, h % 2 * 64 + 64)
                for q, keys, cols in ((slice(0, P), slice(0, P), slice(0, P)),
                                      (slice(P, SEQ), slice(0, SEQ), slice(P, 384))):
                    pe.matmul(bank[:, cols], QN[:, h, q], KN[:, h, keys], start=True, stop=False)
                    mm = pe.matmul(bank[:, cols], QP[half, h // 2, q], KP[half, keys], start=False, stop=True)
                return mm

            pe.wait_ge(MX.ya_used, 4)
            attention_pe(pe, mla, scores, lambda h, t: VM[:, t, h * P:h * P + P])
            turn_pe(pe, "mla", mla.AO)
            for k in range(KD):
                pe.wait_ge(TR.lo, TB["mla"].split + k + 1)
                tokens_still(pe, unit(BASE["omla"] + k), ACC, [8 + k], 512, xhi, xlo, k == 0, k == KD - 1)
            turn_pe(pe, "mixed", GA)
            for k in range(KD):
                pe.wait_ge(TR.lo, TB["mixed"].split + k + 1)
                tokens_still(pe, unit(BASE["w2"] + k), ACC, [k], 512, xhi, xlo, k == 0, k == KD - 1)
            turn_pe(pe, "ffn2", scr)
            ffn_pe(pe, 2, False)

        def block2_act(act):
            def copy(last, dst, bank, func=ACT.Copy, scale=1.0, done=MX.copied):
                act.wait_ge(unit_done, last + 1)
                act.activation(dst, bank, func, scale=scale).then_inc(done, 1)

            act.wait_ge(FS[1].resid, 1)
            act.dma_start(W_A2[0:16, :], w_a2).then_inc(MX.w_a2, 16)
            norm_act(act, "final", FS[1].resid, lambda t: 2 * t + 2)
            norm_act(act, "mix", rescaled, lambda t: t + 1)
            turn_act(act, "mix")
            act.dma_start(scr[:].rearrange("p t c -> p (t c)"),
                          rows["b_gate"].broadcast_to([P, 2 * D])).then_inc(MX.row_gate, 16)
            for name, n, dst, b0, width in (("cq", 4, CQ, 0, QL), ("ckv", 2, CKV, 2, KVL)):
                for k in range(n - 1):
                    refill(act, BASE[name] + k)
                for t in range(NT):
                    copy(BASE[name] + n - 1, dst[:, t, :], ps[b0 + t][:, 0:width])
                refill(act, BASE[name] + n - 1)
            copy(BASE["x"], XB, ps[4][:, 0:SEQ])
            refill(act, BASE["x"])
            for h in range(GH):
                copy(BASE["gq"] + h, GQT[:, h, :], ps[(5, 6, 7, 4)[h]][:, 0:SEQ], scale=float(P) ** -0.5)
                refill(act, BASE["gq"] + h)
            act.wait_ge(MX.copied, 4)
            for i, (src, width) in enumerate(((CQ, QL), (CKV, KVL))):
                for t in range(NT):
                    act.activation(LX[:, t, 0:width], src[:, t, :], ACT.Square,
                                   accum_out=CSQ[:, 2 * i + t:2 * i + t + 1]).then_inc(MX.c_squares, 1)
                act.wait_ge(MX.c_squares, 2 * i + 2)
            act.wait_ge(MX.la_x, 1)
            act_link(act.activation(LT, LA, ACT.Abs))
            act_link(act.activation(LT, LT, ACT.Exp, scale=-1.0))
            act.activation(LT, LT, ACT.Ln, bias=ones[:, 0:1]).then_inc(MX.la_ln, 1)

            def chunk(c):
                name = CHUNKS[c]
                last = BASE[name[:-1]] + int(name[-1]) * 4 + 3
                for k in range(3, 0, -1):
                    refill(act, last - k)
                half = int(name[-1]) * 512
                dst, func = {"gk": (GK, ACT.Copy), "gv": (GV, ACT.Copy), "gg": (GG, ACT.Silu)}.get(name[:-1], (None, None))
                if dst is not None:
                    for t in range(NT):
                        copy(last, dst[:, t, half:half + 512], ps[c % 2 * 2 + t][:], func)
                refill(act, last)

            chunk(0)
            act.wait_ge(MX.suffix, 1)
            for t in range(NT):
                ins = act.activation(LX[:, t, :], ps[5 + t][:], ACT.Exp, scale=1.0 / 16.0)
            ins.then_inc(MX.decays, 1)
            act.activation(DC, ps[7][:, 0:16], ACT.Exp, scale=1.0 / 16.0).then_inc(MX.decays, 1)
            chunk(1)
            chunk(2)
            chunk(3)
            i = 0
            for n, (bank, name, ks, slot) in enumerate(((4, "q_norm", (0, 1), 8), (5, "q_norm", (2,), 10),
                                                        (6, "kv2_norm", (0, 1), 11))):
                act.wait_ge(MX.c_turned, n + 1)
                for i, k in enumerate(ks):
                    act.activation(xhi[:, slot + i, :], ps[bank][:, i * SEQ:i * SEQ + SEQ], ACT.Copy,
                                   scale=colv(name, k)).then_inc(MX.c_hi, 1)
            for c in range(4, 9):
                chunk(c)
            act.wait_ge(MX.gates_in, 8)
            for g in (GA, GB):
                act.activation(g, g, ACT.Sigmoid).then_inc(MX.sigmoid, 1)
            for h in range(NT * GH):
                if h % GH == 0:
                    act.wait_ge(MX.o, 2 * (h // GH) + 2)
                t, q = h // GH, h % GH
                act.activation(scr[:, t, q * GDV:q * GDV + GDV], ACC[t][q // 2][:, q % 2 * GDV:q % 2 * GDV + GDV],
                               ACT.Square, accum_out=OSQ[:, h:h + 1]).then_inc(MX.o_squares, 1)
            for i in range(6):
                dst = QN[:, 2 * i:2 * i + 2, :] if i < 4 else QP[:, 2 * i - 8:2 * i - 6, :]
                copy(BASE["uq"] + i, dst, ps[4 + i % 4][:].rearrange("p (a b) -> p a b", a=2), scale=192.0 ** -0.5, done=MX.up_copied)
                refill(act, BASE["uq"] + i)
            for i in range(4):
                copy(BASE["kn"] + i // 2, KN[:, 2 * i:2 * i + 2, :],
                     ps[(6, 7, 4, 5)[i]][:].rearrange("p (a b) -> p a b", a=2), done=MX.up_copied)
                if i % 2:
                    refill(act, BASE["kn"] + i // 2)
            refill(act, BASE["vm"])
            for i in range(4):
                copy(BASE["vm"] + 1, VM[:, i // 2, i % 2 * 512:i % 2 * 512 + 512], ACC[i // 2][i % 2], done=MX.up_copied)
            refill(act, BASE["vm"] + 1)
            turn_act(act, "gla")
            act.dma_start(row_post, rows["post_mix"].broadcast_to([P, D])).then_inc(MX.row_post, 16)
            act.dma_start(row_ffn, rows["post_ffn"].broadcast_to([P, D])).then_inc(MX.row_ffn, 16)
            for k in range(KD):
                refill(act, BASE["ogla"] + k)
            attention_act(act, mla)
            turn_act(act, "mla")
            for k in range(KD):
                refill(act, BASE["omla"] + k)
            turn_act(act, "mixed")
            for k in range(KD):
                refill(act, BASE["w2"] + k)
            for i in range(4):
                copy(BASE["w2"] + 7, MIXED[:, i // 2, i % 2 * 512:i % 2 * 512 + 512], ACC[i // 2][i % 2], done=MX.w2_copied)
            norm_act(act, "post_mix", MX.w2_copied, lambda t: 2 * t + 2, MIXED)
            norm_act(act, "ffn2", rescaled, lambda t: t + 3)
            turn_act(act, "ffn2")
            ffn_act(act, 2, False)
            for i in range(4):
                copy(UNITS - 1, MIXED[:, i // 2, i % 2 * 512:i % 2 * 512 + 512], ACC[i // 2][i % 2], done=MX.w2_copied)
            norm_act(act, "post_ffn", MX.w2_copied, lambda t: 2 * t + 6, MIXED)

        def block2_dve(dve):
            dve.wait_ge(SW.row_final, 16)
            norm_dve(dve, "final", row_final)
            norm_dve(dve, "mix")
            turn_dve(dve, "mix")
            dve.wait_ge(MX.la_made, 1)
            dve.wait_ge(SW.row_b, 16)
            for t in range(NT):
                ins = dve.tensor_tensor(LA[:, t, :], ps[5 + t][:], row_b_a2, ALU.add)
            ins.then_inc(MX.la_x, 1)
            dve.wait_ge(MX.la_ln, 1)
            dve.scalar_tensor_tensor(LA, LA, 0.0, LT, ALU.min, ALU.subtract).then_inc(MX.la, 1)
            dve.wait_ge(MX.c_squares, 4)
            for i, (src, width) in enumerate(((CQ, QL), (CKV, KVL))):
                ss, r = CSQ[:, 2 * i:2 * i + 2], CSQ[:, 4 + 2 * i:6 + 2 * i]
                inverse_root(dve, r, ss, width * EPS, root_tmp[:, 0:2])
                for t in range(NT):
                    ins = dve.tensor_scalar(src[:, t, :], src[:, t, :], r[:, t:t + 1], None, ALU.mult)
            ins.then_inc(MX.c_ready, 1)
            dve.wait_ge(MX.decays, 1)
            dve.wait_ge(MX.copied, 11)
            dve.tensor_tensor(GK, GK, LX, ALU.mult).then_inc(MX.kdec, 1)
            n = 0
            for bank, name, ks, slot in ((4, "q_norm", (0, 1), 8), (5, "q_norm", (2,), 10), (6, "kv2_norm", (0, 1), 11)):
                n += len(ks)
                dve.wait_ge(MX.c_hi, n)
                for i, k in enumerate(ks):
                    dve.scalar_tensor_tensor(xlo[:, slot + i, :], ps[bank][:, i * SEQ:i * SEQ + SEQ], colv(name, k),
                                             xhi[:, slot + i, :].bitcast(F32), ALU.mult, ALU.subtract).then_inc(MX.c_lo, 1)
            dve.wait_ge(MX.row_gate, 16)
            for c in range(4):
                dve.wait_ge(unit_done, BASE["gates"] + 4 * c + 4)
                for t in range(NT):
                    dve.tensor_tensor((GA, GB)[c // 2][:, t, c % 2 * 512:c % 2 * 512 + 512],
                                      ps[(c + 1) % 2 * 2 + t][:], scr[:, c // 2, c % 2 * 512:c % 2 * 512 + 512],
                                      ALU.add).then_inc(MX.gates_in, 1)
            dve.wait_ge(MX.decays, 2)
            for c in range(2 * NT):
                dve.wait_ge(MX.kv, c + 1)
                if c >= 2:
                    dve.wait_ge(MX.o, c - 1)
                if c:
                    dve.wait_ge(MX.state, c)
                for h in range(GH):
                    new, old = (ST[:, i % 2, h * GDV:h * GDV + GDV] for i in (c, c + 1))
                    kv = ps[4 + c % 2 * 2 + h // 2][:, h % 2 * GDV:h % 2 * GDV + GDV]
                    i = (c // 2 * GH + h) * 2 + c % 2
                    if c == 0:
                        ins = dve.tensor_copy(new, kv)
                    else:
                        ins = dve.scalar_tensor_tensor(new, old, DC[:, i:i + 1], kv, ALU.mult, ALU.add)
                ins.then_inc(MX.state, 1)
            dve.wait_ge(MX.o_squares, 8)
            inverse_root(dve, OSQ[:, 8:16], OSQ[:, 0:8], GDV * EPS, root_tmp[:, 0:8])
            for t in range(NT):
                for half in range(2):
                    i = 8 + t * GH + half * 2
                    o = OG[:, t, half * 512:half * 512 + 512]
                    dve_link(dve.tensor_tensor(o.rearrange("p (h c) -> p h c", h=2),
                                               ACC[t][half].rearrange("p (h c) -> p h c", h=2),
                                               OSQ[:, i:i + 2].unsqueeze(2).broadcast_to([P, 2, GDV]), ALU.mult))
                    ins = dve.tensor_tensor(o, o, GG[:, t, half * 512:half * 512 + 512], ALU.mult)
                ins.then_inc(TR.ready, 1)
            dve.wait_ge(MX.rope_made, 1)
            dve.wait_ge(IN.rope, 1)
            dve.wait_ge(IN.sin, 2)
            part = scr[:, 0, :].rearrange("p (a b) -> p a b", a=4)
            kpart = scr[:, 1, 0:SEQ]
            for i in range(2):
                dve.tensor_tensor(part[:, 2 * i:2 * i + 2, :], ps[4 + i][:].rearrange("p (a b) -> p a b", a=2),
                                  sinT[:].unsqueeze(1).broadcast_to([P, 2, SEQ]), ALU.mult)
            dve.tensor_tensor(QP, QP, cosT[:].unsqueeze(1).broadcast_to([P, 4, SEQ]), ALU.mult)
            dve.tensor_tensor(kpart, ps[6][:, SEQ:512], sinT[:], ALU.mult)
            dve_link(dve.tensor_tensor(KP, ps[6][:, 0:SEQ], cosT[:], ALU.mult))
            dve.tensor_tensor(QP, QP, part, ALU.add)
            dve.tensor_tensor(KP, KP, kpart, ALU.add).then_inc(MX.roped, 1)
            turn_dve(dve, "gla")
            dve.wait_ge(MX.sigmoid, 2)
            dve.wait_ge(unit_done, BASE["ogla"] + KD)
            for t in range(NT):
                for half in range(2):
                    g = GA[:, t, half * 512:half * 512 + 512]
                    dve.tensor_tensor(g, g, ACC[t][half], ALU.mult).then_inc(MX.ya_used, 1)
            mask = tabv("chunk_mask")
            attention_dve(dve, mla, lambda h, t: mask[:, PARTS[t]], lambda h: -BIG)
            attention_finish(dve, mla, lambda: None)
            turn_dve(dve, "mla")
            dve.wait_ge(unit_done, BASE["omla"] + KD)
            dve.wait_ge(MX.ya_used, 4)
            for t in range(NT):
                for half in range(2):
                    a, b = (g[:, t, half * 512:half * 512 + 512] for g in (GA, GB))
                    dve_link(dve.tensor_tensor(b, b, ACC[t][half], ALU.mult))
                    ins = dve.tensor_tensor(a, a, b, ALU.add)
                ins.then_inc(TR.ready, 1)
            turn_dve(dve, "mixed")
            dve.wait_ge(MX.row_post, 16)
            norm_dve(dve, "post_mix", row_post, MIXED)
            norm_dve(dve, "ffn2")
            turn_dve(dve, "ffn2")
            ffn_dve(dve, 2, False)
            dve.wait_ge(MX.row_ffn, 16)
            norm_dve(dve, "post_ffn", row_ffn, MIXED)
        IN = sems("in", "tabs cols small wba pos rel x0 x1 wba_hi band_ps band band_out sin scaled rope angle")
        wba_ready = sem("wba_ready")
        wba_raw, _o = carve(0, KD * 32)
        rel = sb("rel", [P, 16])
        band = sb("band", [P, 384])
        ang, _o = carve(_o, SEQ)
        turns, _o = carve(_o, SEQ)
        posi = area[:, _o:_o + SEQ].bitcast(I32)

        def load_parameters(act):
            act.dma_start(resid[:, 0, :], x[0:P, :]).then_inc(IN.x0, 16)
            act.dma_start(resid[:, 1, :], x[P:SEQ, :]).then_inc(IN.x1, 16)
            act.dma_start(tab[:], tabs).then_inc(IN.tabs, 16)
            act.dma_start(col[:], cols).then_inc(IN.cols, 16)
            act.dma_start(wba_raw, w_ba).then_inc(IN.wba, 16)
            act.dma_start(small[:], rows["small"].broadcast_to([P, 48])).then_inc(IN.small, 16)
            act.dma_start(rel[0:32, :], rel_table).then_inc(IN.rel, 16)
            act.dma_start(posi, positions.broadcast_to([P, SEQ])).then_inc(IN.pos, 16)

        def start_act(act):
            act.wait_ge(IN.wba, 16)
            act.activation(wba_hi[:], wba_raw, ACT.Copy).then_inc(IN.wba_hi, 1)
            for k in range(RING):
                round_unit(act, unit(k))

        def start_act_late(act):
            act.wait_ge(IN.band, 1)
            act.dma_start(band_scratch, band[0:16, :].unsqueeze(1).broadcast_to([16, P, 384])).then_inc(IN.band_out, 16)
            for n, dst in enumerate((sinT, cosT)):
                act.wait_ge(IN.angle, n + 1)
                act.activation(dst[:], dst[:], ACT.Sin).then_inc(IN.sin, 1)

        def start_pe(pe):
            pe.wait_ge(IN.tabs, 16)
            pe.wait_ge(IN.rel, 16)
            pe.wait_ge(IN.scaled, 1)
            pe.matmul(ps[1][0:16, 0:BANDX], rel[0:33, :], tabv("buckets")[0:33, 0:BANDX], start=True,
                      stop=True).then_inc(IN.band_ps, 1)

        def start_dve(dve):
            dve.memset(rel[32:33, :], -BIG).then_inc(IN.scaled, 1)
            dve.wait_ge(IN.wba, 16)
            dve.wait_ge(IN.wba_hi, 1)
            dve.tensor_tensor(wba_lo[:], wba_raw, wba_hi[:].bitcast(F32), ALU.subtract).then_inc(wba_ready, 1)
            dve_link(dve.memset(band[0:16, :], 0.0))
            dve.wait_ge(IN.band_ps, 1)
            dve.tensor_copy(band[0:16, 0:BANDX], ps[1][0:16, 0:BANDX]).then_inc(IN.band, 1)
            dve.wait_ge(IN.cols, 16)

        def start_dve_late(dve):
            for name, n, width in (("out_norm", 1, HD), ("gla_norm", 2, GDV), ("q_norm", 3, QL), ("kv2_norm", 2, KVL)):
                c = col[:, COL[name]:COL[name] + n]
                dve_link(dve.tensor_scalar(c, c, float(width) ** 0.5, None, ALU.mult))
            dve.wait_ge(IN.pos, 16)
            dve_link(dve.tensor_copy(ang, posi))
            dve_link(dve.tensor_scalar(ang, ang, colv("inv_freq"), None, ALU.mult))
            c1, c2 = 6.28125, float(np.float32(int((2 * np.pi - 6.28125) * 2 ** 20) / 2 ** 20))
            c3 = float(2 * np.pi - c1 - c2)
            magic = 1.5 * 2.0 ** 23
            for dst, quarter in ((sinT, 0.0), (cosT, 0.25)):
                dve_link(dve.tensor_scalar(turns, ang, float(0.5 / np.pi), quarter, ALU.mult, ALU.add))
                dve_link(dve.tensor_scalar(turns, turns, magic, -magic, ALU.add, ALU.add))
                dve_link(dve.scalar_tensor_tensor(dst[:], turns, -c1, ang, ALU.mult, ALU.add))
                dve_link(dve.scalar_tensor_tensor(dst[:], turns, -c2, dst[:], ALU.mult, ALU.add))
                dve_link(dve.scalar_tensor_tensor(dst[:], turns, -c3, dst[:], ALU.mult, ALU.add))
                dve_link(dve.tensor_scalar(dst[:], dst[:], quarter * 2 * np.pi, float(np.float32(3.1415925)), ALU.add, ALU.min))
                dve.tensor_scalar(dst[:], dst[:], -float(np.float32(3.1415925)), None, ALU.max).then_inc(IN.angle, 1)
            dve.wait_ge(IN.sin, 1)
            dve.tensor_scalar(sinT[:], sinT[:], colv("rope_sign"), None, ALU.mult).then_inc(IN.rope, 1)
        out_done = sem("out_done")
        block = ctx.enter_context(nc.Block())

        @block.sync
        def _(sp):
            for k in range(RING):
                load_unit(sp, unit(k))
            with sp.Fori(1, UNITS // RING) as i:
                for k in range(RING):
                    load_unit(sp, unit(k, i))
            for k in range(UNITS // RING * RING, UNITS):
                load_unit(sp, unit(k))
            for t in range(NT):
                sp.wait_ge(rescaled, 2 * NT + t + 1)
                sp.dma_start(out[t * P:t * P + P, :], resid[:, t, :]).then_inc(out_done, 16)
            sp.wait_ge(out_done, 16 * NT)

        @block.gpsimd
        def _(pool):
            for k in range(RING):
                rest_of_unit(pool, unit(k))
            with pool.Fori(1, UNITS // RING) as i:
                for k in range(RING):
                    rest_of_unit(pool, unit(k, i))
            for k in range(UNITS // RING * RING, UNITS):
                rest_of_unit(pool, unit(k))

        @block.scalar
        def _(act):
            load_parameters(act)
            start_act(act)
            act.wait_ge(IN.x0, 16)
            norm_act(act, "a", IN.x1, lambda t: 16)
            turn_act(act, "a")
            gates_act(act)
            start_act_late(act)
            qkv_act(act)
            delta_act(act)
            act.wait_ge(DN.resid, 1)
            swa_load(act)
            norm_act(act, "ffn0", DN.resid, lambda t: 2 * t + 2)
            turn_act(act, "ffn0")
            ffn_act(act, 0, True)
            norm_act(act, "b", FS[0].resid, lambda t: 2 * t + 2)
            turn_act(act, "b")
            swa_act(act)
            norm_act(act, "ffn1", SW.resid, lambda t: 2 * t + 2)
            turn_act(act, "ffn1")
            ffn_act(act, 1, True)
            block2_act(act)

        @block.tensor
        def _(pe):
            start_pe(pe)
            turn_pe(pe, "a", scr)
            qkv_pe(pe)
            delta_pe(pe)
            turn_pe(pe, "ffn0", scr)
            ffn_pe(pe, 0, True)
            turn_pe(pe, "b", scr)
            swa_pe(pe)
            turn_pe(pe, "ffn1", scr)
            ffn_pe(pe, 1, True)
            block2_pe(pe)

        @block.vector
        def _(dve):
            start_dve(dve)
            norm_dve(dve, "a")
            turn_dve(dve, "a")
            gates_dve(dve)
            start_dve_late(dve)
            qkv_dve(dve)
            delta_dve(dve)
            norm_dve(dve, "ffn0")
            turn_dve(dve, "ffn0")
            ffn_dve(dve, 0, True)
            add_residual(dve, BASE["kv"] - 1, FS[0].resid)
            norm_dve(dve, "b")
            turn_dve(dve, "b")
            swa_dve(dve)
            norm_dve(dve, "ffn1")
            turn_dve(dve, "ffn1")
            ffn_dve(dve, 1, True)
            add_residual(dve, BASE["cq"] - 1, FS[1].resid)
            block2_dve(dve)




def t5_buckets(dist):
    n = np.maximum(dist, 0)
    nf = np.maximum(n, 1).astype(np.float32)
    scale = np.float32(np.log(128 / 16))
    large = 16 + (np.log(nf / np.float32(16)) / scale * np.float32(16)).astype(np.int32)
    return np.where(n < 16, n, np.minimum(large, 31))


def tables():
    i, j = np.arange(P)[:, None], np.arange(P)[None, :]
    t = {"ident": i == j, "ones": np.ones((P, P)), "tri": i <= j,
         "future": np.where(j >= i, 0.0, -BIG), "later": (i > j) & (i // 64 == j // 64),
         "swap": i == (j ^ 32), "dup": i == 64 + j % 64, "dup_swap": i == 64 + (j % 64 ^ 32)}
    levels = []
    for lv in range(LEVELS):
        s = 1 << lv
        left = np.array([c for c in range(P) if not c & s])[None, :]
        levels.append((i // (2 * s) == left // (2 * s)) & (i & s > 0))
    t["levels"] = np.concatenate(levels, 1)
    k = np.arange(SEQ)[None, :]
    t["chunk_mask"] = np.concatenate([np.where(j // 64 <= i // 64, 0.0, -BIG),
                                      np.where(k // 64 <= (P + i) // 64, 0.0, -BIG)], 1)
    off = np.arange(384)[None, :]
    dist = 255 - off
    inside = (dist >= 0) & (dist < 128)
    t["buckets"] = np.where(i < 32, inside & (t5_buckets(dist) == i), (i == 32) & ~inside)
    return np.concatenate([t[name].astype(np.float32) for name, _ in TABS], 1)


def still(w, blocks_per_unit=1, pad_to=UNIT):
    kt, nb = w.shape[0] // P, w.shape[1] // P
    u = w.reshape(kt, P, nb // blocks_per_unit, blocks_per_unit, P).transpose(2, 1, 3, 0, 4)
    u = u.reshape(u.shape[0], P, -1)
    return np.pad(u, ((0, 0), (0, 0), (0, pad_to - u.shape[2])))


def moving(w, kts, width):
    kt, nc_ = w.shape[0] // P, w.shape[1] // width
    u = w.reshape(kt // kts, kts, P, nc_, width).transpose(3, 0, 2, 1, 4).reshape(-1, P, kts * width)
    return np.pad(u, ((0, 0), (0, 0), (0, UNIT - u.shape[2])))


def ffn_units(up_gate, up_val, down):
    g, v, d = still(up_gate), still(up_val), moving(down, 1, D)
    order = [g[0], v[0], g[1], v[1], d[0]]
    for j in range(2, NF):
        order += [g[j], v[j], d[j - 1]]
    return np.stack(order + [d[NF - 1]])


def lay_out(a):
    f = {k: np.asarray(v) for k, v in a.items()}
    w_in = f["a_w_in"][0]
    k_first = np.concatenate([w_in[:, 1024:2048], w_in[:, 0:1024], w_in[:, 2048:4096]], 1)
    heads_ = [4 * (2 * gp + half) + r for gp in range(2) for r in range(4) for half in range(2)]
    perm = np.concatenate([np.arange(h * AHD, h * AHD + AHD) for h in heads_])
    w2 = f["w_in_2"][0]
    cut = np.cumsum([0, 512, 512, 1024, 1024, 16, QL, KVL, 64])
    gq, gk, gv, gg, ga, cq, ckv, kpe = (w2[:, cut[i]:cut[i + 1]] for i in range(8))
    wx = np.concatenate([ga, np.zeros((D, 48), np.float32), kpe], 1)
    uq = f["w_uq_2"][0].reshape(QL, MH, 192)
    uq = np.concatenate([uq[:, :, :128].reshape(QL, 1024), uq[:, :, 128:].reshape(QL, 512)], 1)
    ukv = f["w_ukv_2"][0].reshape(KVL, MH, 256)
    up, down = f["ffn_w_up"], f["ffn_w_down"]
    parts = {
        "qkv": still(k_first), "z": moving(w_in[:, 4096:6144], 2, 512), "wout": moving(f["a_w_out"][0], 1, D),
        "ffn0": ffn_units(up[0][:, :FF], up[0][:, FF:], down[0]),
        "kv": np.concatenate([still(f["w_kv"][:, :256]), moving(f["w_kv"][:, 256:], 4, 256)]),
        "wq": still(f["b_w_q"][0][:, perm]), "wo": moving(f["b_w_o"][0][perm], 1, D),
        "ffn1": ffn_units(up[1][:, :FF], up[1][:, FF:], down[1]),
        "cq": moving(cq, 2, QL), "ckv": moving(ckv, 4, KVL), "x": still(wx), "gq": still(gq),
        "gk": moving(gk, 2, 512), "gv": moving(gv, 2, 512), "gg": moving(gg, 2, 512),
        "gates": moving(f["w_gate_2"][0], 2, 512), "uq": still(uq, 2),
        "kn": still(ukv[:, :, :128].reshape(KVL, 1024), 4), "vm": moving(ukv[:, :, 128:].reshape(KVL, 1024), 1, D),
        "ogla": moving(f["w_o_gla_2"][0], 1, D), "omla": moving(f["w_o_mla_2"][0], 1, D),
        "w2": moving(f["w_out_2"][0], 1, D),
        "ffn2": ffn_units(f["w_ffn_gate_2"][0], f["w_ffn_up_2"][0], f["w_ffn_down_2"][0]),
    }
    for name, n in PLAN:
        assert parts[name].shape == (n, P, UNIT), (name, parts[name].shape)
    stream = np.concatenate([parts[name] for name, _ in PLAN])

    def by_partition(v):
        return v.reshape(-1, P).T

    cw = f["a_conv_w"][0]
    cw = np.concatenate([cw[:, 1024:2048], cw[:, 0:1024], cw[:, 2048:]], 1)
    i = np.arange(P)
    inv_freq = (1.0 / (10000.0 ** (np.arange(0, 64, 2, dtype=np.float32) / np.float32(64)))).astype(np.float32)
    c = {
        "a_norm": by_partition(f["a_norm_w"][0]), "ffn0_norm": by_partition(f["ffn_norm_w"][0]),
        "kv_norm": by_partition(f["kv_norm_w"]), "b_norm": by_partition(f["b_norm_w"][0]),
        "ffn1_norm": by_partition(f["ffn_norm_w"][1]), "pre_mix": by_partition(f["pre_mix_norm_2"][0]),
        "pre_ffn": by_partition(f["pre_ffn_norm_2"][0]), "out_norm": by_partition(f["a_out_norm_w"][0]),
        "gla_norm": by_partition(f["gla_norm_2"][0]), "q_norm": by_partition(f["q_norm_2"][0]),
        "kv2_norm": by_partition(f["kv_norm_2"][0]), "conv_a": by_partition(cw),
        "conv0": by_partition(f["ffn_conv_w"][0]), "bias0": by_partition(f["ffn_conv_b"][0]),
        "conv1": by_partition(f["ffn_conv_w"][1]), "bias1": by_partition(f["ffn_conv_b"][1]),
        "left": np.stack([np.where(i & (1 << lv), 0.0, -1.0) for lv in range(LEVELS)], 1),
        "inv_freq": inv_freq[i % 32][:, None], "rope_sign": np.where(i % 64 < 32, -1.0, 1.0)[:, None],
        "chunk_of": np.stack([i // 64 == 0, i // 64 == 1], 1),
    }
    cols = np.concatenate([c[name].astype(np.float32) for name, _ in COLS], 1)
    w_ba = w_in[:, 6144:6176].reshape(KD, P, 32).transpose(1, 0, 2).reshape(P, KD * 32)
    r = {"small": np.concatenate([f["a_dt_bias"], f["a_a_log"], f["b_sinks"][:, heads_]], 1),
         "final": f["final_norm_w"][None], "b_gate": f["b_gate_2"], "b_a2": f["b_a2_2"],
         "post_mix": f["post_mix_norm_2"], "post_ffn": f["post_ffn_norm_2"]}
    arrays = {"x": f["x"][0], "stream": stream, "w_ba": w_ba, "cols": cols, "tabs": tables(),
              "w_a2": f["w_a2_2"][0], "rel_table": f["rel_bias_table"][:, heads_], "positions": f["positions_2"]}
    arrays.update({"row_" + k: v for k, v in r.items()})
    return {k: np.ascontiguousarray(v) for k, v in arrays.items()}


def kernel(**inputs):
    import concourse.bacc as _bacc
    from concourse.bass_utils import run_bass_kernel_spmd as _run

    nc = _bacc.Bacc("TRN2", target_bir_lowering=False, num_devices=1, dynamic_dma_scratch_size=1024)
    arrays = {f"in_{k}": v for k, v in lay_out(inputs).items()}
    ap = {k: nc.dram_tensor(k, v.shape, mybir.dt.from_np(v.dtype), kind="ExternalInput").ap()
          for k, v in arrays.items()}
    out = nc.dram_tensor("out_0", (SEQ, D), F32, kind="ExternalOutput").ap()
    band_scratch = nc.dram_tensor("band_scratch", (AH, P, 384), F32).ap()
    rows = {k[7:]: v for k, v in ap.items() if k.startswith("in_row_")}
    build(nc, ap["in_x"], ap["in_stream"], ap["in_w_ba"], ap["in_cols"], ap["in_tabs"], rows, ap["in_w_a2"],
          ap["in_rel_table"], ap["in_positions"], out, band_scratch)
    r = _run(nc, [arrays], core_ids=[0])
    return r.results[0]["out_0"].reshape(1, SEQ, D)
```

```python
from contextlib import ExitStack

import numpy as np

import concourse.bass as bass
from concourse import mybir

F32 = mybir.dt.float32
F32R = mybir.dt.float32r
I32 = mybir.dt.int32
ALU = mybir.AluOpType
ACT = mybir.ActivationFunctionType
AX = mybir.AxisListType

P = 128
SEQ, NT = 256, 2
D, KD = 1024, 8
UNIT = 1024
RING = 6
EPS = 1e-6
BIG = 1e30

VH = 16
QKH = 8
HD = 128
FF, NF = 2816, 22
AH, AHD = 16, 64
LEVELS = 7
GH, GDV = 4, 256
MH = 8
QL, KVL = 384, 256
BANDX = 383

PLAN = [("ba", 1), ("qkv", 32), ("z", 16), ("wout", 16), ("ffn0", 3 * NF), ("kv", 4), ("wq", 8), ("wo", 8),
        ("ffn1", 3 * NF), ("cq", 4), ("ckv", 2), ("x", 1), ("gq", 4), ("gk", 4), ("gv", 8),
        ("gg", 8), ("gates", 16), ("uq", 6), ("kn", 2), ("vm", 2), ("ogla", 8), ("omla", 8),
        ("w2", 8), ("ffn2", 3 * NF)]
BASE, _n = {}, 0
for _name, _count in PLAN:
    BASE[_name] = _n
    _n += _count
UNITS = _n

COLS = [("a_norm", 8), ("ffn0_norm", 8), ("kv_norm", 8), ("b_norm", 8), ("ffn1_norm", 8),
        ("pre_mix", 8), ("pre_ffn", 8), ("out_norm", 1), ("gla_norm", 2), ("q_norm", 3),
        ("kv2_norm", 2), ("conv_a", 32 * 4), ("conv0", 44 * 3), ("bias0", 44), ("conv1", 44 * 3),
        ("bias1", 44), ("left", LEVELS), ("inv_freq", 1), ("rope_sign", 1), ("chunk_of", 2)]
COL, _n = {}, 0
for _name, _count in COLS:
    COL[_name] = _n
    _n += _count
NCOLS = _n

TABS = [("ident", 128), ("buckets", 384), ("ones", 128), ("tri", 128), ("future", 128), ("levels", LEVELS * 64),
        ("later", 128), ("chunk_mask", 384), ("swap", 128), ("dup", 128), ("dup_swap", 128)]
TAB, _n = {}, 0
for _name, _count in TABS:
    TAB[_name] = _n
    _n += _count
NTABS = _n


class Named(dict):

    def __getattr__(self, name):
        return self[name]


def unit(k, i=0):
    return Named(u=k + RING * i, q=k // RING + i, s=k % RING,
                           first=isinstance(i, int) and k + RING * i < RING)


def build(nc, x, stream, cols, tabs, rows, w_a2, rel_table, positions, out, band_scratch):
    with ExitStack() as ctx:
        def sb(name, shape, dt=F32):
            return ctx.enter_context(nc.sbuf_tensor(name, shape, dt))

        def sem(name):
            return ctx.enter_context(nc.semaphore(name))

        def sems(stage, names):
            return Named(**{n: sem(f"{stage}_{n}") for n in names.split()})

        raw = sb("raw", [P, RING, UNIT])
        whi = sb("whi", [P, RING, UNIT], F32R)
        wlo = sb("wlo", [P, RING, UNIT], F32R)
        xhi = sb("xhi", [P, 16, SEQ], F32R)
        xlo = sb("xlo", [P, 16, SEQ], F32R)
        fhi = sb("fhi", [P, 2, SEQ], F32R)
        flo = sb("flo", [P, 2, SEQ], F32R)
        resid = sb("resid", [P, NT, D])
        scr = sb("scr", [P, NT, D])
        col = sb("col", [P, NCOLS])
        tab = sb("tab", [P, NTABS])
        cosT = sb("cosT", [P, SEQ])
        sinT = sb("sinT", [P, SEQ])
        small = sb("small", [P, 48])
        stat = sb("stat", [P, 64])
        AREA = 19100
        area = sb("area", [P, AREA])

        def carve(offset, *shape):
            n = int(np.prod(shape))
            assert offset + n <= AREA, (offset, n)
            v = area[:, offset:offset + n]
            if len(shape) == 2:
                v = v.rearrange("p (a b) -> p a b", a=shape[0])
            if len(shape) == 3:
                v = v.rearrange("p (a b c) -> p a b c", a=shape[0], b=shape[1])
            return v, offset + n

        ps = [ctx.enter_context(nc.psum_tensor(f"bank{b}", [P, 512], F32)) for b in range(8)]

        def tabv(name):
            n = dict(TABS)[name]
            return tab[:, TAB[name]:TAB[name] + n]

        def colv(name, i=0, step=1):
            c = COL[name] + i
            return col[:, c:c + 1] if isinstance(c, int) else col[:, bass.ds(c, 1)]

        ident, ones, tri = tabv("ident"), tabv("ones"), tabv("tri")

        landed = [sem(f"landed{s}") for s in range(RING)]
        hi_ready, lo_ready, unit_done = sem("hi_ready"), sem("lo_ready"), sem("unit_done")

        def load_unit(sp, n):
            if not n.first:
                sp.wait_ge(lo_ready, n.u - RING + 1)
            src = stream[n.u] if isinstance(n.u, int) else stream[bass.ds(n.u, 1)].rearrange("a p c -> p (a c)")
            sp.dma_start(raw[:, n.s, :], src).then_inc(landed[n.s], 16)

        def round_unit(act, n):
            act.wait_ge(landed[n.s], 16 * n.q + 16)
            if not n.first:
                act.wait_ge(unit_done, n.u - RING + 1)
            act.activation(whi[:, n.s, :], raw[:, n.s, :], ACT.Copy).then_inc(hi_ready, 1)

        def rest_of_unit(pool, n):
            pool.wait_ge(hi_ready, n.u + 1)
            pool.tensor_tensor(wlo[:, n.s, :], raw[:, n.s, :], whi[:, n.s, :].bitcast(F32),
                               ALU.subtract).then_inc(lo_ready, 1)

        def refill(act, n):
            k = n if isinstance(n, Named) else unit(n)
            if isinstance(k.u, int) and k.u + RING >= UNITS:
                return
            round_unit(act, Named(u=k.u + RING, q=k.q + 1, s=k.s, first=False))

        def three(out_ap, a_hi, a_lo, b_hi, b_lo, start, stop):
            nc.tensor.matmul(out_ap, a_hi, b_hi, start=start, stop=False)
            nc.tensor.matmul(out_ap, a_hi, b_lo, start=False, stop=False)
            return nc.tensor.matmul(out_ap, a_lo, b_hi, start=False, stop=stop)

        def weights_still(pe, n, outs, kts, xs):
            pe.wait_ge(lo_ready, n.u + 1)
            i = 0
            for o in outs:
                for k in range(kts):
                    w = slice(i * P, i * P + P)
                    mm = three(o, whi[:, n.s, w], wlo[:, n.s, w], xhi[:, xs + k, :], xlo[:, xs + k, :],
                               k == 0, k == kts - 1)
                    i += 1
            mm.then_inc(unit_done, 1)

        def tokens_still(pe, n, banks, slots, width, ah, al, first, last):
            pe.wait_ge(lo_ready, n.u + 1)
            halves = len(banks[0])
            for t in range(NT):
                tok = slice(t * P, t * P + P)
                for h in range(halves):
                    for i, k in enumerate(slots):
                        w0 = (i * halves + h) * width
                        w = slice(w0, w0 + width)
                        mm = three(banks[t][h], ah[:, k, tok], al[:, k, tok], whi[:, n.s, w],
                                   wlo[:, n.s, w], first and i == 0, last and i == len(slots) - 1)
            mm.then_inc(unit_done, 1)

        def chain(eng, name):
            s, n = sem(name), [0]

            def link(ins):
                n[0] += 1
                ins.then_inc(s, 1)
                eng.wait_ge(s, n[0])
            return link

        dve_link = chain(nc.vector, "dve_chain")
        act_link = chain(nc.scalar, "act_chain")
        root_tmp = sb("root_tmp", [P, 32])

        def inverse_root(dve, y, w, eps, tmp):
            dve_link(dve.tensor_scalar(w, w, eps, None, ALU.add))
            dve_link(dve.tensor_scalar(tmp.bitcast(I32), w.bitcast(I32), 1, None, ALU.logical_shift_right))
            dve_link(dve.tensor_scalar(y.bitcast(I32), tmp.bitcast(I32), -1.0, float(0x5F3759DF), ALU.mult, ALU.add))
            for _ in range(3):
                dve_link(dve.tensor_tensor(tmp, y, w, ALU.mult))
                dve_link(dve.scalar_tensor_tensor(tmp, tmp, -0.5, y, ALU.mult, ALU.mult))
                dve_link(dve.scalar_tensor_tensor(y, tmp, 1.5, y, ALU.add, ALU.mult))

        TURNS = {"a": [("a_norm", 0)], "ffn0": [("ffn0_norm", 0)], "b": [("kv_norm", 0), ("b_norm", 8)],
                 "attn": [(None, 0)], "ffn1": [("ffn1_norm", 0)], "mix": [("pre_mix", 0)],
                 "gla": [("gla_norm", 0)], "mla": [(None, 8)], "mixed": [(None, 0)],
                 "ffn2": [("pre_ffn", 0)]}
        TR = sems("turn", "ready turned hi lo")
        TB, _i, _c = {}, 0, 0
        for _k, _v in TURNS.items():
            _c += 8 * len(_v)
            TB[_k] = Named(ready=2 * _i, turned=4 * _i, split=_c - 8 * len(_v), done=_c)
            _i += 1

        def weight_of(name, k):
            return 1.0 if name is None else colv(name, k % 2 if name == "gla_norm" else k)

        def turn_pe(pe, key, src):
            for pair in range(4):
                for t in range(NT):
                    if pair == 0:
                        pe.wait_ge(TR.ready, TB[key].ready + t + 1)
                    for k in (2 * pair, 2 * pair + 1):
                        c = k % 2 * SEQ + t * P
                        mm = pe.transpose(ps[4 + pair][:, c:c + P], src[:, t, k * P:k * P + P], ident)
                mm.then_inc(TR.turned, 1)

        def turn_act(act, key):
            for pair in range(4):
                act.wait_ge(TR.turned, TB[key].turned + pair + 1)
                for name, slot in TURNS[key]:
                    for k in (2 * pair, 2 * pair + 1):
                        act.activation(xhi[:, slot + k, :], ps[4 + pair][:, k % 2 * SEQ:k % 2 * SEQ + SEQ],
                                       ACT.Copy, scale=weight_of(name, k)).then_inc(TR.hi, 1)

        def turn_dve(dve, key):
            for pair in range(4):
                n = len(TURNS[key])
                dve.wait_ge(TR.hi, TB[key].split + 2 * n * (pair + 1))
                for name, slot in TURNS[key]:
                    for k in (2 * pair, 2 * pair + 1):
                        dve.scalar_tensor_tensor(
                            xlo[:, slot + k, :], ps[4 + pair][:, k % 2 * SEQ:k % 2 * SEQ + SEQ],
                            weight_of(name, k), xhi[:, slot + k, :].bitcast(F32), ALU.mult,
                            ALU.subtract).then_inc(TR.lo, 1)

        NORMS = {k: i for i, k in enumerate(["a", "ffn0", "b", "ffn1", "final", "mix", "post_mix",
                                             "ffn2", "post_ffn"])}
        squares, rescaled = sem("squares"), sem("rescaled")

        def norm_act(act, key, ready, value, src=resid):
            st = 4 * NORMS[key]
            for t in range(NT):
                act.wait_ge(ready, value(t))
                act.activation(scr[:, t, :], src[:, t, :], ACT.Square,
                               accum_out=stat[:, st + t:st + t + 1]).then_inc(squares, 1)

        def norm_dve(dve, key, row=None, src=resid):
            i, st = NORMS[key], 4 * NORMS[key]
            dve.wait_ge(squares, NT * (i + 1))
            inverse_root(dve, stat[:, st + 2:st + 4], stat[:, st:st + 2], D * EPS, root_tmp[:, 0:2])
            for t in range(NT):
                r = stat[:, st + 2 + t:st + 3 + t]
                ins = dve.tensor_scalar(scr[:, t, :], src[:, t, :], r, float(D) ** 0.5, ALU.mult, ALU.mult)
                if row is None:
                    ins.then_inc(TR.ready, 1)
                elif key == "final":
                    dve_link(ins)
                    dve.tensor_tensor(resid[:, t, :], scr[:, t, :], row, ALU.mult).then_inc(rescaled, 1)
                else:
                    dve_link(ins)
                    dve_link(dve.tensor_tensor(scr[:, t, :], scr[:, t, :], row, ALU.mult))
                    dve.tensor_tensor(resid[:, t, :], resid[:, t, :], scr[:, t, :], ALU.add).then_inc(rescaled, 1)
        FS = {f: sems(f"ffn{f}", "first tap conv silu act hi lo resid") for f in range(3)}
        ffn_g, _o = carve(AREA - 6 * SEQ, 2, SEQ)
        ffn_v, _o = carve(_o, 2, SEQ)
        ffn_a, _o = carve(_o, 2, SEQ)
        ACC = [[ps[0][:], ps[1][:]], [ps[2][:], ps[3][:]]]

        def ffn_unit(f, j, i, what):
            b = BASE[f"ffn{f}"]
            if what == "down":
                return unit(b + 3 * j + 4 if j < NF - 1 else b + 3 * NF - 1, i)
            half = 0 if what == "gate" else 1
            return unit(b + half if j == 0 else b + 3 * j - 1 + half, i)

        def ffn_pe(pe, f, conv):
            s = FS[f]
            bank_free, per_tile = (s.conv, 2) if conv else (s.act, 1)

            def up(j, i, reused):
                for half, what in enumerate(("gate", "val")):
                    if reused:
                        pe.wait_ge(bank_free, per_tile * (j - 2) + 2 * per_tile * i + (half + 1 if conv else 1))
                    weights_still(pe, ffn_unit(f, j, i, what), [ps[4 + j % 2 * 2 + half][:, 0:SEQ]], KD, 0)

            def down(j, i, first=False, last=False):
                pe.wait_ge(s.lo, j + 2 * i + 1)
                p = j % 2
                tokens_still(pe, ffn_unit(f, j, i, "down"), ACC, [0], 512, fhi[:, p:p + 1, :],
                             flo[:, p:p + 1, :], first, last)

            pe.wait_ge(TR.lo, TB[f"ffn{f}"].done)
            up(0, 0, False)
            up(1, 0, False)
            down(0, 0, first=True)
            with pe.Fori(0, (NF - 2) // 2) as i:
                for j in (2, 3):
                    up(j, i, True)
                    down(j - 1, i)
            down(NF - 1, 0, last=True)

        def ffn_act(act, f, conv):
            s = FS[f]

            def tile_of(j, i, reused):
                tile, p = j + 2 * i, j % 2
                for half, (what, dst) in enumerate((("gate", ffn_g), ("val", ffn_v))):
                    n = ffn_unit(f, j, i, what)
                    src = ps[4 + p * 2 + half][:, 0:SEQ]
                    if conv or half == 0:
                        act.wait_ge(unit_done, n.u + 1)
                        if reused:
                            act.wait_ge(s.lo, tile - 1)
                    if conv:
                        act.activation(dst[:, p, :], src, ACT.Identity, bias=colv(f"bias{f}", tile + half * NF),
                                       scale=colv(f"conv{f}", 88 + tile + half * NF)).then_inc(s.first, 1)
                    elif half == 0:
                        act.activation(dst[:, p, :], src, ACT.Silu).then_inc(s.silu, 1)
                    refill(act, n)
                if conv:
                    act.wait_ge(s.conv, 2 * tile + 1)
                    act.activation(ffn_g[:, p, :], ffn_g[:, p, :], ACT.Silu).then_inc(s.silu, 1)
                act.wait_ge(s.act, tile + 1)
                if reused:
                    act.wait_ge(unit_done, ffn_unit(f, j - 2, i, "down").u + 1)
                act.activation(fhi[:, p, :], ffn_a[:, p, :], ACT.Copy).then_inc(s.hi, 1)

            tile_of(0, 0, False)
            tile_of(1, 0, False)
            refill(act, ffn_unit(f, 0, 0, "down"))
            trips = (NF - 2) // 2 - (f == 2)
            with act.Fori(0, trips) as i:
                for j in (2, 3):
                    tile_of(j, i, True)
                    refill(act, ffn_unit(f, j - 1, i, "down"))
            if f == 2:
                for j in (2, 3):
                    tile_of(j, trips, True)
                    refill(act, ffn_unit(f, j - 1, trips, "down"))
            refill(act, ffn_unit(f, NF - 1, 0, "down"))

        def ffn_dve(dve, f, conv):
            s = FS[f]

            def tile_of(j, i):
                tile, p = j + 2 * i, j % 2
                if conv:
                    for half, dst in enumerate((ffn_g, ffn_v)):
                        src, y = ps[4 + p * 2 + half], dst[:, p, :]
                        nth = 2 * tile + half + 1
                        dve.wait_ge(s.first, nth)
                        dve.scalar_tensor_tensor(y[:, 1:SEQ], src[:, 0:SEQ - 1],
                                                 colv(f"conv{f}", 44 + tile + half * NF), y[:, 1:SEQ],
                                                 ALU.mult, ALU.add).then_inc(s.tap, 1)
                        dve.wait_ge(s.tap, nth)
                        dve.scalar_tensor_tensor(y[:, 2:SEQ], src[:, 0:SEQ - 2],
                                                 colv(f"conv{f}", tile + half * NF), y[:, 2:SEQ],
                                                 ALU.mult, ALU.add).then_inc(s.conv, 1)
                    dve.wait_ge(s.conv, 2 * tile + 2)
                    dve.wait_ge(s.silu, tile + 1)
                    dve.tensor_tensor(ffn_a[:, p, :], ffn_g[:, p, :], ffn_v[:, p, :],
                                      ALU.mult).then_inc(s.act, 1)
                else:
                    dve.wait_ge(s.silu, tile + 1)
                    dve.wait_ge(unit_done, ffn_unit(f, j, i, "val").u + 1)
                    dve.tensor_tensor(ffn_a[:, p, :], ffn_g[:, p, :], ps[5 + p * 2][:, 0:SEQ],
                                      ALU.mult).then_inc(s.act, 1)
                dve.wait_ge(s.hi, tile + 1)
                dve.tensor_tensor(flo[:, p, :], ffn_a[:, p, :], fhi[:, p, :].bitcast(F32),
                                  ALU.subtract).then_inc(s.lo, 1)

            tile_of(0, 0)
            tile_of(1, 0)
            with dve.Fori(0, (NF - 2) // 2) as i:
                tile_of(2, i)
                tile_of(3, i)

        def add_residual(dve, last_unit, done):
            dve.wait_ge(unit_done, last_unit + 1)
            for t in range(NT):
                for h in range(2):
                    r = resid[:, t, h * 512:h * 512 + 512]
                    dve.tensor_tensor(r, r, ACC[t][h], ALU.add).then_inc(done, 1)

        CV = sems("qkv", "first tap conv silu square turned copied_v copied_k")
        GT = sems("gate", "copied ba exp absx logs g beta cum cum_copied")
        QK, _o = carve(0, 16, SEQ)
        V, _o = carve(_o, NT, VH * HD)
        _groups = _o
        cy, _o = carve(_groups, 2, SEQ)
        csq, _o = carve(_o, P)
        cvt, _o = carve(_o, 2, SEQ)
        cba, _o = carve(_o, SEQ)
        bufs = []
        _o = _groups
        for m in range(2):
            bufs.append([])
            for t in range(NT):
                b_ = Named()
                for name in ("M", "T", "TT", "Pm", "A"):
                    if (m, t, name) == (1, 1, "A"):
                        b_[name] = scr[:, 1, 512:D].rearrange("p (h c) -> p h c", h=4)
                    else:
                        b_[name], _o = carve(_o, 4, P)
                bufs[m].append(b_)
        K1, _o = carve(_o, QKH, P)
        Z = carve(_groups, 2, NT * 512)[0]
        gsc = sb("gsc", [P, 17 * 32])

        def gs(i, heads=16):
            return gsc[:, i * 32:i * 32 + 32].rearrange("p (t h) -> p t h", t=NT)

        BETA, G, GC, EGC, NEGC, DEC, RK, NK, BRK, RK2B, RKDEC, ROQ, SSQ, TMP, TMP2, OSS, ORS = range(17)

        def gates_act(act):
            act.wait_ge(unit_done, BASE["ba"] + 1)
            act.activation(cba[0:32, :], ps[0][0:32, 0:SEQ], ACT.Copy).then_inc(GT.copied, 1)
            refill(act, BASE["ba"])
            act.wait_ge(GT.ba, 1)
            bav = ps[7][:, 0:64].rearrange("p (t c) -> p t c", t=NT)
            act.activation(gs(BETA), bav[:, :, 0:16], ACT.Exp, scale=-1.0).then_inc(GT.exp, 1)
            act.wait_ge(IN.small, 16)
            act_link(act.activation(small[:, 16:32], small[:, 16:32], ACT.Exp))
            act.wait_ge(GT.absx, 1)
            act.wait_ge(IN.tabs, 16)
            act_link(act.activation(gs(TMP2), gs(TMP), ACT.Abs))
            act_link(act.activation(gs(TMP2), gs(TMP2), ACT.Exp, scale=-1.0))
            act.activation(gs(TMP2), gs(TMP2), ACT.Ln, bias=ones[:, 0:1]).then_inc(GT.logs, 1)

        def gates_dve(dve):
            dve.wait_ge(GT.ba, 1)
            dve.wait_ge(GT.exp, 1)
            dve.wait_ge(IN.small, 16)
            bav = ps[7][:, 0:64].rearrange("p (t c) -> p t c", t=NT)
            dve.tensor_tensor(gs(TMP), bav[:, :, 16:32], small[:, 0:16].unsqueeze(1).broadcast_to([P, NT, 16]),
                              ALU.add).then_inc(GT.absx, 1)
            dve_link(dve.tensor_scalar(gs(BETA), gs(BETA), 1.0, None, ALU.add))
            dve.reciprocal(gs(BETA), gs(BETA)).then_inc(GT.beta, 1)
            dve.wait_ge(GT.logs, 1)
            dve_link(dve.scalar_tensor_tensor(gs(G), gs(TMP), 0.0, gs(TMP2), ALU.max, ALU.add))
            dve.scalar_tensor_tensor(gs(G), gs(G), -1.0,
                                     small[:, 16:32].unsqueeze(1).broadcast_to([P, NT, 16]), ALU.mult,
                                     ALU.mult).then_inc(GT.g, 1)

        def qkv_pe(pe):
            pe.wait_ge(TR.lo, TB["a"].done)
            weights_still(pe, unit(BASE["ba"]), [ps[0][:, 0:SEQ]], KD, 0)
            pe.wait_ge(GT.copied, 1)
            for t in range(NT):
                mm = pe.transpose(ps[7][:, t * 32:t * 32 + 32], cba[0:32, t * P:t * P + P], ident[0:32, 0:32])
            mm.then_inc(GT.ba, 1)
            for b in range(32 + 2):
                if b < 32:
                    if b >= 4:
                        pe.wait_ge(CV.conv, b - 3)
                    weights_still(pe, unit(BASE["qkv"] + b), [ps[(b + 1) % 4][:, 0:SEQ]], KD, 0)
                if b == 6:
                    pe.wait_ge(GT.g, 1)
                    pe.wait_ge(IN.tabs, 16)
                    pe.matmul(ps[7][:, 0:32], tri, gsc[:, G * 32:G * 32 + 32], start=True, stop=True)
                    pe.matmul(ps[7][:, 32:64], ones, gsc[:, G * 32:G * 32 + 32], start=True,
                              stop=True).then_inc(GT.cum, 1)
                c = b - 2
                if c >= 0:
                    pe.wait_ge(CV.silu, c + 1)
                    if 2 <= c < 10:
                        pe.wait_ge(CV.copied_k, c - 1)
                    elif c >= 18:
                        pe.wait_ge(CV.copied_v, c - 17)
                    elif c >= 2:
                        pe.wait_ge(CV.square, 2 * c - 2)
                    for t in range(NT):
                        src = QK[:, c, t * P:t * P + P] if c < 16 else cvt[:, c % 2, t * P:t * P + P]
                        mm = pe.transpose(ps[5 + c % 2][:, t * P:t * P + P], src, ident)
                    mm.then_inc(CV.turned, 1)

        def qkv_act(act):
            def finish(b):
                act.wait_ge(CV.conv, b + 1)
                if b < 16:
                    dst = QK[:, b, :]
                else:
                    if b >= 18:
                        act.wait_ge(CV.turned, b - 1)
                    dst = cvt[:, b % 2, :]
                act.activation(dst, cy[:, b % 2, :], ACT.Silu).then_inc(CV.silu, 1)

            def sum_squares(b):
                act.wait_ge(CV.turned, b + 1)
                for t in range(NT):
                    if b or t:
                        act.wait_ge(CV.square, 2 * b + t)
                    c = SSQ * 32 + t * 16 + b
                    act.activation(csq, ps[5 + b % 2][:, t * P:t * P + P], ACT.Square,
                                   accum_out=gsc[:, c:c + 1]).then_inc(CV.square, 1)

            for b in range(32):
                act.wait_ge(unit_done, BASE["qkv"] + b + 1)
                if b >= 2:
                    act.wait_ge(CV.silu, b - 1)
                act.activation(cy[:, b % 2, :], ps[(b + 1) % 4][:, 0:SEQ], ACT.Copy,
                               scale=colv("conv_a", 96 + b)).then_inc(CV.first, 1)
                if b >= 1:
                    finish(b - 1)
                refill(act, BASE["qkv"] + b)
                if 3 <= b < 19:
                    sum_squares(b - 3)
            finish(31)

        def qkv_dve(dve):
            def copy_v(b):
                dve.wait_ge(CV.turned, b + 1)
                dve.tensor_copy(V[:, :, (b - 16) * P:(b - 15) * P],
                                ps[5 + b % 2][:, 0:SEQ].rearrange("p (t c) -> p t c", t=NT)).then_inc(CV.copied_v, 1)

            for b in range(32):
                src, y = ps[(b + 1) % 4], cy[:, b % 2, :]
                dve.wait_ge(CV.first, b + 1)
                for tap in (1, 2, 3):
                    ins = dve.scalar_tensor_tensor(y[:, tap:SEQ], src[:, 0:SEQ - tap],
                                                   colv("conv_a", (3 - tap) * 32 + b), y[:, tap:SEQ],
                                                   ALU.mult, ALU.add)
                    if tap < 3:
                        dve_link(ins)
                ins.then_inc(CV.conv, 1)
                if b == 9:
                    dve.wait_ge(GT.cum, 1)
                    dve_link(dve.tensor_copy(gsc[:, GC * 32:GC * 32 + 32], ps[7][:, 0:32]))
                    dve.tensor_tensor(gsc[:, DEC * 32:DEC * 32 + 32], ps[7][:, 32:64],
                                      gsc[:, GC * 32:GC * 32 + 32], ALU.subtract).then_inc(GT.cum_copied, 1)
                if 4 <= b < 12:
                    h = b - 4
                    dve.wait_ge(CV.square, 2 * h + 2)
                    dve.tensor_copy(K1[:, h, :], ps[5 + h % 2][:, 0:P]).then_inc(CV.copied_k, 1)
                if b >= 19:
                    copy_v(b - 3)
            for b in (29, 30, 31):
                copy_v(b)
        DN = sems("delta", "setup diff decay mat init prod masked tpm updated flipped tt r1 vn1p vn1 o1p s1p s1 kqs r2 "
                  "vn2p vn2 o2p o squares normed cleared gated z_silu turned hi lo resid exps")
        XB_, YB_ = ((ps[0], ps[2]), (ps[4], ps[6])), ((ps[1], ps[3]), (ps[5], ps[7]))
        BOTH = [(m, t) for m in range(2) for t in range(NT)]

        def by_head(i, t, g):
            c = i * 32 + t * 16 + 4 * g
            return gsc[:, c:c + 4].unsqueeze(2).broadcast_to([P, 4, P])

        def scalar(i, t, h):
            c = i * 32 + t * 16 + h
            return gsc[:, c:c + 1]

        def heads(bank, n=P):
            return bank[:, 0:4 * n].rearrange("p (h c) -> p h c", h=4)

        def blocks(flat, s, half):
            return flat.rearrange("p (n two s) -> p n two s", two=2, s=s)[:, :, half, :]

        def flat(buf):
            return buf.rearrange("p h c -> p (h c)")

        def group_cols(x, t, g):
            return x[:, t, g * 512:g * 512 + 512].rearrange("p (h c) -> p h c", h=4)

        def slot_of(k):
            return (k + 8) % 16

        def delta_pe(pe):
            pe.wait_ge(CV.copied_v, 16)
            def flip(p, lv, i):
                m, t = BOTH[i]
                for h in range(4):
                    mm = pe.transpose(YB_[m][t][:, h * P:h * P + P], bufs[m][t].T[:, h, :], ident)
                mm.then_inc(DN.flipped, 1)

            for p in range(2):
                if p:
                    pe.wait_ge(DN.o, 4 * p)
                for m, t in BOTH:
                    g, tok = 2 * p + m, slice(t * P, t * P + P)
                    for kq in range(2):
                        k, q = QK[:, 2 * g + kq, tok], QK[:, 8 + 2 * g + kq, tok]
                        pe.matmul(XB_[m][t][:, kq * 256:kq * 256 + P], k, k, start=True, stop=True)
                        pe.matmul(XB_[m][t][:, kq * 256 + P:kq * 256 + 256], k, q, start=True, stop=True)
                    for h in range(4):
                        mm = pe.matmul(YB_[m][t][:, h * P:h * P + P],
                                       scalar(G, t, 4 * g + h).broadcast_to([P, P]), tri, start=True, stop=True)
                    mm.then_inc(DN.setup, 1)
                for lv in range(LEVELS):
                    for i, (m, t) in enumerate(BOTH):
                        b = bufs[m][t]
                        if lv == 0:
                            pe.wait_ge(DN.init, 4 * p + i + 1)
                        else:
                            pe.wait_ge(DN.updated, (p * LEVELS + lv - 1) * 4 + i + 1)
                        for h in range(4):
                            mm = pe.matmul(XB_[m][t][:, h * P:h * P + P], b.M[:, h, :], b.T[:, h, :],
                                           start=True, stop=True)
                        mm.then_inc(DN.prod, 1)
                        if lv:
                            flip(p, lv - 1, i)
                    if lv == 0:
                        continue
                    for i, (m, t) in enumerate(BOTH):
                        b = bufs[m][t]
                        pe.wait_ge(DN.masked, (p * LEVELS + lv) * 4 + i + 1)
                        pe.wait_ge(DN.tt, (p * LEVELS + lv - 1) * 4 + i + 1)
                        for h in range(4):
                            mm = pe.matmul(XB_[m][t][:, h * P:h * P + P], b.TT[:, h, :], b.Pm[:, h, :],
                                           start=True, stop=True)
                        mm.then_inc(DN.tpm, 1)
                for i in range(4):
                    pe.wait_ge(DN.updated, (p * LEVELS + LEVELS - 1) * 4 + i + 1)
                    flip(p, LEVELS - 1, i)
                pe.wait_ge(DN.tt, 4 * LEVELS * (p + 1))
                for m, (b0, b1) in enumerate(bufs):
                    pe.wait_ge(DN.r1, 2 * p + m + 1)
                    for h in range(4):
                        mm = pe.matmul(XB_[m][0][:, h * P:h * P + P], b0.TT[:, h, :], b0.M[:, h, :],
                                       start=True, stop=True)
                    mm.then_inc(DN.vn1p, 1)
                for m, (b0, b1) in enumerate(bufs):
                    g = 2 * p + m
                    pe.wait_ge(DN.vn1, g + 1)
                    for kq in range(2):
                        mm = pe.matmul(YB_[m][0][:, kq * 256:kq * 256 + 256], K1[:, 2 * g + kq, :],
                                       b0.T[:, 2 * kq:2 * kq + 2, :], start=True, stop=True)
                    mm.then_inc(DN.s1p, 1)
                    for h in range(4):
                        mm = pe.matmul(XB_[m][0][:, h * P:h * P + P], b0.A[:, h, :], b0.Pm[:, h, :],
                                       start=True, stop=True)
                    mm.then_inc(DN.o1p, 1)
                for m, (b0, b1) in enumerate(bufs):
                    g = 2 * p + m
                    pe.wait_ge(DN.s1, g + 1)
                    for bank, which in ((XB_[m][1], 0), (YB_[m][1], 8)):
                        for kq in range(2):
                            mm = pe.matmul(bank[:, kq * 256:kq * 256 + 256], QK[:, which + 2 * g + kq, P:SEQ],
                                           b1.T[:, 2 * kq:2 * kq + 2, :], start=True, stop=True)
                    mm.then_inc(DN.kqs, 1)
                for m, (b0, b1) in enumerate(bufs):
                    pe.wait_ge(DN.r2, 2 * p + m + 1)
                    for h in range(4):
                        mm = pe.matmul(YB_[m][0][:, h * P:h * P + P], b1.TT[:, h, :], b1.M[:, h, :],
                                       start=True, stop=True)
                    mm.then_inc(DN.vn2p, 1)
                for m, (b0, b1) in enumerate(bufs):
                    pe.wait_ge(DN.vn2, 2 * p + m + 1)
                    for h in range(4):
                        mm = pe.matmul(XB_[m][1][:, h * P:h * P + P], b1.A[:, h, :], b0.T[:, h, :],
                                       start=True, stop=True)
                    mm.then_inc(DN.o2p, 1)

            def z_units(c):
                if c >= 2:
                    pe.wait_ge(DN.z_silu, 2 * c - 2)
                banks = [[ps[c % 2 * 2 + t][:]] for t in range(NT)]
                for k in range(4):
                    tokens_still(pe, unit(BASE["z"] + 4 * c + k), banks, [2 * k, 2 * k + 1], 512, xhi, xlo,
                                 k == 0, k == 3)

            def turn(pair):
                pe.wait_ge(DN.gated, (pair // 2 + 1) * 2)
                if pair >= 4:
                    pe.wait_ge(DN.lo, pair - 3)
                for k in (2 * pair, 2 * pair + 1):
                    for t in range(NT):
                        c = k % 2 * SEQ + t * P
                        mm = pe.transpose(ps[4 + pair % 4][:, c:c + P], V[:, t, k * P:k * P + P], ident)
                mm.then_inc(DN.turned, 1)

            z_units(0)
            pe.wait_ge(DN.o, 8)
            z_units(1)
            turn(0)
            turn(1)
            z_units(2)
            turn(2)
            turn(3)
            z_units(3)
            turn(4)
            turn(5)
            for pair in range(8):
                if pair == 0:
                    pe.wait_ge(DN.z_silu, 8)
                pe.wait_ge(DN.lo, pair + 1)
                for k in (2 * pair, 2 * pair + 1):
                    tokens_still(pe, unit(BASE["wout"] + k), ACC, [slot_of(k)], 512, xhi, xlo, k == 0, k == 15)
                if pair < 2:
                    turn(pair + 6)

        def delta_act(act):
            act.wait_ge(GT.cum_copied, 1)
            act.activation(gsc[:, EGC * 32:EGC * 32 + 32], gsc[:, GC * 32:GC * 32 + 32], ACT.Exp).then_inc(DN.exps, 1)
            act.activation(gsc[:, DEC * 32:DEC * 32 + 32], gsc[:, DEC * 32:DEC * 32 + 32], ACT.Exp).then_inc(DN.exps, 1)
            for p in range(2):
                for i, (m, t) in enumerate(BOTH):
                    act.wait_ge(DN.diff, 4 * p + i + 1)
                    act.activation(flat(bufs[m][t].T), flat(bufs[m][t].T), ACT.Exp).then_inc(DN.decay, 1)
                for i, (m, t) in enumerate(BOTH):
                    act.wait_ge(DN.mat, 4 * p + i + 1)
                    act.activation(bufs[m][t].T, ident.unsqueeze(1).broadcast_to([P, 4, P]), ACT.Copy).then_inc(DN.init, 1)
                for n in range(4 * LEVELS):
                    m, t = BOTH[n % 4]
                    act.wait_ge(DN.flipped, 4 * LEVELS * p + n + 1)
                    act.activation(flat(bufs[m][t].TT), YB_[m][t][:], ACT.Copy).then_inc(DN.tt, 1)
                for m in range(2):
                    act.wait_ge(DN.s1p, 2 * p + m + 1)
                    act.activation(flat(bufs[m][1].T), YB_[m][0][:], ACT.Copy).then_inc(DN.s1, 1)
                for i, (t, m) in enumerate(((0, 0), (0, 1), (1, 0), (1, 1))):
                    act.wait_ge(DN.o, 4 * p + i + 1)
                    for h in range(4):
                        hh = 8 * p + 4 * m + h
                        act.activation(scr[:, 0, h * P:h * P + P], V[:, t, hh * P:hh * P + P], ACT.Square,
                                       accum_out=scalar(OSS, t, hh)).then_inc(DN.squares, 1)
                    act.wait_ge(DN.squares, 16 * p + 4 * i + 4)
            def refill_pair(pair):
                for k in (2 * pair, 2 * pair + 1):
                    refill(act, BASE["wout"] + k)

            def split(pair):
                if pair == 4:
                    act.wait_ge(unit_done, BASE["wout"])
                act.wait_ge(DN.turned, pair + 1)
                s = slot_of(2 * pair)
                act.activation(xhi[:, s:s + 2, :].rearrange("p a b -> p (a b)"),
                               ps[4 + pair % 4][:], ACT.Copy, scale=colv("out_norm")).then_inc(DN.hi, 1)

            for c in range(4):
                for k in range(4):
                    refill(act, BASE["z"] + 4 * c + k)
                for t in range(NT):
                    if c >= 2:
                        act.wait_ge(DN.gated, 2 * c - 3 + t)
                    act.activation(Z[:, c % 2, t * 512:t * 512 + 512], ps[c % 2 * 2 + t][:], ACT.Silu).then_inc(DN.z_silu, 1)
                if c in (1, 2):
                    split(2 * c - 2)
                    split(2 * c - 1)
            split(4)
            split(5)
            refill_pair(0)
            split(6)
            refill_pair(1)
            split(7)
            for pair in range(2, 8):
                refill_pair(pair)

        def delta_dve(dve):
            dve.wait_ge(IN.tabs, 16)
            for m, t in BOTH:
                dve.memset(bufs[m][t].Pm, 0.0).then_inc(DN.cleared, 1)
            w, rk, nk = (gsc[:, i * 32:i * 32 + 32] for i in (SSQ, RK, NK))
            dve.wait_ge(CV.square, 32)
            inverse_root(dve, rk, w, EPS, root_tmp[:])
            dve_link(dve.tensor_tensor(nk, w, rk, ALU.mult))
            dve.wait_ge(DN.exps, 2)

            def pairs(i):
                return gs(i).rearrange("p t (h r) -> p t h r", r=2)

            def shared(i, q=0):
                return gs(i)[:, :, 8 * q:8 * q + 8].unsqueeze(3).broadcast_to([P, NT, 8, 2])

            dve_link(dve.tensor_tensor(pairs(BRK), pairs(BETA), shared(RK), ALU.mult))
            dve_link(dve.tensor_tensor(pairs(RK2B), pairs(BRK), shared(RK), ALU.mult))
            dve_link(dve.tensor_tensor(pairs(RKDEC), pairs(DEC), shared(RK), ALU.mult))
            dve_link(dve.tensor_scalar(gs(NEGC), gs(EGC), -1.0, None, ALU.mult))
            dve_link(dve.tensor_copy(pairs(TMP), shared(NK)))
            dve_link(dve.tensor_copy(pairs(ROQ), shared(RK, 1)))
            dve_link(dve.tensor_scalar(gs(ROQ), gs(ROQ), float(HD) ** -0.5, None, ALU.mult))

            for p in range(2):
                for i, (m, t) in enumerate(BOTH):
                    g, b = 2 * p + m, bufs[m][t]
                    dve.wait_ge(DN.setup, 4 * p + i + 1)
                    if p:
                        dve.wait_ge(DN.o, 4)
                    for h in range(4):
                        ins = dve.scalar_tensor_tensor(b.T[:, h, :], YB_[m][t][:, h * P:h * P + P],
                                                       scalar(GC, t, 4 * g + h), tabv("future"),
                                                       ALU.subtract, ALU.min)
                    ins.then_inc(DN.diff, 1)
                for i, (m, t) in enumerate(BOTH):
                    g, b = 2 * p + m, bufs[m][t]
                    dve.wait_ge(DN.decay, 4 * p + i + 1)
                    for h in range(4):
                        hh, c = 4 * g + h, h // 2 * 256
                        dve.scalar_tensor_tensor(b.M[:, h, :], XB_[m][t][:, c:c + P], scalar(RK2B, t, hh),
                                                 b.T[:, h, :], ALU.mult, ALU.mult)
                        ins = dve.scalar_tensor_tensor(b.A[:, h, :], XB_[m][t][:, c + P:c + 256],
                                                       scalar(RK, t, hh // 2), b.T[:, h, :], ALU.mult, ALU.mult)
                    ins.then_inc(DN.mat, 1)
                for lv in range(LEVELS):
                    s = 1 << lv
                    for i, (m, t) in enumerate(BOTH):
                        b = bufs[m][t]
                        dve.wait_ge(DN.prod, (p * LEVELS + lv) * 4 + i + 1)
                        mask = tabv("levels")[:, lv * 64:lv * 64 + 64].rearrange("p (n s) -> p n s", s=s)
                        dst = b.Pm.rearrange("p h (n two s) -> p h n two s", two=2, s=s)[:, :, :, 0, :]
                        src = XB_[m][t][:].rearrange("p (h n two s) -> p h n two s", h=4, two=2, s=s)[:, :, :, 0, :]
                        dve.tensor_tensor(dst, src, mask.unsqueeze(1).broadcast_to([P, 4, 64 // s, s]),
                                          ALU.mult).then_inc(DN.masked, 1)
                    for i, (m, t) in enumerate(BOTH):
                        b = bufs[m][t]
                        if lv:
                            product = XB_[m][t][:]
                            dve.wait_ge(DN.tpm, (p * (LEVELS - 1) + lv - 1) * 4 + i + 1)
                        else:
                            product = flat(b.Pm)
                            dve.wait_ge(DN.masked, p * LEVELS * 4 + i + 1)
                        left = blocks(flat(b.T), s, 0)
                        dve.tensor_tensor(left, left, blocks(product, s, 0), ALU.subtract).then_inc(DN.updated, 1)
                for m, (b0, b1) in enumerate(bufs):
                    g = 2 * p + m
                    dve.tensor_tensor(b0.M, group_cols(V, 0, g), by_head(TMP, 0, g), ALU.mult).then_inc(DN.r1, 1)
                    dve_link(dve.tensor_tensor(b1.M, group_cols(V, 1, g), by_head(TMP, 1, g), ALU.mult))
                for m, (b0, b1) in enumerate(bufs):
                    g = 2 * p + m
                    dve.wait_ge(DN.vn1p, g + 1)
                    dve_link(dve.tensor_tensor(b0.Pm, heads(XB_[m][0]), by_head(BRK, 0, g), ALU.mult))
                    dve.tensor_tensor(b0.T, b0.Pm, by_head(RKDEC, 0, g), ALU.mult).then_inc(DN.vn1, 1)
                for m, (b0, b1) in enumerate(bufs):
                    g = 2 * p + m
                    dve.wait_ge(DN.kqs, g + 1)
                    dve_link(dve.tensor_tensor(b1.Pm, heads(XB_[m][1]), by_head(NEGC, 1, g), ALU.mult))
                    dve.tensor_tensor(b1.M, b1.M, b1.Pm, ALU.add).then_inc(DN.r2, 1)
                    dve.wait_ge(DN.r2, g + 1)
                    dve_link(dve.tensor_tensor(b1.Pm, heads(YB_[m][1]), by_head(EGC, 1, g), ALU.mult))
                for m in range(2):
                    g = 2 * p + m
                    dve.wait_ge(DN.o1p, g + 1)
                    dve.tensor_tensor(group_cols(V, 0, g), heads(XB_[m][0]), by_head(ROQ, 0, g),
                                      ALU.mult).then_inc(DN.o, 1)
                for m, (b0, b1) in enumerate(bufs):
                    g = 2 * p + m
                    dve.wait_ge(DN.vn2p, g + 1)
                    dve.tensor_tensor(b0.T, heads(YB_[m][0]), by_head(BRK, 1, g), ALU.mult).then_inc(DN.vn2, 1)
                for m, (b0, b1) in enumerate(bufs):
                    g = 2 * p + m
                    dve.wait_ge(DN.o2p, g + 1)
                    dve_link(dve.tensor_tensor(b1.Pm, heads(XB_[m][1]), b1.Pm, ALU.add))
                    dve.tensor_tensor(group_cols(V, 1, g), b1.Pm, by_head(ROQ, 1, g), ALU.mult).then_inc(DN.o, 1)

            dve.wait_ge(DN.squares, 32)
            inverse_root(dve, gsc[:, ORS * 32:ORS * 32 + 32], gsc[:, OSS * 32:OSS * 32 + 32], HD * EPS, root_tmp[:])
            for c in range(4):
                for t in range(NT):
                    v = group_cols(V, t, c)
                    dve.tensor_tensor(v, v, by_head(ORS, t, c), ALU.mult).then_inc(DN.normed, 1)
            def split(pair):
                dve.wait_ge(DN.hi, pair + 1)
                s = slot_of(2 * pair)
                dve.scalar_tensor_tensor(xlo[:, s:s + 2, :].rearrange("p a b -> p (a b)"),
                                         ps[4 + pair % 4][:], colv("out_norm"),
                                         xhi[:, s:s + 2, :].rearrange("p a b -> p (a b)").bitcast(F32),
                                         ALU.mult, ALU.subtract).then_inc(DN.lo, 1)

            for c in range(4):
                for t in range(NT):
                    dve.wait_ge(DN.z_silu, 2 * c + t + 1)
                    dve.wait_ge(DN.normed, 2 * c + t + 1)
                    v = group_cols(V, t, c)
                    dve.tensor_tensor(v, v, Z[:, c % 2, t * 512:t * 512 + 512].rearrange("p (h c) -> p h c", h=4),
                                      ALU.mult).then_inc(DN.gated, 1)
                if c in (1, 2):
                    split(2 * c - 2)
                    split(2 * c - 1)
            for pair in range(4, 8):
                split(pair)
            add_residual(dve, BASE["wout"] + 15, DN.resid)
        AT = sems("attn", "scores maxed exps turned copied outs sunk total inverse")
        bias_, _o = carve(0, AH, SEQ)
        QT, _o = carve(_o, 8, SEQ)
        KT, _o = carve(_o, 2, SEQ)
        VN = carve(_o, NT, 4 * P)[0].rearrange("p t (g c) -> p t g c", g=4)
        _o += NT * 4 * P
        swa = Named(heads=AH, width=AHD, share=2, base=0, AO=carve(8192, NT, D)[0])
        swa["S"], _o = carve(12288, 3, 384)
        swa["PT"], _o = carve(_o, 2, 384)
        row_b_a2, _o = carve(15872, 512)
        row_final, _o = carve(_o, D)
        PARTS = (slice(0, P), slice(P, 384))
        att_stat = sb("att_stat", [P, 4 * 32])

        def att(i, n):
            return att_stat[:, i * 32:i * 32 + 2 * n].rearrange("p (h t) -> p h t", t=NT)

        def attention_pe(pe, a, scores, v):
            n, b = a.heads, a.base
            for j in range(n + 2):
                if j < n:
                    if j >= 2:
                        pe.wait_ge(AT.maxed, b + j - 1)
                    scores(j, ps[4 + j % 2]).then_inc(AT.scores, 1)
                h = j - 1
                if 0 <= h < n:
                    pe.wait_ge(AT.exps, b + h + 1)
                    if h >= 2:
                        pe.wait_ge(AT.copied, b + h - 1)
                    for c in range(3):
                        mm = pe.transpose(ps[6 + h % 2][:, c * P:c * P + P], a.S[:, h % 3, c * P:c * P + P], ident)
                    mm.then_inc(AT.turned, 1)
                h = j - 2
                if h >= 0:
                    pe.wait_ge(AT.copied, b + h + 1)
                    pt, c = a.PT[:, h % 2, :], h // a.share * P
                    o = [ACC[t][c // 512][:, c % 512:c % 512 + P] for t in range(NT)]
                    first, last = h % a.share == 0, h % a.share == a.share - 1
                    pe.matmul(o[0], pt[:, 0:P], v(h, 0), start=first, stop=last)
                    pe.matmul(o[1], pt[:, P:SEQ], v(h, 0), start=first, stop=False)
                    pe.matmul(o[1], pt[:, SEQ:384], v(h, 1), start=False, stop=last).then_inc(AT.outs, 1)

        def attention_act(act, a):
            n, b = a.heads, a.base
            for j in range(n + 1):
                if j < n:
                    act.wait_ge(AT.maxed, b + j + 1)
                    for t in range(NT):
                        ins = act.activation(a.S[:, j % 3, PARTS[t]], a.S[:, j % 3, PARTS[t]], ACT.Exp,
                                             bias=att(0, n)[:, j, t:t + 1], accum_out=att(1, n)[:, j, t:t + 1])
                    ins.then_inc(AT.exps, 1)
                h = j - 1
                if h >= 0:
                    act.wait_ge(AT.turned, b + h + 1)
                    if h >= 2:
                        act.wait_ge(AT.outs, b + h - 1)
                    act.activation(a.PT[:, h % 2, :], ps[6 + h % 2][:, 0:384], ACT.Copy).then_inc(AT.copied, 1)

        def attention_dve(dve, a, bias, least):
            n, b = a.heads, a.base
            for j in range(n):
                dve.wait_ge(AT.scores, b + j + 1)
                if j >= 3:
                    dve.wait_ge(AT.turned, b + j - 2)
                for t in range(NT):
                    ins = dve.tensor_tensor_reduce(a.S[:, j % 3, PARTS[t]], ps[4 + j % 2][:, PARTS[t]], bias(j, t),
                                                   1.0, least(j), ALU.add, ALU.max,
                                                   accum_out=att(2, n)[:, j, t:t + 1])
                dve_link(ins)
                dve.tensor_scalar(att(0, n)[:, j, :], att(2, n)[:, j, :], -1.0, None, ALU.mult).then_inc(AT.maxed, 1)

        def attention_finish(dve, a, extra):
            n, b = a.heads, a.base
            dve.wait_ge(AT.exps, b + n)
            extra()
            dve_link(dve.reciprocal(att(3, n), att(1, n)))
            dve.wait_ge(AT.outs, b + n)
            for t in range(NT):
                for half in range(2):
                    hs = n // 2
                    ins = dve.tensor_tensor(
                        a.AO[:, t, half * 512:half * 512 + 512].rearrange("p (h c) -> p h c", h=hs),
                        ACC[t][half].rearrange("p (h c) -> p h c", h=hs),
                        att(3, n)[:, half * hs:half * hs + hs, t:t + 1].broadcast_to([P, hs, a.width]), ALU.mult)
                ins.then_inc(TR.ready, 1)

        SW = sems("swa", "bias row_final row_b cleared copied resid")

        def swa_load(act):
            act.wait_ge(IN.band_out, 16)
            skewed = bass.AP(tensor=band_scratch.tensor, offset=band_scratch.offset + P - 1,
                             ap=[[BANDX, P], [P * 384, AH], [1, SEQ]])
            act.dma_start(bias_, skewed).then_inc(SW.bias, 16)
            act.dma_start(row_final, rows["final"].broadcast_to([P, D])).then_inc(SW.row_final, 16)
            act.dma_start(row_b_a2, rows["b_a2"].broadcast_to([P, 512])).then_inc(SW.row_b, 16)

        def swa_pe(pe):
            pe.wait_ge(TR.lo, TB["b"].done)
            for b in range(2):
                weights_still(pe, unit(BASE["kv"] + b), [ps[b][:, 0:SEQ]], KD, 0)
            for k in range(2):
                tokens_still(pe, unit(BASE["kv"] + 2 + k), [[ps[4][:, 0:SEQ]], [ps[5][:, 0:SEQ]]],
                             [4 * k + i for i in range(4)], SEQ, xhi, xlo, k == 0, k == 1)
            for b in range(8):
                if b >= 2:
                    pe.wait_ge(SW.copied, b + 1 if b >= 4 else b - 1)
                weights_still(pe, unit(BASE["wq"] + b), [ps[(2 + b) % 4][:, 0:SEQ]], KD, 8)

            def scores(j, bank):
                half = slice(j % 2 * AHD, j % 2 * AHD + AHD)
                q, k = QT[half, j // 2, :], KT[half, j // 8, :]
                pe.matmul(bank[:, 0:P], q[:, 0:P], k[:, 0:P], start=True, stop=True)
                return pe.matmul(bank[:, P:384], q[:, P:SEQ], k, start=True, stop=True)

            def v(j, t):
                return VN[:, t, j // 8 * 2 + j % 2, :]

            pe.wait_ge(SW.copied, 12)
            attention_pe(pe, swa, scores, v)
            turn_pe(pe, "attn", swa.AO)
            for k in range(KD):
                pe.wait_ge(TR.lo, TB["attn"].split + k + 1)
                tokens_still(pe, unit(BASE["wo"] + k), ACC, [k], 512, xhi, xlo, k == 0, k == KD - 1)

        def swa_act(act):
            def copy(last, dst, bank, scale=1.0):
                act.wait_ge(unit_done, last + 1)
                act.activation(dst, ps[bank][:, 0:SEQ], ACT.Copy, scale=scale).then_inc(SW.copied, 1)

            for b in range(2):
                copy(BASE["kv"] + b, KT[:, b, :], b)
                refill(act, BASE["kv"] + b)
            refill(act, BASE["kv"] + 2)
            for t in range(NT):
                act.wait_ge(unit_done, BASE["kv"] + 4)
                act.wait_ge(SW.cleared, 1)
                for half in range(2):
                    ins = act.activation(
                        VN[:, t].rearrange("p (g two) c -> p g two c", two=2)[:, :, half, half * AHD:half * AHD + AHD],
                        ps[4 + t][:, 0:SEQ].rearrange("p (g two c) -> p g two c", g=2, two=2)[:, :, half, :], ACT.Copy)
                ins.then_inc(SW.copied, 1)
            refill(act, BASE["kv"] + 3)
            for b in range(8):
                copy(BASE["wq"] + b, QT[:, b, :], (2 + b) % 4, AHD ** -0.5)
                refill(act, BASE["wq"] + b)
            attention_act(act, swa)
            act.wait_ge(AT.sunk, 1)
            act.activation(att(2, AH), att(2, AH), ACT.Exp).then_inc(AT.total, 1)
            turn_act(act, "attn")
            for k in range(KD):
                refill(act, BASE["wo"] + k)

        def swa_clear(dve):
            dve.memset(VN, 0.0).then_inc(SW.cleared, 1)

        def swa_dve(dve):
            sinks = small[:, 32:48]
            dve.wait_ge(SW.bias, 16)
            attention_dve(dve, swa, lambda j, t: bias_[:, j, (P, 0)[t]:SEQ], lambda j: sinks[:, j:j + 1])

            def sink_terms():
                dve.tensor_tensor(att(2, AH), att(0, AH), sinks.unsqueeze(2).broadcast_to([P, AH, NT]),
                                  ALU.add).then_inc(AT.sunk, 1)
                dve.wait_ge(AT.total, 1)
                dve_link(dve.tensor_tensor(att(1, AH), att(1, AH), att(2, AH), ALU.add))

            attention_finish(dve, swa, sink_terms)
            turn_dve(dve, "attn")
            add_residual(dve, BASE["wo"] + KD - 1, SW.resid)
        MX = sems("mix", "w_a2 row_gate row_post row_ffn copied la_made la_x la_ln la suffix decays kdec "
                  "c_squares c_ready c_turned c_hi c_lo gates_in sigmoid kv state o o_squares up_copied "
                  "rope_made roped ya_used w2_copied")
        GV, _o = carve(0, NT, D)
        GK, _o = carve(_o, NT, 512)
        GQT, _o = carve(_o, GH, SEQ)
        LA, _s1 = carve(_o, NT, 512)
        ST, _o = carve(_o, 2, GH * GDV)
        GG, _o = carve(_o, NT, D)
        GA, _o = carve(_o, NT, D)
        GB, _o = carve(_o, NT, D)
        OG, _t = carve(_o, NT, D)
        LT, _t = carve(_o, NT, 512)
        LX, _t = carve(_t, NT, 512)
        CQ, _o = carve(_t, NT, QL)
        CKV, _o = carve(_o, NT, KVL)
        XB, _o = carve(_o, SEQ)
        QN, _t = carve(0, MH, SEQ)
        KN, _t = carve(_t, MH, SEQ)
        VM, _t = carve(_t, NT, D)
        row_post, _t = carve(14336, D)
        row_ffn, _t = carve(_t, D)
        QP, _t = carve(16384, 4, SEQ)
        W_A2, _t = carve(17408, 512)
        KP, _t = carve(17920, SEQ)
        MIXED = carve(0, NT, D)[0]
        mla = Named(heads=MH, width=P, share=1, base=AH, S=swa.S, PT=swa.PT, AO=carve(6144, NT, D)[0])
        DC = att_stat[:, 0:16]
        OSQ, CSQ = att_stat[:, 32:48], att_stat[:, 64:72]
        CHUNKS = ("gk0", "gv0", "gv1", "gg0", "gg1", "gates0", "gates1", "gates2", "gates3")

        def block2_pe(pe):
            turn_pe(pe, "mix", scr)
            pe.wait_ge(TR.lo, TB["mix"].done)
            for k in range(4):
                tokens_still(pe, unit(BASE["cq"] + k), [[ps[t][:, 0:QL]] for t in range(NT)], [2 * k, 2 * k + 1],
                             QL, xhi, xlo, k == 0, k == 3)
            for k in range(2):
                tokens_still(pe, unit(BASE["ckv"] + k), [[ps[2 + t][:, 0:KVL]] for t in range(NT)],
                             [4 * k + i for i in range(4)], KVL, xhi, xlo, k == 0, k == 1)
            weights_still(pe, unit(BASE["x"]), [ps[4][:, 0:SEQ]], KD, 0)
            for h in range(GH):
                if h == 3:
                    pe.wait_ge(MX.copied, 5)
                weights_still(pe, unit(BASE["gq"] + h), [ps[(5, 6, 7, 4)[h]][:, 0:SEQ]], KD, 0)
            pe.wait_ge(MX.w_a2, 16)
            pe.wait_ge(MX.copied, 7)
            for t in range(NT):
                mm = pe.matmul(ps[5 + t][:], XB[0:16, t * P:t * P + P], W_A2[0:16, :], start=True, stop=True)
            mm.then_inc(MX.la_made, 1)
            for c, name in enumerate(CHUNKS):
                pair = c % 2 * 2
                if c <= 6:
                    pe.wait_ge(MX.copied, (2, 4, 11, 13, 15, 17, 19)[c])
                else:
                    pe.wait_ge(MX.gates_in, 2 * (c - 6))
                for k in range(4):
                    tokens_still(pe, unit(BASE[name[:-1]] + int(name[-1]) * 4 + k), [[ps[pair][:]], [ps[pair + 1][:]]],
                                 [2 * k, 2 * k + 1], 512, xhi, xlo, k == 0, k == 3)
                if c == 0:
                    pe.wait_ge(MX.la, 1)
                    pe.wait_ge(MX.copied, 8)
                    for t in range(NT):
                        pe.matmul(ps[5 + t][:], tabv("later"), LA[:, t, :], start=True, stop=True)
                        for h in range(GH):
                            i = (t * GH + h) * 2
                            mm = pe.matmul(ps[7][:, i:i + 2], LA[:, t, h * P:h * P + P],
                                           col[:, COL["chunk_of"]:COL["chunk_of"] + 2], start=True, stop=True)
                    mm.then_inc(MX.suffix, 1)
                if c == 3:
                    pe.wait_ge(MX.c_ready, 1)
                    pe.wait_ge(MX.decays, 2)
                    pe.wait_ge(MX.copied, 9)
                    for bank, src, ks in ((4, CQ, (0, 1)), (5, CQ, (2,)), (6, CKV, (0, 1))):
                        for i, k in enumerate(ks):
                            for t in range(NT):
                                mm = pe.transpose(ps[bank][:, i * SEQ + t * P:i * SEQ + t * P + P],
                                                  src[:, t, k * P:k * P + P], ident)
                        mm.then_inc(MX.c_turned, 1)

            pe.wait_ge(MX.c_lo, 5)
            pe.wait_ge(MX.kdec, 1)
            pe.wait_ge(MX.gates_in, 8)
            for c in range(2 * NT + 1):
                if c < 2 * NT:
                    t, half = c // 2, slice(c % 2 * 64, c % 2 * 64 + 64)
                    if c >= 2:
                        pe.wait_ge(MX.state, c - 1)
                    for h in range(GH):
                        mm = pe.matmul(ps[4 + c % 2 * 2 + h // 2][:, h % 2 * GDV:h % 2 * GDV + GDV],
                                       GK[half, t, h * P:h * P + P], GV[half, t, h * GDV:h * GDV + GDV],
                                       start=True, stop=True)
                    mm.then_inc(MX.kv, 1)
                c -= 1
                if c >= 0:
                    t, half = c // 2, slice(c % 2 * 64, c % 2 * 64 + 64)
                    pe.wait_ge(MX.state, c + 1)
                    for h in range(GH):
                        mm = pe.matmul(ACC[t][h // 2][half, h % 2 * GDV:h % 2 * GDV + GDV],
                                       GQT[:, h, c * 64:c * 64 + 64], ST[:, c % 2, h * GDV:h * GDV + GDV],
                                       start=True, stop=True)
                    mm.then_inc(MX.o, 1)

            for i in range(6):
                if i >= 4:
                    pe.wait_ge(MX.up_copied, i - 3)
                b = ps[4 + i % 4]
                weights_still(pe, unit(BASE["uq"] + i), [b[:, 0:SEQ], b[:, SEQ:512]], 3, 8)
            for i in range(2):
                pe.wait_ge(MX.up_copied, 4 + 2 * i)
                banks = (ps[6], ps[7]) if i == 0 else (ps[4], ps[5])
                weights_still(pe, unit(BASE["kn"] + i), [b[:, c:c + SEQ] for b in banks for c in (0, SEQ)], 2, 11)
            pe.wait_ge(TR.ready, TB["gla"].ready + 2)
            for i in range(2):
                tokens_still(pe, unit(BASE["vm"] + i), ACC, [11 + i], 512, xhi, xlo, i == 0, i == 1)
            pe.wait_ge(MX.up_copied, 10)
            for i in range(2):
                pe.matmul(ps[4 + i][:], tabv("swap"), QP[:, 2 * i:2 * i + 2, :], start=True, stop=True)
            pe.matmul(ps[6][:, 0:SEQ], tabv("dup")[64:P, :], XB[64:P, :], start=True, stop=True)
            pe.matmul(ps[6][:, SEQ:512], tabv("dup_swap")[64:P, :], XB[64:P, :], start=True,
                      stop=True).then_inc(MX.rope_made, 1)
            pe.wait_ge(MX.roped, 1)
            turn_pe(pe, "gla", OG)
            pe.wait_ge(MX.up_copied, 14)
            for k in range(KD):
                pe.wait_ge(TR.lo, TB["gla"].split + k + 1)
                tokens_still(pe, unit(BASE["ogla"] + k), ACC, [k], 512, xhi, xlo, k == 0, k == KD - 1)

            def scores(h, bank):
                half = slice(h % 2 * 64, h % 2 * 64 + 64)
                for q, keys, cols in ((slice(0, P), slice(0, P), slice(0, P)),
                                      (slice(P, SEQ), slice(0, SEQ), slice(P, 384))):
                    pe.matmul(bank[:, cols], QN[:, h, q], KN[:, h, keys], start=True, stop=False)
                    mm = pe.matmul(bank[:, cols], QP[half, h // 2, q], KP[half, keys], start=False, stop=True)
                return mm

            pe.wait_ge(MX.ya_used, 4)
            attention_pe(pe, mla, scores, lambda h, t: VM[:, t, h * P:h * P + P])
            turn_pe(pe, "mla", mla.AO)
            for k in range(KD):
                pe.wait_ge(TR.lo, TB["mla"].split + k + 1)
                tokens_still(pe, unit(BASE["omla"] + k), ACC, [8 + k], 512, xhi, xlo, k == 0, k == KD - 1)
            turn_pe(pe, "mixed", GA)
            for k in range(KD):
                pe.wait_ge(TR.lo, TB["mixed"].split + k + 1)
                tokens_still(pe, unit(BASE["w2"] + k), ACC, [k], 512, xhi, xlo, k == 0, k == KD - 1)
            turn_pe(pe, "ffn2", scr)
            ffn_pe(pe, 2, False)

        def block2_act(act):
            def copy(last, dst, bank, func=ACT.Copy, scale=1.0, done=MX.copied):
                act.wait_ge(unit_done, last + 1)
                act.activation(dst, bank, func, scale=scale).then_inc(done, 1)

            act.wait_ge(FS[1].resid, 1)
            act.dma_start(W_A2[0:16, :], w_a2).then_inc(MX.w_a2, 16)
            norm_act(act, "final", FS[1].resid, lambda t: 2 * t + 2)
            norm_act(act, "mix", rescaled, lambda t: t + 1)
            turn_act(act, "mix")
            act.dma_start(scr[:].rearrange("p t c -> p (t c)"),
                          rows["b_gate"].broadcast_to([P, 2 * D])).then_inc(MX.row_gate, 16)
            for name, n, dst, b0, width in (("cq", 4, CQ, 0, QL), ("ckv", 2, CKV, 2, KVL)):
                for k in range(n - 1):
                    refill(act, BASE[name] + k)
                for t in range(NT):
                    copy(BASE[name] + n - 1, dst[:, t, :], ps[b0 + t][:, 0:width])
                refill(act, BASE[name] + n - 1)
            copy(BASE["x"], XB, ps[4][:, 0:SEQ])
            refill(act, BASE["x"])
            for h in range(GH):
                copy(BASE["gq"] + h, GQT[:, h, :], ps[(5, 6, 7, 4)[h]][:, 0:SEQ], scale=float(P) ** -0.5)
                refill(act, BASE["gq"] + h)
            act.wait_ge(MX.copied, 4)
            for i, (src, width) in enumerate(((CQ, QL), (CKV, KVL))):
                for t in range(NT):
                    act.activation(LX[:, t, 0:width], src[:, t, :], ACT.Square,
                                   accum_out=CSQ[:, 2 * i + t:2 * i + t + 1]).then_inc(MX.c_squares, 1)
                act.wait_ge(MX.c_squares, 2 * i + 2)
            act.wait_ge(MX.la_x, 1)
            act_link(act.activation(LT, LA, ACT.Abs))
            act_link(act.activation(LT, LT, ACT.Exp, scale=-1.0))
            act.activation(LT, LT, ACT.Ln, bias=ones[:, 0:1]).then_inc(MX.la_ln, 1)

            def chunk(c):
                name = CHUNKS[c]
                last = BASE[name[:-1]] + int(name[-1]) * 4 + 3
                for k in range(3, 0, -1):
                    refill(act, last - k)
                half = int(name[-1]) * 512
                dst, func = {"gk": (GK, ACT.Copy), "gv": (GV, ACT.Copy), "gg": (GG, ACT.Silu)}.get(name[:-1], (None, None))
                if dst is not None:
                    for t in range(NT):
                        copy(last, dst[:, t, half:half + 512], ps[c % 2 * 2 + t][:], func)
                refill(act, last)

            chunk(0)
            act.wait_ge(MX.suffix, 1)
            for t in range(NT):
                ins = act.activation(LX[:, t, :], ps[5 + t][:], ACT.Exp, scale=1.0 / 16.0)
            ins.then_inc(MX.decays, 1)
            act.activation(DC, ps[7][:, 0:16], ACT.Exp, scale=1.0 / 16.0).then_inc(MX.decays, 1)
            chunk(1)
            chunk(2)
            chunk(3)
            i = 0
            for n, (bank, name, ks, slot) in enumerate(((4, "q_norm", (0, 1), 8), (5, "q_norm", (2,), 10),
                                                        (6, "kv2_norm", (0, 1), 11))):
                act.wait_ge(MX.c_turned, n + 1)
                for i, k in enumerate(ks):
                    act.activation(xhi[:, slot + i, :], ps[bank][:, i * SEQ:i * SEQ + SEQ], ACT.Copy,
                                   scale=colv(name, k)).then_inc(MX.c_hi, 1)
            for c in range(4, 9):
                chunk(c)
            act.wait_ge(MX.gates_in, 8)
            for g in (GA, GB):
                act.activation(g, g, ACT.Sigmoid).then_inc(MX.sigmoid, 1)
            for h in range(NT * GH):
                if h % GH == 0:
                    act.wait_ge(MX.o, 2 * (h // GH) + 2)
                t, q = h // GH, h % GH
                act.activation(scr[:, t, q * GDV:q * GDV + GDV], ACC[t][q // 2][:, q % 2 * GDV:q % 2 * GDV + GDV],
                               ACT.Square, accum_out=OSQ[:, h:h + 1]).then_inc(MX.o_squares, 1)
            for i in range(6):
                dst = QN[:, 2 * i:2 * i + 2, :] if i < 4 else QP[:, 2 * i - 8:2 * i - 6, :]
                copy(BASE["uq"] + i, dst, ps[4 + i % 4][:].rearrange("p (a b) -> p a b", a=2), scale=192.0 ** -0.5, done=MX.up_copied)
                refill(act, BASE["uq"] + i)
            for i in range(4):
                copy(BASE["kn"] + i // 2, KN[:, 2 * i:2 * i + 2, :],
                     ps[(6, 7, 4, 5)[i]][:].rearrange("p (a b) -> p a b", a=2), done=MX.up_copied)
                if i % 2:
                    refill(act, BASE["kn"] + i // 2)
            refill(act, BASE["vm"])
            for i in range(4):
                copy(BASE["vm"] + 1, VM[:, i // 2, i % 2 * 512:i % 2 * 512 + 512], ACC[i // 2][i % 2], done=MX.up_copied)
            refill(act, BASE["vm"] + 1)
            turn_act(act, "gla")
            act.dma_start(row_post, rows["post_mix"].broadcast_to([P, D])).then_inc(MX.row_post, 16)
            act.dma_start(row_ffn, rows["post_ffn"].broadcast_to([P, D])).then_inc(MX.row_ffn, 16)
            for k in range(KD):
                refill(act, BASE["ogla"] + k)
            attention_act(act, mla)
            turn_act(act, "mla")
            for k in range(KD):
                refill(act, BASE["omla"] + k)
            turn_act(act, "mixed")
            for k in range(KD):
                refill(act, BASE["w2"] + k)
            for i in range(4):
                copy(BASE["w2"] + 7, MIXED[:, i // 2, i % 2 * 512:i % 2 * 512 + 512], ACC[i // 2][i % 2], done=MX.w2_copied)
            norm_act(act, "post_mix", MX.w2_copied, lambda t: 2 * t + 2, MIXED)
            norm_act(act, "ffn2", rescaled, lambda t: t + 3)
            turn_act(act, "ffn2")
            ffn_act(act, 2, False)
            for i in range(4):
                copy(UNITS - 1, MIXED[:, i // 2, i % 2 * 512:i % 2 * 512 + 512], ACC[i // 2][i % 2], done=MX.w2_copied)
            norm_act(act, "post_ffn", MX.w2_copied, lambda t: 2 * t + 6, MIXED)

        def block2_dve(dve):
            dve.wait_ge(SW.row_final, 16)
            norm_dve(dve, "final", row_final)
            norm_dve(dve, "mix")
            turn_dve(dve, "mix")
            dve.wait_ge(MX.la_made, 1)
            dve.wait_ge(SW.row_b, 16)
            for t in range(NT):
                ins = dve.tensor_tensor(LA[:, t, :], ps[5 + t][:], row_b_a2, ALU.add)
            ins.then_inc(MX.la_x, 1)
            dve.wait_ge(MX.la_ln, 1)
            dve.scalar_tensor_tensor(LA, LA, 0.0, LT, ALU.min, ALU.subtract).then_inc(MX.la, 1)
            dve.wait_ge(MX.c_squares, 4)
            for i, (src, width) in enumerate(((CQ, QL), (CKV, KVL))):
                ss, r = CSQ[:, 2 * i:2 * i + 2], CSQ[:, 4 + 2 * i:6 + 2 * i]
                inverse_root(dve, r, ss, width * EPS, root_tmp[:, 0:2])
                for t in range(NT):
                    ins = dve.tensor_scalar(src[:, t, :], src[:, t, :], r[:, t:t + 1], None, ALU.mult)
            ins.then_inc(MX.c_ready, 1)
            dve.wait_ge(MX.decays, 1)
            dve.wait_ge(MX.copied, 11)
            dve.tensor_tensor(GK, GK, LX, ALU.mult).then_inc(MX.kdec, 1)
            n = 0
            for bank, name, ks, slot in ((4, "q_norm", (0, 1), 8), (5, "q_norm", (2,), 10), (6, "kv2_norm", (0, 1), 11)):
                n += len(ks)
                dve.wait_ge(MX.c_hi, n)
                for i, k in enumerate(ks):
                    dve.scalar_tensor_tensor(xlo[:, slot + i, :], ps[bank][:, i * SEQ:i * SEQ + SEQ], colv(name, k),
                                             xhi[:, slot + i, :].bitcast(F32), ALU.mult, ALU.subtract).then_inc(MX.c_lo, 1)
            dve.wait_ge(MX.row_gate, 16)
            for c in range(4):
                dve.wait_ge(unit_done, BASE["gates"] + 4 * c + 4)
                for t in range(NT):
                    dve.tensor_tensor((GA, GB)[c // 2][:, t, c % 2 * 512:c % 2 * 512 + 512],
                                      ps[(c + 1) % 2 * 2 + t][:], scr[:, c // 2, c % 2 * 512:c % 2 * 512 + 512],
                                      ALU.add).then_inc(MX.gates_in, 1)
            dve.wait_ge(MX.decays, 2)
            for c in range(2 * NT):
                dve.wait_ge(MX.kv, c + 1)
                if c >= 2:
                    dve.wait_ge(MX.o, c - 1)
                if c:
                    dve.wait_ge(MX.state, c)
                for h in range(GH):
                    new, old = (ST[:, i % 2, h * GDV:h * GDV + GDV] for i in (c, c + 1))
                    kv = ps[4 + c % 2 * 2 + h // 2][:, h % 2 * GDV:h % 2 * GDV + GDV]
                    i = (c // 2 * GH + h) * 2 + c % 2
                    if c == 0:
                        ins = dve.tensor_copy(new, kv)
                    else:
                        ins = dve.scalar_tensor_tensor(new, old, DC[:, i:i + 1], kv, ALU.mult, ALU.add)
                ins.then_inc(MX.state, 1)
            dve.wait_ge(MX.o_squares, 8)
            inverse_root(dve, OSQ[:, 8:16], OSQ[:, 0:8], GDV * EPS, root_tmp[:, 0:8])
            for t in range(NT):
                for half in range(2):
                    i = 8 + t * GH + half * 2
                    o = OG[:, t, half * 512:half * 512 + 512]
                    dve_link(dve.tensor_tensor(o.rearrange("p (h c) -> p h c", h=2),
                                               ACC[t][half].rearrange("p (h c) -> p h c", h=2),
                                               OSQ[:, i:i + 2].unsqueeze(2).broadcast_to([P, 2, GDV]), ALU.mult))
                    ins = dve.tensor_tensor(o, o, GG[:, t, half * 512:half * 512 + 512], ALU.mult)
                ins.then_inc(TR.ready, 1)
            dve.wait_ge(MX.rope_made, 1)
            dve.wait_ge(IN.rope, 1)
            dve.wait_ge(IN.sin, 2)
            part = scr[:, 0, :].rearrange("p (a b) -> p a b", a=4)
            kpart = scr[:, 1, 0:SEQ]
            for i in range(2):
                dve.tensor_tensor(part[:, 2 * i:2 * i + 2, :], ps[4 + i][:].rearrange("p (a b) -> p a b", a=2),
                                  sinT[:].unsqueeze(1).broadcast_to([P, 2, SEQ]), ALU.mult)
            dve.tensor_tensor(QP, QP, cosT[:].unsqueeze(1).broadcast_to([P, 4, SEQ]), ALU.mult)
            dve.tensor_tensor(kpart, ps[6][:, SEQ:512], sinT[:], ALU.mult)
            dve_link(dve.tensor_tensor(KP, ps[6][:, 0:SEQ], cosT[:], ALU.mult))
            dve.tensor_tensor(QP, QP, part, ALU.add)
            dve.tensor_tensor(KP, KP, kpart, ALU.add).then_inc(MX.roped, 1)
            turn_dve(dve, "gla")
            dve.wait_ge(MX.sigmoid, 2)
            dve.wait_ge(unit_done, BASE["ogla"] + KD)
            for t in range(NT):
                for half in range(2):
                    g = GA[:, t, half * 512:half * 512 + 512]
                    dve.tensor_tensor(g, g, ACC[t][half], ALU.mult).then_inc(MX.ya_used, 1)
            mask = tabv("chunk_mask")
            attention_dve(dve, mla, lambda h, t: mask[:, PARTS[t]], lambda h: -BIG)
            attention_finish(dve, mla, lambda: None)
            turn_dve(dve, "mla")
            dve.wait_ge(unit_done, BASE["omla"] + KD)
            dve.wait_ge(MX.ya_used, 4)
            for t in range(NT):
                for half in range(2):
                    a, b = (g[:, t, half * 512:half * 512 + 512] for g in (GA, GB))
                    dve_link(dve.tensor_tensor(b, b, ACC[t][half], ALU.mult))
                    ins = dve.tensor_tensor(a, a, b, ALU.add)
                ins.then_inc(TR.ready, 1)
            turn_dve(dve, "mixed")
            dve.wait_ge(MX.row_post, 16)
            norm_dve(dve, "post_mix", row_post, MIXED)
            norm_dve(dve, "ffn2")
            turn_dve(dve, "ffn2")
            ffn_dve(dve, 2, False)
            dve.wait_ge(MX.row_ffn, 16)
            norm_dve(dve, "post_ffn", row_ffn, MIXED)
        IN = sems("in", "tabs ident cols small pos rel x0 x1 band_ps band band_out sin scaled rope angle")
        rel = sb("rel", [P, 16])
        band = sb("band", [P, 384])
        ang, _o = carve(0, SEQ)
        turns, _o = carve(_o, SEQ)
        posi = area[:, _o:_o + SEQ].bitcast(I32)

        def load_x(sp):
            sp.dma_start(resid[:, 0, :], x[0:P, :]).then_inc(IN.x0, 16)
            sp.dma_start(resid[:, 1, :], x[P:SEQ, :]).then_inc(IN.x1, 16)

        def load_parameters(act):
            act.dma_start(tab[:, 0:512], tabs[:, 0:512]).then_inc(IN.ident, 16)
            act.dma_start(col[:], cols).then_inc(IN.cols, 16)
            act.dma_start(rel[0:32, :], rel_table).then_inc(IN.rel, 16)
            act.dma_start(small[:], rows["small"].broadcast_to([P, 48])).then_inc(IN.small, 16)
            act.dma_start(posi, positions.broadcast_to([P, SEQ])).then_inc(IN.pos, 16)
            act.dma_start(tab[:, 512:NTABS], tabs[:, 512:NTABS]).then_inc(IN.tabs, 16)

        def start_act_late(act):
            act.wait_ge(IN.band, 1)
            act.dma_start(band_scratch, band[0:16, :].unsqueeze(1).broadcast_to([16, P, 384])).then_inc(IN.band_out, 16)
            for n, dst in enumerate((sinT, cosT)):
                act.wait_ge(IN.angle, n + 1)
                act.activation(dst[:], dst[:], ACT.Sin).then_inc(IN.sin, 1)

        def start_pe(pe):
            pe.wait_ge(IN.ident, 16)
            pe.wait_ge(IN.rel, 16)
            pe.wait_ge(IN.scaled, 1)
            pe.matmul(ps[1][0:16, 0:BANDX], rel[0:33, :], tabv("buckets")[0:33, 0:BANDX], start=True,
                      stop=True).then_inc(IN.band_ps, 1)

        def start_dve(dve):
            dve.memset(rel[32:33, :], -BIG).then_inc(IN.scaled, 1)
            dve_link(dve.memset(band[0:16, :], 0.0))
            dve.wait_ge(IN.band_ps, 1)
            dve.tensor_copy(band[0:16, 0:BANDX], ps[1][0:16, 0:BANDX]).then_inc(IN.band, 1)
            dve.wait_ge(IN.cols, 16)

        def start_dve_late(dve):
            for name, n, width in (("out_norm", 1, HD), ("gla_norm", 2, GDV), ("q_norm", 3, QL), ("kv2_norm", 2, KVL)):
                c = col[:, COL[name]:COL[name] + n]
                dve_link(dve.tensor_scalar(c, c, float(width) ** 0.5, None, ALU.mult))
            dve.wait_ge(IN.pos, 16)
            dve_link(dve.tensor_copy(ang, posi))
            dve_link(dve.tensor_scalar(ang, ang, colv("inv_freq"), None, ALU.mult))
            c1, c2 = 6.28125, float(np.float32(int((2 * np.pi - 6.28125) * 2 ** 20) / 2 ** 20))
            c3 = float(2 * np.pi - c1 - c2)
            magic = 1.5 * 2.0 ** 23
            for dst, quarter in ((sinT, 0.0), (cosT, 0.25)):
                dve_link(dve.tensor_scalar(turns, ang, float(0.5 / np.pi), quarter, ALU.mult, ALU.add))
                dve_link(dve.tensor_scalar(turns, turns, magic, -magic, ALU.add, ALU.add))
                dve_link(dve.scalar_tensor_tensor(dst[:], turns, -c1, ang, ALU.mult, ALU.add))
                dve_link(dve.scalar_tensor_tensor(dst[:], turns, -c2, dst[:], ALU.mult, ALU.add))
                dve_link(dve.scalar_tensor_tensor(dst[:], turns, -c3, dst[:], ALU.mult, ALU.add))
                dve_link(dve.tensor_scalar(dst[:], dst[:], quarter * 2 * np.pi, float(np.float32(3.1415925)), ALU.add, ALU.min))
                dve.tensor_scalar(dst[:], dst[:], -float(np.float32(3.1415925)), None, ALU.max).then_inc(IN.angle, 1)
            dve.wait_ge(IN.sin, 1)
            dve.tensor_scalar(sinT[:], sinT[:], colv("rope_sign"), None, ALU.mult).then_inc(IN.rope, 1)
        out_done = sem("out_done")
        block = ctx.enter_context(nc.Block())

        @block.sync
        def _(sp):
            load_x(sp)
            for k in range(RING):
                load_unit(sp, unit(k))
            with sp.Fori(1, UNITS // RING) as i:
                for k in range(RING):
                    load_unit(sp, unit(k, i))
            for k in range(UNITS // RING * RING, UNITS):
                load_unit(sp, unit(k))
            for t in range(NT):
                sp.wait_ge(rescaled, 2 * NT + t + 1)
                sp.dma_start(out[t * P:t * P + P, :], resid[:, t, :]).then_inc(out_done, 16)
            sp.wait_ge(out_done, 16 * NT)

        @block.gpsimd
        def _(pool):
            for k in range(RING):
                rest_of_unit(pool, unit(k))
            with pool.Fori(1, UNITS // RING) as i:
                for k in range(RING):
                    rest_of_unit(pool, unit(k, i))
            for k in range(UNITS // RING * RING, UNITS):
                rest_of_unit(pool, unit(k))

        @block.scalar
        def _(act):
            load_parameters(act)
            act.wait_ge(IN.x0, 16)
            norm_act(act, "a", IN.x1, lambda t: 16)
            round_unit(act, unit(0))
            round_unit(act, unit(1))
            act.wait_ge(IN.cols, 16)
            turn_act(act, "a")
            for k in range(2, RING):
                round_unit(act, unit(k))
            gates_act(act)
            start_act_late(act)
            qkv_act(act)
            delta_act(act)
            act.wait_ge(DN.resid, 1)
            swa_load(act)
            norm_act(act, "ffn0", DN.resid, lambda t: 2 * t + 2)
            turn_act(act, "ffn0")
            ffn_act(act, 0, True)
            norm_act(act, "b", FS[0].resid, lambda t: 2 * t + 2)
            turn_act(act, "b")
            swa_act(act)
            norm_act(act, "ffn1", SW.resid, lambda t: 2 * t + 2)
            turn_act(act, "ffn1")
            ffn_act(act, 1, True)
            block2_act(act)

        @block.tensor
        def _(pe):
            start_pe(pe)
            turn_pe(pe, "a", scr)
            qkv_pe(pe)
            delta_pe(pe)
            turn_pe(pe, "ffn0", scr)
            ffn_pe(pe, 0, True)
            turn_pe(pe, "b", scr)
            swa_pe(pe)
            turn_pe(pe, "ffn1", scr)
            ffn_pe(pe, 1, True)
            block2_pe(pe)

        @block.vector
        def _(dve):
            start_dve(dve)
            norm_dve(dve, "a")
            turn_dve(dve, "a")
            gates_dve(dve)
            start_dve_late(dve)
            qkv_dve(dve)
            delta_dve(dve)
            norm_dve(dve, "ffn0")
            turn_dve(dve, "ffn0")
            ffn_dve(dve, 0, True)
            swa_clear(dve)
            add_residual(dve, BASE["kv"] - 1, FS[0].resid)
            norm_dve(dve, "b")
            turn_dve(dve, "b")
            swa_dve(dve)
            norm_dve(dve, "ffn1")
            turn_dve(dve, "ffn1")
            ffn_dve(dve, 1, True)
            add_residual(dve, BASE["cq"] - 1, FS[1].resid)
            block2_dve(dve)




def t5_buckets(dist):
    n = np.maximum(dist, 0)
    nf = np.maximum(n, 1).astype(np.float32)
    scale = np.float32(np.log(128 / 16))
    large = 16 + (np.log(nf / np.float32(16)) / scale * np.float32(16)).astype(np.int32)
    return np.where(n < 16, n, np.minimum(large, 31))


def tables():
    i, j = np.arange(P)[:, None], np.arange(P)[None, :]
    t = {"ident": i == j, "ones": np.ones((P, P)), "tri": i <= j,
         "future": np.where(j >= i, 0.0, -BIG), "later": (i > j) & (i // 64 == j // 64),
         "swap": i == (j ^ 32), "dup": i == 64 + j % 64, "dup_swap": i == 64 + (j % 64 ^ 32)}
    levels = []
    for lv in range(LEVELS):
        s = 1 << lv
        left = np.array([c for c in range(P) if not c & s])[None, :]
        levels.append((i // (2 * s) == left // (2 * s)) & (i & s > 0))
    t["levels"] = np.concatenate(levels, 1)
    k = np.arange(SEQ)[None, :]
    t["chunk_mask"] = np.concatenate([np.where(j // 64 <= i // 64, 0.0, -BIG),
                                      np.where(k // 64 <= (P + i) // 64, 0.0, -BIG)], 1)
    off = np.arange(384)[None, :]
    dist = 255 - off
    inside = (dist >= 0) & (dist < 128)
    t["buckets"] = np.where(i < 32, inside & (t5_buckets(dist) == i), (i == 32) & ~inside)
    return np.concatenate([t[name].astype(np.float32) for name, _ in TABS], 1)


def still(w, blocks_per_unit=1, pad_to=UNIT):
    kt, nb = w.shape[0] // P, w.shape[1] // P
    u = w.reshape(kt, P, nb // blocks_per_unit, blocks_per_unit, P).transpose(2, 1, 3, 0, 4)
    u = u.reshape(u.shape[0], P, -1)
    return np.pad(u, ((0, 0), (0, 0), (0, pad_to - u.shape[2])))


def moving(w, kts, width):
    kt, nc_ = w.shape[0] // P, w.shape[1] // width
    u = w.reshape(kt // kts, kts, P, nc_, width).transpose(3, 0, 2, 1, 4).reshape(-1, P, kts * width)
    return np.pad(u, ((0, 0), (0, 0), (0, UNIT - u.shape[2])))


def ffn_units(up_gate, up_val, down):
    g, v, d = still(up_gate), still(up_val), moving(down, 1, D)
    order = [g[0], v[0], g[1], v[1], d[0]]
    for j in range(2, NF):
        order += [g[j], v[j], d[j - 1]]
    return np.stack(order + [d[NF - 1]])


def lay_out(a):
    f = {k: np.asarray(v) for k, v in a.items()}
    w_in = f["a_w_in"][0]
    k_first = np.concatenate([w_in[:, 1024:2048], w_in[:, 0:1024], w_in[:, 2048:4096]], 1)
    heads_ = [4 * (2 * gp + half) + r for gp in range(2) for r in range(4) for half in range(2)]
    perm = np.concatenate([np.arange(h * AHD, h * AHD + AHD) for h in heads_])
    w2 = f["w_in_2"][0]
    cut = np.cumsum([0, 512, 512, 1024, 1024, 16, QL, KVL, 64])
    gq, gk, gv, gg, ga, cq, ckv, kpe = (w2[:, cut[i]:cut[i + 1]] for i in range(8))
    wx = np.concatenate([ga, np.zeros((D, 48), np.float32), kpe], 1)
    uq = f["w_uq_2"][0].reshape(QL, MH, 192)
    uq = np.concatenate([uq[:, :, :128].reshape(QL, 1024), uq[:, :, 128:].reshape(QL, 512)], 1)
    ukv = f["w_ukv_2"][0].reshape(KVL, MH, 256)
    up, down = f["ffn_w_up"], f["ffn_w_down"]
    w_ba = np.pad(w_in[:, 6144:6176], ((0, 0), (0, P - 32)))
    parts = {
        "ba": still(w_ba),
        "qkv": still(k_first), "z": moving(w_in[:, 4096:6144], 2, 512), "wout": moving(f["a_w_out"][0], 1, D),
        "ffn0": ffn_units(up[0][:, :FF], up[0][:, FF:], down[0]),
        "kv": np.concatenate([still(f["w_kv"][:, :256]), moving(f["w_kv"][:, 256:], 4, 256)]),
        "wq": still(f["b_w_q"][0][:, perm]), "wo": moving(f["b_w_o"][0][perm], 1, D),
        "ffn1": ffn_units(up[1][:, :FF], up[1][:, FF:], down[1]),
        "cq": moving(cq, 2, QL), "ckv": moving(ckv, 4, KVL), "x": still(wx), "gq": still(gq),
        "gk": moving(gk, 2, 512), "gv": moving(gv, 2, 512), "gg": moving(gg, 2, 512),
        "gates": moving(f["w_gate_2"][0], 2, 512), "uq": still(uq, 2),
        "kn": still(ukv[:, :, :128].reshape(KVL, 1024), 4), "vm": moving(ukv[:, :, 128:].reshape(KVL, 1024), 1, D),
        "ogla": moving(f["w_o_gla_2"][0], 1, D), "omla": moving(f["w_o_mla_2"][0], 1, D),
        "w2": moving(f["w_out_2"][0], 1, D),
        "ffn2": ffn_units(f["w_ffn_gate_2"][0], f["w_ffn_up_2"][0], f["w_ffn_down_2"][0]),
    }
    for name, n in PLAN:
        assert parts[name].shape == (n, P, UNIT), (name, parts[name].shape)
    stream = np.concatenate([parts[name] for name, _ in PLAN])

    def by_partition(v):
        return v.reshape(-1, P).T

    cw = f["a_conv_w"][0]
    cw = np.concatenate([cw[:, 1024:2048], cw[:, 0:1024], cw[:, 2048:]], 1)
    i = np.arange(P)
    inv_freq = (1.0 / (10000.0 ** (np.arange(0, 64, 2, dtype=np.float32) / np.float32(64)))).astype(np.float32)
    c = {
        "a_norm": by_partition(f["a_norm_w"][0]), "ffn0_norm": by_partition(f["ffn_norm_w"][0]),
        "kv_norm": by_partition(f["kv_norm_w"]), "b_norm": by_partition(f["b_norm_w"][0]),
        "ffn1_norm": by_partition(f["ffn_norm_w"][1]), "pre_mix": by_partition(f["pre_mix_norm_2"][0]),
        "pre_ffn": by_partition(f["pre_ffn_norm_2"][0]), "out_norm": by_partition(f["a_out_norm_w"][0]),
        "gla_norm": by_partition(f["gla_norm_2"][0]), "q_norm": by_partition(f["q_norm_2"][0]),
        "kv2_norm": by_partition(f["kv_norm_2"][0]), "conv_a": by_partition(cw),
        "conv0": by_partition(f["ffn_conv_w"][0]), "bias0": by_partition(f["ffn_conv_b"][0]),
        "conv1": by_partition(f["ffn_conv_w"][1]), "bias1": by_partition(f["ffn_conv_b"][1]),
        "left": np.stack([np.where(i & (1 << lv), 0.0, -1.0) for lv in range(LEVELS)], 1),
        "inv_freq": inv_freq[i % 32][:, None], "rope_sign": np.where(i % 64 < 32, -1.0, 1.0)[:, None],
        "chunk_of": np.stack([i // 64 == 0, i // 64 == 1], 1),
    }
    cols = np.concatenate([c[name].astype(np.float32) for name, _ in COLS], 1)
    r = {"small": np.concatenate([f["a_dt_bias"], f["a_a_log"], f["b_sinks"][:, heads_]], 1),
         "final": f["final_norm_w"][None], "b_gate": f["b_gate_2"], "b_a2": f["b_a2_2"],
         "post_mix": f["post_mix_norm_2"], "post_ffn": f["post_ffn_norm_2"]}
    arrays = {"x": f["x"][0], "stream": stream, "cols": cols, "tabs": tables(),
              "w_a2": f["w_a2_2"][0], "rel_table": f["rel_bias_table"][:, heads_], "positions": f["positions_2"]}
    arrays.update({"row_" + k: v for k, v in r.items()})
    return {k: np.ascontiguousarray(v) for k, v in arrays.items()}


def kernel(**inputs):
    import concourse.bacc as _bacc
    from concourse.bass_utils import run_bass_kernel_spmd as _run

    nc = _bacc.Bacc("TRN2", target_bir_lowering=False, num_devices=1, dynamic_dma_scratch_size=1024)
    arrays = {f"in_{k}": v for k, v in lay_out(inputs).items()}
    ap = {k: nc.dram_tensor(k, v.shape, mybir.dt.from_np(v.dtype), kind="ExternalInput").ap()
          for k, v in arrays.items()}
    out = nc.dram_tensor("out_0", (SEQ, D), F32, kind="ExternalOutput").ap()
    band_scratch = nc.dram_tensor("band_scratch", (AH, P, 384), F32).ap()
    rows = {k[7:]: v for k, v in ap.items() if k.startswith("in_row_")}
    build(nc, ap["in_x"], ap["in_stream"], ap["in_cols"], ap["in_tabs"], rows, ap["in_w_a2"],
          ap["in_rel_table"], ap["in_positions"], out, band_scratch)
    r = _run(nc, [arrays], core_ids=[0])
    return r.results[0]["out_0"].reshape(1, SEQ, D)
```

```python
from contextlib import ExitStack

import numpy as np

import concourse.bass as bass
from concourse import mybir

F32 = mybir.dt.float32
F32R = mybir.dt.float32r
I32 = mybir.dt.int32
ALU = mybir.AluOpType
ACT = mybir.ActivationFunctionType
AX = mybir.AxisListType

P = 128
SEQ, NT = 256, 2
D, KD = 1024, 8
UNIT = 1024
RING = 6
EPS = 1e-6
BIG = 1e30

VH = 16
QKH = 8
HD = 128
FF, NF = 2816, 22
AH, AHD = 16, 64
LEVELS = 7
SMALL = 5
GH, GDV = 4, 256
MH = 8
QL, KVL = 384, 256
BANDX = 383

PLAN = [("ba", 1), ("qkv", 32), ("z", 16), ("wout", 16), ("ffn0", 3 * NF), ("kv", 4), ("wq", 8), ("wo", 8),
        ("ffn1", 3 * NF), ("cq", 4), ("ckv", 2), ("x", 1), ("gq", 4), ("gk", 4), ("gv", 8),
        ("gg", 8), ("gates", 16), ("uq", 6), ("kn", 2), ("vm", 2), ("ogla", 8), ("omla", 8),
        ("w2", 8), ("ffn2", 3 * NF)]
BASE, _n = {}, 0
for _name, _count in PLAN:
    BASE[_name] = _n
    _n += _count
UNITS = _n

COLS = [("a_norm", 8), ("ffn0_norm", 8), ("kv_norm", 8), ("b_norm", 8), ("ffn1_norm", 8),
        ("pre_mix", 8), ("pre_ffn", 8), ("out_norm", 1), ("gla_norm", 2), ("q_norm", 3),
        ("kv2_norm", 2), ("conv_a", 32 * 4), ("conv0", 44 * 3), ("bias0", 44), ("conv1", 44 * 3),
        ("bias1", 44), ("left", LEVELS), ("inv_freq", 1), ("rope_sign", 1), ("chunk_of", 2)]
COL, _n = {}, 0
for _name, _count in COLS:
    COL[_name] = _n
    _n += _count
NCOLS = _n

TABS = [("ident", 128), ("buckets", 384), ("ones", 128), ("tri", 128), ("future", 128), ("levels", LEVELS * 64),
        ("later", 128), ("chunk_mask", 384), ("swap", 128), ("dup", 128), ("dup_swap", 128)]
TAB, _n = {}, 0
for _name, _count in TABS:
    TAB[_name] = _n
    _n += _count
NTABS = _n


class Named(dict):

    def __getattr__(self, name):
        return self[name]


NORM_WAIT, TWO_NORMS_WAIT, SHORT_WAIT = 24, 50, 4


def unit(k, i=0):
    return Named(u=k + RING * i, q=k // RING + i, s=k % RING,
                           first=isinstance(i, int) and k + RING * i < RING)


def build(nc, x, stream, cols, tabs, rows, w_a2, rel_table, positions, out, band_scratch):
    with ExitStack() as ctx:
        def sb(name, shape, dt=F32):
            return ctx.enter_context(nc.sbuf_tensor(name, shape, dt))

        def sem(name):
            return ctx.enter_context(nc.semaphore(name))

        def sems(stage, names):
            return Named(**{n: sem(f"{stage}_{n}") for n in names.split()})

        raw = sb("raw", [P, RING, UNIT])
        whi = sb("whi", [P, RING, UNIT], F32R)
        wlo = sb("wlo", [P, RING, UNIT], F32R)
        xhi = sb("xhi", [P, 16, SEQ], F32R)
        xlo = sb("xlo", [P, 16, SEQ], F32R)
        fhi = sb("fhi", [P, 2, SEQ], F32R)
        flo = sb("flo", [P, 2, SEQ], F32R)
        resid = sb("resid", [P, NT, D])
        scr = sb("scr", [P, NT, D])
        col = sb("col", [P, NCOLS])
        tab = sb("tab", [P, NTABS])
        cosT = sb("cosT", [P, SEQ])
        sinT = sb("sinT", [P, SEQ])
        small = sb("small", [P, 48])
        stat = sb("stat", [P, 72])
        AREA = 19100
        area = sb("area", [P, AREA])

        def carve(offset, *shape):
            n = int(np.prod(shape))
            assert offset + n <= AREA, (offset, n)
            v = area[:, offset:offset + n]
            if len(shape) == 2:
                v = v.rearrange("p (a b) -> p a b", a=shape[0])
            if len(shape) == 3:
                v = v.rearrange("p (a b c) -> p a b c", a=shape[0], b=shape[1])
            return v, offset + n

        ps = [ctx.enter_context(nc.psum_tensor(f"bank{b}", [P, 512], F32)) for b in range(8)]

        def tabv(name):
            n = dict(TABS)[name]
            return tab[:, TAB[name]:TAB[name] + n]

        def colv(name, i=0):
            c = COL[name] + i
            return col[:, c:c + 1] if isinstance(c, int) else col[:, bass.ds(c, 1)]

        ident, ones, tri = tabv("ident"), tabv("ones"), tabv("tri")

        landed = [sem(f"landed{s}") for s in range(RING)]
        hi_ready, lo_ready, unit_done = sem("hi_ready"), sem("lo_ready"), sem("unit_done")

        def load_unit(sp, n):
            if not n.first:
                sp.wait_ge(lo_ready, n.u - RING + 1)
            src = stream[n.u] if isinstance(n.u, int) else stream[bass.ds(n.u, 1)].rearrange("a p c -> p (a c)")
            sp.dma_start(raw[:, n.s, :], src).then_inc(landed[n.s], 16)

        def round_unit(act, n):
            act.wait_ge(landed[n.s], 16 * n.q + 16)
            if not n.first:
                act.wait_ge(unit_done, n.u - RING + 1)
            act.activation(whi[:, n.s, :], raw[:, n.s, :], ACT.Copy).then_inc(hi_ready, 1)

        def rest_of_unit(pool, n):
            pool.wait_ge(hi_ready, n.u + 1)
            pool.tensor_tensor(wlo[:, n.s, :], raw[:, n.s, :], whi[:, n.s, :].bitcast(F32),
                               ALU.subtract).then_inc(lo_ready, 1)

        def refill(act, n):
            k = n if isinstance(n, Named) else unit(n)
            if isinstance(k.u, int) and k.u + RING >= UNITS:
                return
            round_unit(act, Named(u=k.u + RING, q=k.q + 1, s=k.s, first=False))

        def three(out_ap, a_hi, a_lo, b_hi, b_lo, start, stop):
            nc.tensor.matmul(out_ap, a_hi, b_hi, start=start, stop=False)
            nc.tensor.matmul(out_ap, a_hi, b_lo, start=False, stop=False)
            return nc.tensor.matmul(out_ap, a_lo, b_hi, start=False, stop=stop)

        def weights_still(pe, n, outs, kts, xs, split=None):
            pe.wait_ge(lo_ready, n.u + 1)
            i = 0
            for o in outs:
                for k in range(kts):
                    if split:
                        pe.wait_ge(TR.lo, split(k | 1))
                    w = slice(i * P, i * P + P)
                    mm = three(o, whi[:, n.s, w], wlo[:, n.s, w], xhi[:, xs + k, :], xlo[:, xs + k, :],
                               k == 0, k == kts - 1)
                    i += 1
            mm.then_inc(unit_done, 1)

        def tokens_still(pe, n, banks, slots, width, ah, al, first, last, halves_first=False):
            pe.wait_ge(lo_ready, n.u + 1)
            halves = len(banks[0])
            order = [(t, h) for t in range(NT) for h in range(halves)]
            if halves_first:
                order = [(t, h) for h in range(halves) for t in range(NT)]
            for t, h in order:
                tok = slice(t * P, t * P + P)
                for i, k in enumerate(slots):
                    w0 = (i * halves + h) * width
                    w = slice(w0, w0 + width)
                    mm = three(banks[t][h], ah[:, k, tok], al[:, k, tok], whi[:, n.s, w],
                               wlo[:, n.s, w], first and i == 0, last and i == len(slots) - 1)
            mm.then_inc(unit_done, 1)

        def chain(eng, name):
            s, n = sem(name), [0]

            def link(ins):
                n[0] += 1
                ins.then_inc(s, 1)
                eng.wait_ge(s, n[0])
            return link

        dve_link = chain(nc.vector, "dve_chain")
        act_link = chain(nc.scalar, "act_chain")
        root_tmp = sb("root_tmp", [P, 32])

        def inverse_root(dve, y, w, n, eps, tmp):
            dve_link(dve.tensor_scalar(w, w, 1.0 / n, eps, ALU.mult, ALU.add))
            dve_link(dve.tensor_scalar(y.bitcast(I32), w.bitcast(I32), -0.5, float(0x5F3759DF), ALU.mult, ALU.add))
            for _ in range(3):
                dve_link(dve.tensor_tensor(tmp, y, w, ALU.mult))
                dve_link(dve.scalar_tensor_tensor(tmp, tmp, -0.5, y, ALU.mult, ALU.mult))
                dve_link(dve.scalar_tensor_tensor(y, tmp, 1.5, y, ALU.add, ALU.mult))

        def inverse_root_of_one(dve, y, w, n, eps, tmp):
            dve_link(dve.tensor_scalar(w, w, -0.5 / n, -0.5 * eps, ALU.mult, ALU.add))
            dve_link(dve.tensor_scalar(y.bitcast(I32), w.bitcast(I32), -0.5,
                                       float(0x5F3759DF - 0x400000 - 0x40000000), ALU.mult, ALU.add))
            for _ in range(3):
                dve_link(dve.scalar_tensor_tensor(tmp, w, y, y, ALU.mult, ALU.mult))
                dve_link(dve.scalar_tensor_tensor(y, tmp, 1.5, y, ALU.add, ALU.mult))

        TURNS = {"a": [("a_norm", 0)], "ffn0": [("ffn0_norm", 0)], "b": [("kv_norm", 0), ("b_norm", 8)],
                 "attn": [(None, 0)], "ffn1": [("ffn1_norm", 0)], "mix": [("pre_mix", 0)],
                 "gla": [("gla_norm", 0)], "mla": [(None, 8)], "mixed": [(None, 0)],
                 "ffn2": [("pre_ffn", 0)]}
        TR = sems("turn", "ready turned hi lo")
        TB, _i, _c = {}, 0, 0
        for _k, _v in TURNS.items():
            _c += 8 * len(_v)
            TB[_k] = Named(ready=4 * _i, halves_first=_k in ("attn", "gla", "mla", "mixed"), turned=4 * _i, split=_c - 8 * len(_v), done=_c)
            _i += 1

        def weight_of(name, k):
            return 1.0 if name is None else colv(name, k % 2 if name == "gla_norm" else k)

        def keep_clock(pe, bank, n):
            for _ in range(n // 4):
                pe.matmul(bank[:], ident, tab[:, 0:512], start=True, stop=True)
            for _ in range(n % 4):
                pe.matmul(bank[:, 0:P], ident, ident, start=True, stop=True)

        def turn_pe(pe, key, src, before=0, between=0, after=0):
            b = TB[key]
            keep_clock(pe, ps[7], before)
            order = [(t, pair) for t in range(NT) for pair in range(4)]
            if b.halves_first:
                order = [(t, pair) for pair in range(4) for t in range(NT)]
            for i, (t, pair) in enumerate(order):
                half = pair // 2
                if i == 4:
                    keep_clock(pe, ps[3], between)
                if pair % 2 == 0:
                    pe.wait_ge(TR.ready, b.ready + 1 + (2 * half + t if b.halves_first else 2 * t + half))
                for k in (2 * pair, 2 * pair + 1):
                    c = k % 2 * SEQ + t * P
                    mm = pe.transpose(ps[4 + pair][:, c:c + P], src[:, t, k * P:k * P + P], ident)
                if t == NT - 1:
                    mm.then_inc(TR.turned, 1)
            keep_clock(pe, ps[3], after)

        def split_of(key, copy=0):
            n = len(TURNS[key])
            return lambda k: TB[key].split + 2 * n * (k // 2) + 2 * copy + k % 2 + 1

        def turn_act(act, key):
            for pair in range(4):
                act.wait_ge(TR.turned, TB[key].turned + pair + 1)
                for name, slot in TURNS[key]:
                    for k in (2 * pair, 2 * pair + 1):
                        act.activation(xhi[:, slot + k, :], ps[4 + pair][:, k % 2 * SEQ:k % 2 * SEQ + SEQ],
                                       ACT.Copy, scale=weight_of(name, k)).then_inc(TR.hi, 1)

        def turn_dve(dve, key):
            for pair in range(4):
                n = len(TURNS[key])
                dve.wait_ge(TR.hi, TB[key].split + 2 * n * (pair + 1))
                for name, slot in TURNS[key]:
                    for k in (2 * pair, 2 * pair + 1):
                        dve.scalar_tensor_tensor(
                            xlo[:, slot + k, :], ps[4 + pair][:, k % 2 * SEQ:k % 2 * SEQ + SEQ],
                            weight_of(name, k), xhi[:, slot + k, :].bitcast(F32), ALU.mult,
                            ALU.subtract).then_inc(TR.lo, 1)

        NORMS = {k: i for i, k in enumerate(["a", "ffn0", "b", "ffn1", "final", "mix", "post_mix",
                                             "ffn2", "post_ffn"])}
        squares, rescaled = sem("squares"), sem("rescaled")

        HALVES = [(t, h, slice(h * 512, h * 512 + 512)) for t in range(NT) for h in range(2)]

        def norm_act(act, key, ready, value, src=None):
            for i, (t, h, cols) in enumerate(HALVES):
                st = 8 * NORMS[key] + i
                act.wait_ge(ready, value(t, h))
                act.activation(scr[:, t, cols], src[t][h] if src else resid[:, t, cols], ACT.Square,
                               accum_out=stat[:, st:st + 1]).then_inc(squares, 1)

        def norm_dve(dve, key, row=None, src=None):
            n, base = NORMS[key], 8 * NORMS[key]
            for t in range(NT):
                a, b, r = (stat[:, base + i:base + i + 1] for i in (2 * t, 2 * t + 1, 4 + 2 * t))
                tmp = stat[:, base + 5 + 2 * t:base + 6 + 2 * t]
                dve.wait_ge(squares, 4 * n + 2 * t + 2)
                dve_link(dve.tensor_tensor(a, a, b, ALU.add))
                inverse_root_of_one(dve, r, a, D, EPS, tmp)
                for h in range(2):
                    cols = slice(h * 512, h * 512 + 512)
                    x, y = resid[:, t, cols], scr[:, t, cols]
                    if row is None:
                        dve.tensor_scalar(y, x, r, None, ALU.mult).then_inc(TR.ready, 1)
                    elif src is None:
                        dve.scalar_tensor_tensor(x, x, r, row[:, cols], ALU.mult, ALU.mult).then_inc(rescaled, 1)
                    else:
                        dve_link(dve.scalar_tensor_tensor(y, src[t][h], r, row[:, cols], ALU.mult, ALU.mult))
                        dve.tensor_tensor(x, x, y, ALU.add).then_inc(rescaled, 1)
        FS = {f: sems(f"ffn{f}", "first tap conv silu act hi lo resid") for f in range(3)}
        ffn_g, _o = carve(AREA - 6 * SEQ, 2, SEQ)
        ffn_v, _o = carve(_o, 2, SEQ)
        ffn_a, _o = carve(_o, 2, SEQ)
        ACC = [[ps[0][:], ps[1][:]], [ps[2][:], ps[3][:]]]

        def ffn_unit(f, j, i, what):
            b = BASE[f"ffn{f}"]
            if what == "down":
                return unit(b + 3 * j + 4 if j < NF - 1 else b + 3 * NF - 1, i)
            half = 0 if what == "gate" else 1
            return unit(b + half if j == 0 else b + 3 * j - 1 + half, i)

        def ffn_pe(pe, f, conv):
            s = FS[f]
            bank_free, per_tile = (s.conv, 2) if conv else (s.act, 1)

            def up(j, i, reused):
                for half, what in enumerate(("gate", "val")):
                    if reused:
                        pe.wait_ge(bank_free, per_tile * (j - 2) + 2 * per_tile * i + (half + 1 if conv else 1))
                    weights_still(pe, ffn_unit(f, j, i, what), [ps[4 + j % 2 * 2 + half][:, 0:SEQ]], KD, 0,
                                  None if reused or j or half else split_of(f"ffn{f}"))

            def down(j, i, first=False, last=False):
                pe.wait_ge(s.lo, j + 2 * i + 1)
                p = j % 2
                tokens_still(pe, ffn_unit(f, j, i, "down"), ACC, [0], 512, fhi[:, p:p + 1, :],
                             flo[:, p:p + 1, :], first, last)

            up(0, 0, False)
            up(1, 0, False)
            down(0, 0, first=True)
            with pe.Fori(0, (NF - 2) // 2) as i:
                for j in (2, 3):
                    up(j, i, True)
                    down(j - 1, i)
            down(NF - 1, 0, last=True)

        def ffn_act(act, f, conv):
            s = FS[f]

            def tile_of(j, i, reused):
                tile, p = j + 2 * i, j % 2
                for half, (what, dst) in enumerate((("gate", ffn_g), ("val", ffn_v))):
                    n = ffn_unit(f, j, i, what)
                    src = ps[4 + p * 2 + half][:, 0:SEQ]
                    if conv or half == 0:
                        act.wait_ge(unit_done, n.u + 1)
                        if reused:
                            act.wait_ge(s.lo, tile - 1)
                    if conv:
                        act.activation(dst[:, p, :], src, ACT.Identity, bias=colv(f"bias{f}", tile + half * NF),
                                       scale=colv(f"conv{f}", 88 + tile + half * NF)).then_inc(s.first, 1)
                    elif half == 0:
                        act.activation(dst[:, p, :], src, ACT.Silu).then_inc(s.silu, 1)
                    refill(act, n)
                if conv:
                    act.wait_ge(s.conv, 2 * tile + 1)
                    act.activation(ffn_g[:, p, :], ffn_g[:, p, :], ACT.Silu).then_inc(s.silu, 1)
                act.wait_ge(s.act, tile + 1)
                if reused:
                    act.wait_ge(unit_done, ffn_unit(f, j - 2, i, "down").u + 1)
                act.activation(fhi[:, p, :], ffn_a[:, p, :], ACT.Copy).then_inc(s.hi, 1)

            tile_of(0, 0, False)
            tile_of(1, 0, False)
            refill(act, ffn_unit(f, 0, 0, "down"))
            trips = (NF - 2) // 2 - (f == 2)
            with act.Fori(0, trips) as i:
                for j in (2, 3):
                    tile_of(j, i, True)
                    refill(act, ffn_unit(f, j - 1, i, "down"))
            if f == 2:
                for j in (2, 3):
                    tile_of(j, trips, True)
                    refill(act, ffn_unit(f, j - 1, trips, "down"))
            refill(act, ffn_unit(f, NF - 1, 0, "down"))

        def ffn_dve(dve, f, conv):
            s = FS[f]

            def tile_of(j, i):
                tile, p = j + 2 * i, j % 2
                if conv:
                    for half, dst in enumerate((ffn_g, ffn_v)):
                        src, y = ps[4 + p * 2 + half], dst[:, p, :]
                        nth = 2 * tile + half + 1
                        dve.wait_ge(s.first, nth)
                        dve.scalar_tensor_tensor(y[:, 1:SEQ], src[:, 0:SEQ - 1],
                                                 colv(f"conv{f}", 44 + tile + half * NF), y[:, 1:SEQ],
                                                 ALU.mult, ALU.add).then_inc(s.tap, 1)
                        dve.wait_ge(s.tap, nth)
                        dve.scalar_tensor_tensor(y[:, 2:SEQ], src[:, 0:SEQ - 2],
                                                 colv(f"conv{f}", tile + half * NF), y[:, 2:SEQ],
                                                 ALU.mult, ALU.add).then_inc(s.conv, 1)
                    dve.wait_ge(s.conv, 2 * tile + 2)
                    dve.wait_ge(s.silu, tile + 1)
                    dve.tensor_tensor(ffn_a[:, p, :], ffn_g[:, p, :], ffn_v[:, p, :],
                                      ALU.mult).then_inc(s.act, 1)
                else:
                    dve.wait_ge(s.silu, tile + 1)
                    dve.wait_ge(unit_done, ffn_unit(f, j, i, "val").u + 1)
                    dve.tensor_tensor(ffn_a[:, p, :], ffn_g[:, p, :], ps[5 + p * 2][:, 0:SEQ],
                                      ALU.mult).then_inc(s.act, 1)
                dve.wait_ge(s.hi, tile + 1)
                dve.tensor_tensor(flo[:, p, :], ffn_a[:, p, :], fhi[:, p, :].bitcast(F32),
                                  ALU.subtract).then_inc(s.lo, 1)

            tile_of(0, 0)
            tile_of(1, 0)
            with dve.Fori(0, (NF - 2) // 2) as i:
                tile_of(2, i)
                tile_of(3, i)

        def add_residual(dve, last_unit, done):
            dve.wait_ge(unit_done, last_unit + 1)
            for t in range(NT):
                for h in range(2):
                    r = resid[:, t, h * 512:h * 512 + 512]
                    dve.tensor_tensor(r, r, ACC[t][h], ALU.add).then_inc(done, 1)

        CV = sems("qkv", "first tap conv silu square turned copied_v copied_k")
        GT = sems("gate", "copied ba exp absx logs g beta cum cum_copied")
        QK, _o = carve(0, 16, SEQ)
        V, _o = carve(_o, NT, VH * HD)
        _groups = _o
        cy, _o = carve(_groups, 2, SEQ)
        csq, _o = carve(_o, P)
        cvt, _o = carve(_o, 2, SEQ)
        cba, _o = carve(_o, SEQ)
        bufs = []
        _o = _groups
        for m in range(2):
            bufs.append([])
            for t in range(NT):
                b_ = Named()
                for name in ("M", "T", "TT", "Pm", "A"):
                    if (m, t, name) == (1, 1, "A"):
                        b_[name] = scr[:, 1, 512:D].rearrange("p (h c) -> p h c", h=4)
                    else:
                        b_[name], _o = carve(_o, 4, P)
                bufs[m].append(b_)
        K1, _o = carve(_o, QKH, P)
        Z = carve(_groups, 2, NT * 512)[0]
        gsc = sb("gsc", [P, 18 * 32])

        def gs(i, heads=16):
            return gsc[:, i * 32:i * 32 + 32].rearrange("p (t h) -> p t h", t=NT)

        BETA, G, GC, EGC, NEGC, DEC, RK, NK, BRK, RK2B, RKDEC, ROQ, SSQ, TMP, TMP2, OSS, ORS, NGC = range(18)

        def gates_copy(act):
            act.wait_ge(unit_done, BASE["ba"] + 1)
            act.activation(cba[0:32, :], ps[0][0:32, 0:SEQ], ACT.Copy).then_inc(GT.copied, 1)
            refill(act, BASE["ba"])

        def gates_act(act):
            act.wait_ge(GT.ba, 1)
            bav = ps[7][:, 0:64].rearrange("p (t c) -> p t c", t=NT)
            act.activation(gs(BETA), bav[:, :, 0:16], ACT.Exp, scale=-1.0).then_inc(GT.exp, 1)
            act.wait_ge(IN.small, 16)
            act_link(act.activation(small[:, 16:32], small[:, 16:32], ACT.Exp))
            act.wait_ge(GT.absx, 1)
            act.wait_ge(IN.tabs, 16)
            act_link(act.activation(gs(TMP2), gs(TMP), ACT.Abs))
            act_link(act.activation(gs(TMP2), gs(TMP2), ACT.Exp, scale=-1.0))
            act.activation(gs(TMP2), gs(TMP2), ACT.Ln, bias=ones[:, 0:1]).then_inc(GT.logs, 1)

        def gates_dve(dve):
            dve.wait_ge(GT.ba, 1)
            dve.wait_ge(GT.exp, 1)
            dve.wait_ge(IN.small, 16)
            bav = ps[7][:, 0:64].rearrange("p (t c) -> p t c", t=NT)
            dve.tensor_tensor(gs(TMP), bav[:, :, 16:32], small[:, 0:16].unsqueeze(1).broadcast_to([P, NT, 16]),
                              ALU.add).then_inc(GT.absx, 1)
            dve_link(dve.tensor_scalar(gs(BETA), gs(BETA), 1.0, None, ALU.add))
            dve.reciprocal(gs(BETA), gs(BETA)).then_inc(GT.beta, 1)
            dve.wait_ge(GT.logs, 1)
            dve_link(dve.scalar_tensor_tensor(gs(G), gs(TMP), 0.0, gs(TMP2), ALU.max, ALU.add))
            dve.scalar_tensor_tensor(gs(G), gs(G), -1.0,
                                     small[:, 16:32].unsqueeze(1).broadcast_to([P, NT, 16]), ALU.mult,
                                     ALU.mult).then_inc(GT.g, 1)

        def qkv_pe(pe):
            weights_still(pe, unit(BASE["ba"]), [ps[0][:, 0:SEQ]], KD, 0, split_of("a"))
            for b in range(32 + 2):
                if b < 32:
                    if b == 3:
                        pe.wait_ge(GT.copied, 1)
                    if b >= 4:
                        pe.wait_ge(CV.conv, b - 3)
                    weights_still(pe, unit(BASE["qkv"] + b), [ps[(b + 1) % 4][:, 0:SEQ]], KD, 0)
                if b == 1:
                    pe.wait_ge(GT.copied, 1)
                    for t in range(NT):
                        mm = pe.transpose(ps[7][:, t * 32:t * 32 + 32], cba[0:32, t * P:t * P + P], ident[0:32, 0:32])
                    mm.then_inc(GT.ba, 1)
                if b == 8:
                    pe.wait_ge(GT.g, 1)
                    pe.wait_ge(IN.tabs, 16)
                    pe.matmul(ps[7][:, 0:32], tri, gsc[:, G * 32:G * 32 + 32], start=True, stop=True)
                    pe.matmul(ps[7][:, 32:64], ones, gsc[:, G * 32:G * 32 + 32], start=True,
                              stop=True).then_inc(GT.cum, 1)
                c = b - 2
                if c >= 0:
                    pe.wait_ge(CV.silu, c + 1)
                    if 3 <= c < 11:
                        pe.wait_ge(CV.copied_k, c - 2)
                    elif c >= 19:
                        pe.wait_ge(CV.copied_v, c - 18)
                    elif c >= 3:
                        pe.wait_ge(CV.square, 2 * c - 4)
                    for t in range(NT):
                        src = QK[:, c, t * P:t * P + P] if c < 16 else cvt[:, c % 2, t * P:t * P + P]
                        mm = pe.transpose(ps[4 + c % 3][:, t * P:t * P + P], src, ident)
                    mm.then_inc(CV.turned, 1)

        def qkv_act(act):
            def finish(b):
                act.wait_ge(CV.conv, b + 1)
                if b < 16:
                    dst = QK[:, b, :]
                else:
                    if b >= 18:
                        act.wait_ge(CV.turned, b - 1)
                    dst = cvt[:, b % 2, :]
                act.activation(dst, cy[:, b % 2, :], ACT.Silu).then_inc(CV.silu, 1)

            def sum_squares(b):
                act.wait_ge(CV.turned, b + 1)
                for t in range(NT):
                    if b or t:
                        act.wait_ge(CV.square, 2 * b + t)
                    c = SSQ * 32 + t * 16 + b
                    act.activation(csq, ps[4 + b % 3][:, t * P:t * P + P], ACT.Square,
                                   accum_out=gsc[:, c:c + 1]).then_inc(CV.square, 1)

            for b in range(32):
                act.wait_ge(unit_done, BASE["qkv"] + b + 1)
                if b >= 2:
                    act.wait_ge(CV.silu, b - 1)
                act.activation(cy[:, b % 2, :], ps[(b + 1) % 4][:, 0:SEQ], ACT.Copy,
                               scale=colv("conv_a", 96 + b)).then_inc(CV.first, 1)
                if b >= 1:
                    finish(b - 1)
                refill(act, BASE["qkv"] + b)
                if 3 <= b < 19:
                    sum_squares(b - 3)
                if b == 3:
                    gates_act(act)
            finish(31)

        def qkv_dve(dve):
            def copy_v(b):
                dve.wait_ge(CV.turned, b + 1)
                dve.tensor_copy(V[:, :, (b - 16) * P:(b - 15) * P],
                                ps[4 + b % 3][:, 0:SEQ].rearrange("p (t c) -> p t c", t=NT)).then_inc(CV.copied_v, 1)

            for b in range(32):
                src, y = ps[(b + 1) % 4], cy[:, b % 2, :]
                dve.wait_ge(CV.first, b + 1)
                for tap in (1, 2, 3):
                    ins = dve.scalar_tensor_tensor(y[:, tap:SEQ], src[:, 0:SEQ - tap],
                                                   colv("conv_a", (3 - tap) * 32 + b), y[:, tap:SEQ],
                                                   ALU.mult, ALU.add)
                    if tap < 3:
                        dve_link(ins)
                ins.then_inc(CV.conv, 1)
                if b == 3:
                    gates_dve(dve)
                if b == 11:
                    dve.wait_ge(GT.cum, 1)
                    dve_link(dve.tensor_copy(gsc[:, GC * 32:GC * 32 + 32], ps[7][:, 0:32]))
                    dve.tensor_tensor(gsc[:, DEC * 32:DEC * 32 + 32], ps[7][:, 32:64],
                                      gsc[:, GC * 32:GC * 32 + 32], ALU.subtract).then_inc(GT.cum_copied, 1)
                if 4 <= b < 12:
                    h = b - 4
                    dve.wait_ge(CV.square, 2 * h + 2)
                    dve.tensor_copy(K1[:, h, :], ps[4 + h % 3][:, 0:P]).then_inc(CV.copied_k, 1)
                if b >= 19:
                    copy_v(b - 3)
            for b in (29, 30, 31):
                copy_v(b)
        DN = sems("delta", "setup decay mat init prod masked tpm updated flipped tt turned32 r1 vn1p vn1 o1p s1p s1 kqs r2 "
                  "vn2p vn2 o2p o0 qs o squares normed cleared gated z_silu turned hi lo resid exps")
        XB_, YB_ = ((ps[0], ps[2]), (ps[4], ps[6])), ((ps[1], ps[3]), (ps[5], ps[7]))
        BOTH = [(m, t) for t in range(NT) for m in range(2)]

        def by_head(i, t, g):
            c = i * 32 + t * 16 + 4 * g
            return gsc[:, c:c + 4].unsqueeze(2).broadcast_to([P, 4, P])

        def scalar(i, t, h):
            c = i * 32 + t * 16 + h
            return gsc[:, c:c + 1]

        def heads(bank, n=P):
            return bank[:, 0:4 * n].rearrange("p (h c) -> p h c", h=4)

        def blocks(flat, s, half):
            return flat.rearrange("p (n two s) -> p n two s", two=2, s=s)[:, :, half, :]

        def flat(buf):
            return buf.rearrange("p h c -> p (h c)")

        def group_cols(x, t, g):
            return x[:, t, g * 512:g * 512 + 512].rearrange("p (h c) -> p h c", h=4)

        def slot_of(k):
            return (k + 8) % 16

        def delta_pe(pe):
            pe.wait_ge(CV.copied_v, 16)
            def flip(p, lv, i):
                m, t = BOTH[i]
                for h in range(4):
                    mm = pe.transpose(YB_[m][t][:, h * P:h * P + P], bufs[m][t].T[:, h, :], ident)
                mm.then_inc(DN.flipped, 1)

            def key_products(p, t):
                tok = slice(t * P, t * P + P)
                for m in range(2):
                    g = 2 * p + m
                    if p:
                        pe.wait_ge((DN.o0, DN.o)[t], m + 1)
                    for kq in range(2):
                        k, q = QK[:, 2 * g + kq, tok], QK[:, 8 + 2 * g + kq, tok]
                        pe.matmul(XB_[m][t][:, kq * 256:kq * 256 + P], k, k, start=True, stop=True)
                        pe.matmul(XB_[m][t][:, kq * 256 + P:kq * 256 + 256], k, q, start=True, stop=True)

            def decay_sums(p, t):
                for m in range(2):
                    if p:
                        pe.wait_ge((DN.vn2, DN.qs)[t], m + 1)
                    for h in range(4):
                        pe.matmul(YB_[m][t][:, h * P:h * P + P],
                                  scalar(G, t, 4 * (2 * p + m) + h).broadcast_to([P, P]), tri, start=True, stop=False)
                        mm = pe.matmul(YB_[m][t][:, h * P:h * P + P], ident, tabv("future"), start=False, stop=True)
                    mm.then_inc(DN.setup, 1)

            for p in range(2):
                if p == 0:
                    key_products(p, 0)
                decay_sums(p, 0)
                key_products(p, 1)
                decay_sums(p, 1)
                for lv in range(LEVELS):
                    for i, (m, t) in enumerate(BOTH):
                        b = bufs[m][t]
                        if lv == 0:
                            pe.wait_ge(DN.init, 4 * p + i + 1)
                        else:
                            pe.wait_ge(DN.updated, (p * LEVELS + lv - 1) * 4 + i + 1)
                        for h in range(4):
                            mm = pe.matmul(XB_[m][t][:, h * P:h * P + P], b.M[:, h, :], b.T[:, h, :],
                                           start=True, stop=True)
                        mm.then_inc(DN.prod, 1)
                        if lv > SMALL:
                            flip(p, lv - 1, i)
                    if lv == 0:
                        continue
                    for i, (m, t) in enumerate(BOTH):
                        b = bufs[m][t]
                        pe.wait_ge(DN.masked, (p * LEVELS + lv) * 4 + i + 1)
                        if lv <= SMALL:
                            pe.wait_ge(DN.turned32, (p * SMALL + lv - 1) * 4 + i + 1)
                        else:
                            pe.wait_ge(DN.tt, (p * (LEVELS - SMALL) + lv - 1 - SMALL) * 4 + i + 1)
                        for h in range(4):
                            mm = pe.matmul(XB_[m][t][:, h * P:h * P + P], b.TT[:, h, :], b.Pm[:, h, :],
                                           start=True, stop=True)
                        mm.then_inc(DN.tpm, 1)
                for i in range(4):
                    pe.wait_ge(DN.updated, (p * LEVELS + LEVELS - 1) * 4 + i + 1)
                    flip(p, LEVELS - 1, i)
                pe.wait_ge(DN.tt, 4 * (LEVELS - SMALL) * (p + 1))
                for m, (b0, b1) in enumerate(bufs):
                    pe.wait_ge(DN.r1, 4 * p + m + 1)
                    for h in range(4):
                        mm = pe.matmul(XB_[m][0][:, h * P:h * P + P], b0.TT[:, h, :],
                                       V[:, 0, (2 * p + m) * 512 + h * P:(2 * p + m) * 512 + h * P + P],
                                       start=True, stop=True)
                    mm.then_inc(DN.vn1p, 1)
                for m, (b0, b1) in enumerate(bufs):
                    g = 2 * p + m
                    pe.wait_ge(DN.vn1, g + 1)
                    for kq in range(2):
                        mm = pe.matmul(YB_[m][0][:, kq * 256:kq * 256 + 256], K1[:, 2 * g + kq, :],
                                       b0.T[:, 2 * kq:2 * kq + 2, :], start=True, stop=True)
                    mm.then_inc(DN.s1p, 1)
                    for h in range(4):
                        mm = pe.matmul(XB_[m][0][:, h * P:h * P + P], b0.A[:, h, :], b0.Pm[:, h, :],
                                       start=True, stop=True)
                    mm.then_inc(DN.o1p, 1)
                for m, (b0, b1) in enumerate(bufs):
                    g = 2 * p + m
                    pe.wait_ge(DN.s1, g + 1)
                    for bank, which in ((XB_[m][1], 0), (YB_[m][1], 8)):
                        for kq in range(2):
                            mm = pe.matmul(bank[:, kq * 256:kq * 256 + 256], QK[:, which + 2 * g + kq, P:SEQ],
                                           b1.T[:, 2 * kq:2 * kq + 2, :], start=True, stop=True)
                    mm.then_inc(DN.kqs, 1)
                for m, (b0, b1) in enumerate(bufs):
                    pe.wait_ge(DN.r2, 2 * p + m + 1)
                    for h in range(4):
                        mm = pe.matmul(YB_[m][0][:, h * P:h * P + P], b1.TT[:, h, :], b1.M[:, h, :],
                                       start=True, stop=True)
                    mm.then_inc(DN.vn2p, 1)
                if p == 0:
                    key_products(1, 0)
                for m, (b0, b1) in enumerate(bufs):
                    pe.wait_ge(DN.vn2, 2 * p + m + 1)
                    for h in range(4):
                        mm = pe.matmul(XB_[m][1][:, h * P:h * P + P], b1.A[:, h, :], b0.T[:, h, :],
                                       start=True, stop=True)
                    mm.then_inc(DN.o2p, 1)

            def z_units(c):
                if c >= 2:
                    pe.wait_ge(DN.z_silu, 2 * c - 2)
                banks = [[ps[c % 2 * 2 + t][:]] for t in range(NT)]
                for k in range(4):
                    tokens_still(pe, unit(BASE["z"] + 4 * c + k), banks, [2 * k, 2 * k + 1], 512, xhi, xlo,
                                 k == 0, k == 3)

            def turn(pair):
                pe.wait_ge(DN.gated, (pair // 2 + 1) * 2)
                if pair >= 4:
                    pe.wait_ge(DN.lo, pair - 3)
                for k in (2 * pair, 2 * pair + 1):
                    for t in range(NT):
                        c = k % 2 * SEQ + t * P
                        mm = pe.transpose(ps[4 + pair % 4][:, c:c + P], V[:, t, k * P:k * P + P], ident)
                mm.then_inc(DN.turned, 1)

            pe.wait_ge(DN.o0, 4)
            z_units(0)
            pe.wait_ge(DN.o, 4)
            z_units(1)
            turn(0)
            turn(1)
            z_units(2)
            turn(2)
            turn(3)
            z_units(3)
            turn(4)
            turn(5)
            for pair in range(8):
                if pair == 0:
                    pe.wait_ge(DN.z_silu, 8)
                pe.wait_ge(DN.lo, pair + 1)
                for k in (2 * pair, 2 * pair + 1):
                    tokens_still(pe, unit(BASE["wout"] + k), ACC, [slot_of(k)], 512, xhi, xlo, k == 0, k == 15)
                if pair < 2:
                    turn(pair + 6)

        def delta_act(act):
            act.wait_ge(GT.cum_copied, 1)
            act.activation(gsc[:, EGC * 32:EGC * 32 + 32], gsc[:, GC * 32:GC * 32 + 32], ACT.Exp).then_inc(DN.exps, 1)
            act.activation(gsc[:, DEC * 32:DEC * 32 + 32], gsc[:, DEC * 32:DEC * 32 + 32], ACT.Exp).then_inc(DN.exps, 1)
            def squares_of(p):
                for i, (t, m) in enumerate(((0, 0), (0, 1), (1, 0), (1, 1))):
                    act.wait_ge((DN.o0, DN.o)[t], 2 * p + m + 1)
                    for h in range(4):
                        hh = 8 * p + 4 * m + h
                        act.activation(scr[:, 0, h * P:h * P + P], V[:, t, hh * P:hh * P + P], ACT.Square,
                                       accum_out=scalar(OSS, t, hh)).then_inc(DN.squares, 1)
                    act.wait_ge(DN.squares, 16 * p + 4 * i + 4)

            act.wait_ge(DN.exps, 3)
            for p in range(2):
                for i, (m, t) in enumerate(BOTH):
                    act.wait_ge(DN.setup, 4 * p + i + 1)
                    if p:
                        act.wait_ge(DN.o, 1 + m)
                    for h in range(4):
                        hh = 8 * p + 4 * m + h
                        ins = act.activation(bufs[m][t].T[:, h, :], YB_[m][t][:, h * P:h * P + P], ACT.Exp,
                                             bias=scalar(NGC, t, hh))
                    ins.then_inc(DN.decay, 1)
                for i, (m, t) in enumerate(BOTH):
                    act.wait_ge(DN.mat, 4 * p + i + 1)
                    act.activation(bufs[m][t].T, ident.unsqueeze(1).broadcast_to([P, 4, P]), ACT.Copy).then_inc(DN.init, 1)
                if p:
                    squares_of(p - 1)
                for n in range(4 * (LEVELS - SMALL)):
                    m, t = BOTH[n % 4]
                    act.wait_ge(DN.flipped, 4 * (LEVELS - SMALL) * p + n + 1)
                    act.activation(flat(bufs[m][t].TT), YB_[m][t][:], ACT.Copy).then_inc(DN.tt, 1)
                for m in range(2):
                    act.wait_ge(DN.s1p, 2 * p + m + 1)
                    act.activation(flat(bufs[m][1].T), YB_[m][0][:], ACT.Copy).then_inc(DN.s1, 1)
                for m in range(2):
                    act.wait_ge(DN.o1p, 2 * p + m + 1)
                    for h in range(4):
                        hh = 8 * p + 4 * m + h
                        ins = act.activation(V[:, 0, hh * P:hh * P + P], XB_[m][0][:, h * P:h * P + P], ACT.Copy,
                                             scale=scalar(ROQ, 0, hh))
                    ins.then_inc(DN.o0, 1)
                for m in range(2):
                    act.wait_ge(DN.kqs, 2 * p + m + 1)
                    for h in range(4):
                        ins = act.activation(bufs[m][1].T[:, h, :], YB_[m][1][:, h * P:h * P + P], ACT.Copy,
                                             scale=scalar(EGC, 1, 8 * p + 4 * m + h))
                    ins.then_inc(DN.qs, 1)
            squares_of(1)

            def refill_pair(pair):
                for k in (2 * pair, 2 * pair + 1):
                    refill(act, BASE["wout"] + k)

            def split(pair):
                if pair == 4:
                    act.wait_ge(unit_done, BASE["wout"])
                act.wait_ge(DN.turned, pair + 1)
                s = slot_of(2 * pair)
                act.activation(xhi[:, s:s + 2, :].rearrange("p a b -> p (a b)"),
                               ps[4 + pair % 4][:], ACT.Copy, scale=colv("out_norm")).then_inc(DN.hi, 1)

            for c in range(4):
                for k in range(4):
                    refill(act, BASE["z"] + 4 * c + k)
                for t in range(NT):
                    if c >= 2:
                        act.wait_ge(DN.gated, 2 * c - 3 + t)
                    act.activation(Z[:, c % 2, t * 512:t * 512 + 512], ps[c % 2 * 2 + t][:], ACT.Silu).then_inc(DN.z_silu, 1)
                if c in (1, 2):
                    split(2 * c - 2)
                    split(2 * c - 1)
            split(4)
            split(5)
            refill_pair(0)
            split(6)
            refill_pair(1)
            split(7)
            for pair in range(2, 8):
                refill_pair(pair)

        def delta_dve(dve):
            dve.wait_ge(IN.tabs, 16)
            for m, t in BOTH:
                dve.memset(bufs[m][t].Pm, 0.0).then_inc(DN.cleared, 1)
            w, rk, nk = (gsc[:, i * 32:i * 32 + 32] for i in (SSQ, RK, NK))
            dve.wait_ge(CV.square, 32)
            inverse_root(dve, rk, w, 1, EPS, root_tmp[:])
            dve_link(dve.tensor_tensor(nk, w, rk, ALU.mult))
            dve.wait_ge(DN.exps, 2)

            def pairs(i):
                return gs(i).rearrange("p t (h r) -> p t h r", r=2)

            def shared(i, q=0):
                return gs(i)[:, :, 8 * q:8 * q + 8].unsqueeze(3).broadcast_to([P, NT, 8, 2])

            dve_link(dve.tensor_tensor(pairs(BRK), pairs(BETA), shared(RK), ALU.mult))
            dve_link(dve.tensor_tensor(pairs(RK2B), pairs(BRK), shared(RK), ALU.mult))
            dve_link(dve.tensor_tensor(pairs(RKDEC), pairs(DEC), shared(RK), ALU.mult))
            dve.tensor_scalar(gs(NGC), gs(GC), -1.0, None, ALU.mult).then_inc(DN.exps, 1)
            dve_link(dve.tensor_scalar(gs(NEGC), gs(EGC), -1.0, None, ALU.mult))
            dve_link(dve.tensor_copy(pairs(TMP), shared(NK)))
            dve_link(dve.tensor_copy(pairs(ROQ), shared(RK, 1)))
            dve_link(dve.tensor_scalar(gs(ROQ), gs(ROQ), float(HD) ** -0.5, None, ALU.mult))

            for p in range(2):
                for i, (m, t) in enumerate(BOTH):
                    g, b = 2 * p + m, bufs[m][t]
                    dve.wait_ge(DN.decay, 4 * p + i + 1)
                    for h in range(4):
                        hh, c = 4 * g + h, h // 2 * 256
                        dve.scalar_tensor_tensor(b.M[:, h, :], XB_[m][t][:, c:c + P], scalar(RK2B, t, hh),
                                                 b.T[:, h, :], ALU.mult, ALU.mult)
                        ins = dve.scalar_tensor_tensor(b.A[:, h, :], XB_[m][t][:, c + P:c + 256],
                                                       scalar(RK, t, hh // 2), b.T[:, h, :], ALU.mult, ALU.mult)
                    ins.then_inc(DN.mat, 1)
                for lv in range(LEVELS):
                    s = 1 << lv
                    for i, (m, t) in enumerate(BOTH):
                        b = bufs[m][t]
                        dve.wait_ge(DN.prod, (p * LEVELS + lv) * 4 + i + 1)
                        mask = tabv("levels")[:, lv * 64:lv * 64 + 64].rearrange("p (n s) -> p n s", s=s)
                        dst = b.Pm.rearrange("p h (n two s) -> p h n two s", two=2, s=s)[:, :, :, 0, :]
                        src = XB_[m][t][:].rearrange("p (h n two s) -> p h n two s", h=4, two=2, s=s)[:, :, :, 0, :]
                        dve.tensor_tensor(dst, src, mask.unsqueeze(1).broadcast_to([P, 4, 64 // s, s]),
                                          ALU.mult).then_inc(DN.masked, 1)
                    for i, (m, t) in enumerate(BOTH):
                        b = bufs[m][t]
                        if lv:
                            product = XB_[m][t][:]
                            dve.wait_ge(DN.tpm, (p * (LEVELS - 1) + lv - 1) * 4 + i + 1)
                        else:
                            product = flat(b.Pm)
                            dve.wait_ge(DN.masked, p * LEVELS * 4 + i + 1)
                        left = blocks(flat(b.T), s, 0)
                        dve.tensor_tensor(left, left, blocks(product, s, 0), ALU.subtract).then_inc(DN.updated, 1)
                        if lv < SMALL:
                            dve.wait_ge(DN.updated, (p * LEVELS + lv) * 4 + i + 1)
                            dve.transpose(flat(b.TT), flat(b.T)).then_inc(DN.turned32, 1)
                    if 1 <= lv <= 4:
                        m, t = BOTH[lv - 1]
                        v = group_cols(V, t, 2 * p + m)
                        dve.tensor_tensor(v, v, by_head(TMP, t, 2 * p + m), ALU.mult).then_inc(DN.r1, 1)
                for m, (b0, b1) in enumerate(bufs):
                    g = 2 * p + m
                    dve.wait_ge(DN.vn1p, g + 1)
                    dve_link(dve.tensor_tensor(b0.Pm, heads(XB_[m][0]), by_head(BRK, 0, g), ALU.mult))
                    dve.tensor_tensor(b0.T, b0.Pm, by_head(RKDEC, 0, g), ALU.mult).then_inc(DN.vn1, 1)
                for m, (b0, b1) in enumerate(bufs):
                    g = 2 * p + m
                    dve.wait_ge(DN.kqs, g + 1)
                    dve_link(dve.tensor_tensor(b1.Pm, heads(XB_[m][1]), by_head(NEGC, 1, g), ALU.mult))
                    dve.wait_ge(DN.r1, 4 * p + 4)
                    dve.tensor_tensor(b1.M, group_cols(V, 1, g), b1.Pm, ALU.add).then_inc(DN.r2, 1)
                for m, (b0, b1) in enumerate(bufs):
                    g = 2 * p + m
                    dve.wait_ge(DN.vn2p, g + 1)
                    dve.tensor_tensor(b0.T, heads(YB_[m][0]), by_head(BRK, 1, g), ALU.mult).then_inc(DN.vn2, 1)
                for m, (b0, b1) in enumerate(bufs):
                    g = 2 * p + m
                    dve.wait_ge(DN.o2p, g + 1)
                    dve.wait_ge(DN.qs, g + 1)
                    dve_link(dve.tensor_tensor(b1.Pm, heads(XB_[m][1]), b1.T, ALU.add))
                    dve.tensor_tensor(group_cols(V, 1, g), b1.Pm, by_head(ROQ, 1, g), ALU.mult).then_inc(DN.o, 1)

            dve.wait_ge(DN.squares, 32)
            inverse_root(dve, gsc[:, ORS * 32:ORS * 32 + 32], gsc[:, OSS * 32:OSS * 32 + 32], HD, EPS, root_tmp[:])
            for c in range(4):
                for t in range(NT):
                    v = group_cols(V, t, c)
                    dve.tensor_tensor(v, v, by_head(ORS, t, c), ALU.mult).then_inc(DN.normed, 1)
            def split(pair):
                dve.wait_ge(DN.hi, pair + 1)
                s = slot_of(2 * pair)
                dve.scalar_tensor_tensor(xlo[:, s:s + 2, :].rearrange("p a b -> p (a b)"),
                                         ps[4 + pair % 4][:], colv("out_norm"),
                                         xhi[:, s:s + 2, :].rearrange("p a b -> p (a b)").bitcast(F32),
                                         ALU.mult, ALU.subtract).then_inc(DN.lo, 1)

            for c in range(4):
                for t in range(NT):
                    dve.wait_ge(DN.z_silu, 2 * c + t + 1)
                    dve.wait_ge(DN.normed, 2 * c + t + 1)
                    v = group_cols(V, t, c)
                    dve.tensor_tensor(v, v, Z[:, c % 2, t * 512:t * 512 + 512].rearrange("p (h c) -> p h c", h=4),
                                      ALU.mult).then_inc(DN.gated, 1)
                if c in (1, 2):
                    split(2 * c - 2)
                    split(2 * c - 1)
            for pair in range(4, 8):
                split(pair)
            add_residual(dve, BASE["wout"] + 15, DN.resid)
        AT = sems("attn", "scores maxed exps turned copied outs sunk total inverse")
        bias_, _o = carve(0, AH, SEQ)
        QT, _o = carve(_o, 8, SEQ)
        KT, _o = carve(_o, 2, SEQ)
        VN = carve(_o, NT, 4 * P)[0].rearrange("p t (g c) -> p t g c", g=4)
        _o += NT * 4 * P
        swa = Named(heads=AH, width=AHD, share=2, base=0, AO=carve(8192, NT, D)[0])
        swa["S"], _o = carve(12288, 3, 384)
        swa["PT"], _o = carve(_o, 2, 384)
        row_b_a2, _o = carve(15872, 512)
        row_final, _o = carve(_o, D)
        PARTS = (slice(0, P), slice(P, 384))
        att_stat = sb("att_stat", [P, 4 * 32])

        def att(i, n):
            return att_stat[:, i * 32:i * 32 + 2 * n].rearrange("p (h t) -> p h t", t=NT)

        def attention_pe(pe, a, scores, v):
            n, b = a.heads, a.base
            for j in range(n + 2):
                if j < n:
                    if j >= 2:
                        pe.wait_ge(AT.maxed, b + j - 1)
                    scores(j, ps[4 + j % 2]).then_inc(AT.scores, 1)
                h = j - 1
                if 0 <= h < n:
                    pe.wait_ge(AT.exps, b + h + 1)
                    if h >= 2:
                        pe.wait_ge(AT.copied, b + h - 1)
                    for c in range(3):
                        mm = pe.transpose(ps[6 + h % 2][:, c * P:c * P + P], a.S[:, h % 3, c * P:c * P + P], ident)
                    mm.then_inc(AT.turned, 1)
                h = j - 2
                if h >= 0:
                    pe.wait_ge(AT.copied, b + h + 1)
                    pt, c = a.PT[:, h % 2, :], h // a.share * P
                    o = [ACC[t][c // 512][:, c % 512:c % 512 + P] for t in range(NT)]
                    first, last = h % a.share == 0, h % a.share == a.share - 1
                    pe.matmul(o[0], pt[:, 0:P], v(h, 0), start=first, stop=last)
                    pe.matmul(o[1], pt[:, P:SEQ], v(h, 0), start=first, stop=False)
                    pe.matmul(o[1], pt[:, SEQ:384], v(h, 1), start=False, stop=last).then_inc(AT.outs, 1)

        def attention_act(act, a, extra):
            n, b = a.heads, a.base
            for j in range(n + 1):
                if j < n:
                    act.wait_ge(AT.maxed, b + j + 1)
                    for t in range(NT):
                        ins = act.activation(a.S[:, j % 3, PARTS[t]], a.S[:, j % 3, PARTS[t]], ACT.Exp,
                                             bias=att(0, n)[:, j, t:t + 1], accum_out=att(1, n)[:, j, t:t + 1])
                    ins.then_inc(AT.exps, 1)
                h = j - 1
                if h >= 0:
                    act.wait_ge(AT.turned, b + h + 1)
                    if h >= 2:
                        act.wait_ge(AT.outs, b + h - 1)
                    act.activation(a.PT[:, h % 2, :], ps[6 + h % 2][:, 0:384], ACT.Copy).then_inc(AT.copied, 1)
                if j == n // 2 + 1:
                    extra(0)
            extra(1)

        def attention_dve(dve, a, bias, least, extra):
            n, b = a.heads, a.base
            for j in range(n):
                dve.wait_ge(AT.scores, b + j + 1)
                if j >= 3:
                    dve.wait_ge(AT.turned, b + j - 2)
                for t in range(NT):
                    ins = dve.tensor_tensor_reduce(a.S[:, j % 3, PARTS[t]], ps[4 + j % 2][:, PARTS[t]], bias(j, t),
                                                   1.0, least(j), ALU.add, ALU.max,
                                                   accum_out=att(2, n)[:, j, t:t + 1])
                dve_link(ins)
                dve.tensor_scalar(att(0, n)[:, j, :], att(2, n)[:, j, :], -1.0, None, ALU.mult).then_inc(AT.maxed, 1)
                if j == n // 2 + 2:
                    attention_finish(dve, a, extra, 0)
            attention_finish(dve, a, extra, 1)

        def attention_finish(dve, a, extra, half):
            n, b, hs = a.heads, a.base, a.heads // 2
            own = slice(half * hs, half * hs + hs)
            dve.wait_ge(AT.exps, b + hs * (half + 1))
            extra(half)
            dve_link(dve.reciprocal(att(3, n)[:, own, :], att(1, n)[:, own, :]))
            dve.wait_ge(AT.outs, b + hs * (half + 1))
            for t in range(NT):
                dve.tensor_tensor(
                    a.AO[:, t, half * 512:half * 512 + 512].rearrange("p (h c) -> p h c", h=hs),
                    ACC[t][half].rearrange("p (h c) -> p h c", h=hs),
                    att(3, n)[:, own, t:t + 1].broadcast_to([P, hs, a.width]), ALU.mult).then_inc(TR.ready, 1)

        SW = sems("swa", "bias row_final row_b cleared copied resid")

        def swa_load(act):
            act.wait_ge(IN.band_out, 16)
            skewed = bass.AP(tensor=band_scratch.tensor, offset=band_scratch.offset + P - 1,
                             ap=[[BANDX, P], [P * 384, AH], [1, SEQ]])
            act.dma_start(bias_, skewed).then_inc(SW.bias, 16)
            act.dma_start(posi, positions.broadcast_to([P, SEQ])).then_inc(IN.pos, 16)
            act.dma_start(row_final, rows["final"].broadcast_to([P, D])).then_inc(SW.row_final, 16)
            act.dma_start(row_b_a2, rows["b_a2"].broadcast_to([P, 512])).then_inc(SW.row_b, 16)

        def swa_pe(pe):
            for b in range(2):
                weights_still(pe, unit(BASE["kv"] + b), [ps[b][:, 0:SEQ]], KD, 0, None if b else split_of("b"))
            for k in range(2):
                tokens_still(pe, unit(BASE["kv"] + 2 + k), [[ps[4][:, 0:SEQ]], [ps[5][:, 0:SEQ]]],
                             [4 * k + i for i in range(4)], SEQ, xhi, xlo, k == 0, k == 1)
            pe.wait_ge(TR.lo, TB["b"].done)
            for b in range(8):
                if b >= 2:
                    pe.wait_ge(SW.copied, b + 1 if b >= 4 else b - 1)
                weights_still(pe, unit(BASE["wq"] + b), [ps[(2 + b) % 4][:, 0:SEQ]], KD, 8)

            def scores(j, bank):
                half = slice(j % 2 * AHD, j % 2 * AHD + AHD)
                q, k = QT[half, j // 2, :], KT[half, j // 8, :]
                pe.matmul(bank[:, 0:P], q[:, 0:P], k[:, 0:P], start=True, stop=True)
                return pe.matmul(bank[:, P:384], q[:, P:SEQ], k, start=True, stop=True)

            def v(j, t):
                return VN[:, t, j // 8 * 2 + j % 2, :]

            pe.wait_ge(SW.copied, 12)
            attention_pe(pe, swa, scores, v)
            turn_pe(pe, "attn", swa.AO, 4)
            for k in range(KD):
                pe.wait_ge(TR.lo, split_of("attn")(k))
                tokens_still(pe, unit(BASE["wo"] + k), ACC, [k], 512, xhi, xlo, k == 0, k == KD - 1)

        def swa_act(act):
            def copy(last, dst, bank, scale=1.0):
                act.wait_ge(unit_done, last + 1)
                act.activation(dst, ps[bank][:, 0:SEQ], ACT.Copy, scale=scale).then_inc(SW.copied, 1)

            for b in range(2):
                copy(BASE["kv"] + b, KT[:, b, :], b)
                refill(act, BASE["kv"] + b)
            refill(act, BASE["kv"] + 2)
            for t in range(NT):
                act.wait_ge(unit_done, BASE["kv"] + 4)
                act.wait_ge(SW.cleared, 1)
                for half in range(2):
                    ins = act.activation(
                        VN[:, t].rearrange("p (g two) c -> p g two c", two=2)[:, :, half, half * AHD:half * AHD + AHD],
                        ps[4 + t][:, 0:SEQ].rearrange("p (g two c) -> p g two c", g=2, two=2)[:, :, half, :], ACT.Copy)
                ins.then_inc(SW.copied, 1)
            refill(act, BASE["kv"] + 3)
            for b in range(8):
                copy(BASE["wq"] + b, QT[:, b, :], (2 + b) % 4, AHD ** -0.5)
                refill(act, BASE["wq"] + b)

            def sink_exps(half):
                own = att(2, AH)[:, half * 8:half * 8 + 8, :]
                act.wait_ge(AT.sunk, half + 1)
                act.activation(own, own, ACT.Exp).then_inc(AT.total, 1)

            attention_act(act, swa, sink_exps)
            turn_act(act, "attn")
            for k in range(KD):
                refill(act, BASE["wo"] + k)

        def swa_clear(dve):
            dve.memset(VN, 0.0).then_inc(SW.cleared, 1)

        def swa_dve(dve):
            sinks = small[:, 32:48]
            dve.wait_ge(SW.bias, 16)

            def sink_terms(half):
                own = slice(half * 8, half * 8 + 8)
                dve.tensor_tensor(att(2, AH)[:, own, :], att(0, AH)[:, own, :],
                                  sinks[:, own].unsqueeze(2).broadcast_to([P, 8, NT]), ALU.add).then_inc(AT.sunk, 1)
                dve.wait_ge(AT.total, half + 1)
                sums = att(1, AH)[:, own, :]
                dve_link(dve.tensor_tensor(sums, sums, att(2, AH)[:, own, :], ALU.add))

            attention_dve(dve, swa, lambda j, t: bias_[:, j, (P, 0)[t]:SEQ], lambda j: sinks[:, j:j + 1], sink_terms)
            turn_dve(dve, "attn")
            add_residual(dve, BASE["wo"] + KD - 1, SW.resid)
        MX = sems("mix", "w_a2 row_gate row_post row_ffn copied la_made la_x la_ln la suffix decays kdec "
                  "c_squares c_ready c_turned c_hi c_lo gates_in sigmoid kv state o o_squares up_copied "
                  "rope_made roped ya_used")
        GV, _o = carve(0, NT, D)
        GK, _o = carve(_o, NT, 512)
        GQT, _o = carve(_o, GH, SEQ)
        LA, _s1 = carve(_o, NT, 512)
        ST, _o = carve(_o, 2, GH * GDV)
        GG, _o = carve(_o, NT, D)
        GA, _o = carve(_o, NT, D)
        GB, _o = carve(_o, NT, D)
        OG, _t = carve(_o, NT, D)
        LT, _t = carve(_o, NT, 512)
        LX, _t = carve(_t, NT, 512)
        CQ, _o = carve(_t, NT, QL)
        CKV, _o = carve(_o, NT, KVL)
        XB, _o = carve(_o, SEQ)
        QN, _t = carve(0, MH, SEQ)
        KN, _t = carve(_t, MH, SEQ)
        VM, _t = carve(_t, NT, D)
        row_post, _t = carve(14336, D)
        row_ffn, _t = carve(_t, D)
        QP, _t = carve(16384, 4, SEQ)
        W_A2, _t = carve(17408, 512)
        KP, _t = carve(17920, SEQ)
        mla = Named(heads=MH, width=P, share=1, base=AH, S=swa.S, PT=swa.PT, AO=carve(6144, NT, D)[0])
        DC = att_stat[:, 0:16]
        OSQ, CSQ = att_stat[:, 32:48], att_stat[:, 64:72]
        CHUNKS = ("gk0", "gv0", "gv1", "gg0", "gg1", "gates0", "gates1", "gates2", "gates3")

        def block2_pe(pe):
            turn_pe(pe, "mix", scr, TWO_NORMS_WAIT, SHORT_WAIT, SHORT_WAIT)
            for k in range(4):
                pe.wait_ge(TR.lo, split_of("mix")(2 * k + 1))
                tokens_still(pe, unit(BASE["cq"] + k), [[ps[t][:, 0:QL]] for t in range(NT)], [2 * k, 2 * k + 1],
                             QL, xhi, xlo, k == 0, k == 3)
            for k in range(2):
                tokens_still(pe, unit(BASE["ckv"] + k), [[ps[2 + t][:, 0:KVL]] for t in range(NT)],
                             [4 * k + i for i in range(4)], KVL, xhi, xlo, k == 0, k == 1)
            weights_still(pe, unit(BASE["x"]), [ps[4][:, 0:SEQ]], KD, 0)
            for h in range(GH):
                if h == 3:
                    pe.wait_ge(MX.copied, 5)
                weights_still(pe, unit(BASE["gq"] + h), [ps[(5, 6, 7, 4)[h]][:, 0:SEQ]], KD, 0)
            pe.wait_ge(MX.w_a2, 16)
            pe.wait_ge(MX.copied, 7)
            for t in range(NT):
                mm = pe.matmul(ps[5 + t][:], XB[0:16, t * P:t * P + P], W_A2[0:16, :], start=True, stop=True)
            mm.then_inc(MX.la_made, 1)
            for c, name in enumerate(CHUNKS):
                pair = c % 2 * 2
                if c <= 6:
                    pe.wait_ge(MX.copied, (2, 4, 11, 13, 15, 17, 19)[c])
                else:
                    pe.wait_ge(MX.gates_in, 2 * (c - 6))
                for k in range(4):
                    tokens_still(pe, unit(BASE[name[:-1]] + int(name[-1]) * 4 + k), [[ps[pair][:]], [ps[pair + 1][:]]],
                                 [2 * k, 2 * k + 1], 512, xhi, xlo, k == 0, k == 3)
                if c == 0:
                    pe.wait_ge(MX.la, 1)
                    pe.wait_ge(MX.copied, 8)
                    for t in range(NT):
                        pe.matmul(ps[5 + t][:], tabv("later"), LA[:, t, :], start=True, stop=True)
                        for h in range(GH):
                            i = (t * GH + h) * 2
                            mm = pe.matmul(ps[7][:, i:i + 2], LA[:, t, h * P:h * P + P],
                                           col[:, COL["chunk_of"]:COL["chunk_of"] + 2], start=True, stop=True)
                    mm.then_inc(MX.suffix, 1)
                if c == 3:
                    pe.wait_ge(MX.c_ready, 1)
                    pe.wait_ge(MX.decays, 2)
                    pe.wait_ge(MX.copied, 9)
                    for bank, src, ks in ((4, CQ, (0, 1)), (5, CQ, (2,)), (6, CKV, (0, 1))):
                        for i, k in enumerate(ks):
                            for t in range(NT):
                                mm = pe.transpose(ps[bank][:, i * SEQ + t * P:i * SEQ + t * P + P],
                                                  src[:, t, k * P:k * P + P], ident)
                        mm.then_inc(MX.c_turned, 1)

            pe.wait_ge(MX.c_lo, 5)
            pe.wait_ge(MX.kdec, 1)
            pe.wait_ge(MX.gates_in, 8)
            for c in range(2 * NT + 1):
                if c < 2 * NT:
                    t, half = c // 2, slice(c % 2 * 64, c % 2 * 64 + 64)
                    if c >= 2:
                        pe.wait_ge(MX.state, c - 1)
                    for h in range(GH):
                        mm = pe.matmul(ps[4 + c % 2 * 2 + h // 2][:, h % 2 * GDV:h % 2 * GDV + GDV],
                                       GK[half, t, h * P:h * P + P], GV[half, t, h * GDV:h * GDV + GDV],
                                       start=True, stop=True)
                    mm.then_inc(MX.kv, 1)
                c -= 1
                if c >= 0:
                    t, half = c // 2, slice(c % 2 * 64, c % 2 * 64 + 64)
                    pe.wait_ge(MX.state, c + 1)
                    for h in range(GH):
                        mm = pe.matmul(ACC[t][h // 2][half, h % 2 * GDV:h % 2 * GDV + GDV],
                                       GQT[:, h, c * 64:c * 64 + 64], ST[:, c % 2, h * GDV:h * GDV + GDV],
                                       start=True, stop=True)
                    mm.then_inc(MX.o, 1)

            for i in range(6):
                if i >= 4:
                    pe.wait_ge(MX.up_copied, i - 3)
                b = ps[4 + i % 4]
                weights_still(pe, unit(BASE["uq"] + i), [b[:, 0:SEQ], b[:, SEQ:512]], 3, 8)
            for i in range(2):
                pe.wait_ge(MX.up_copied, 4 + 2 * i)
                banks = (ps[6], ps[7]) if i == 0 else (ps[4], ps[5])
                weights_still(pe, unit(BASE["kn"] + i), [b[:, c:c + SEQ] for b in banks for c in (0, SEQ)], 2, 11)
            pe.wait_ge(TR.ready, TB["gla"].ready + 4)
            for i in range(2):
                tokens_still(pe, unit(BASE["vm"] + i), ACC, [11 + i], 512, xhi, xlo, i == 0, i == 1)
            pe.wait_ge(MX.up_copied, 10)
            turn_pe(pe, "gla", OG)
            pe.wait_ge(MX.up_copied, 14)
            for k in range(KD):
                pe.wait_ge(TR.lo, split_of("gla")(k))
                tokens_still(pe, unit(BASE["ogla"] + k), ACC, [k], 512, xhi, xlo, k == 0, k == KD - 1)
                if k == 2:
                    pe.wait_ge(TR.lo, TB["gla"].done)
                    for i in range(2):
                        pe.matmul(ps[4 + i][:], tabv("swap"), QP[:, 2 * i:2 * i + 2, :], start=True, stop=True)
                    pe.matmul(ps[6][:, 0:SEQ], tabv("dup")[64:P, :], XB[64:P, :], start=True, stop=True)
                    pe.matmul(ps[6][:, SEQ:512], tabv("dup_swap")[64:P, :], XB[64:P, :], start=True,
                              stop=True).then_inc(MX.rope_made, 1)

            pe.wait_ge(MX.roped, 1)
            def scores(h, bank):
                half = slice(h % 2 * 64, h % 2 * 64 + 64)
                for q, keys, cols in ((slice(0, P), slice(0, P), slice(0, P)),
                                      (slice(P, SEQ), slice(0, SEQ), slice(P, 384))):
                    pe.matmul(bank[:, cols], QN[:, h, q], KN[:, h, keys], start=True, stop=False)
                    mm = pe.matmul(bank[:, cols], QP[half, h // 2, q], KP[half, keys], start=False, stop=True)
                return mm

            pe.wait_ge(MX.ya_used, 4)
            attention_pe(pe, mla, scores, lambda h, t: VM[:, t, h * P:h * P + P])
            turn_pe(pe, "mla", mla.AO, 4)
            for k in range(KD):
                pe.wait_ge(TR.lo, split_of("mla")(k))
                tokens_still(pe, unit(BASE["omla"] + k), ACC, [8 + k], 512, xhi, xlo, k == 0, k == KD - 1,
                             halves_first=True)
            turn_pe(pe, "mixed", GA, 10, 0, 4)
            for k in range(KD):
                pe.wait_ge(TR.lo, split_of("mixed")(k))
                tokens_still(pe, unit(BASE["w2"] + k), ACC, [k], 512, xhi, xlo, k == 0, k == KD - 1)
            turn_pe(pe, "ffn2", scr, TWO_NORMS_WAIT, SHORT_WAIT, SHORT_WAIT)
            ffn_pe(pe, 2, False)

        def block2_act(act):
            def copy(last, dst, bank, func=ACT.Copy, scale=1.0, done=MX.copied):
                act.wait_ge(unit_done, last + 1)
                act.activation(dst, bank, func, scale=scale).then_inc(done, 1)

            act.wait_ge(FS[1].resid, 1)
            act.dma_start(W_A2[0:16, :], w_a2).then_inc(MX.w_a2, 16)
            norm_act(act, "final", FS[1].resid, lambda t, h: 2 * t + h + 1)
            norm_act(act, "mix", rescaled, lambda t, h: 2 * t + h + 1)
            turn_act(act, "mix")
            act.dma_start(scr[:].rearrange("p t c -> p (t c)"),
                          rows["b_gate"].broadcast_to([P, 2 * D])).then_inc(MX.row_gate, 16)
            for name, n, dst, b0, width in (("cq", 4, CQ, 0, QL), ("ckv", 2, CKV, 2, KVL)):
                for k in range(n - 1):
                    refill(act, BASE[name] + k)
                for t in range(NT):
                    copy(BASE[name] + n - 1, dst[:, t, :], ps[b0 + t][:, 0:width])
                refill(act, BASE[name] + n - 1)
            copy(BASE["x"], XB, ps[4][:, 0:SEQ])
            refill(act, BASE["x"])
            for h in range(GH):
                copy(BASE["gq"] + h, GQT[:, h, :], ps[(5, 6, 7, 4)[h]][:, 0:SEQ], scale=float(P) ** -0.5)
                refill(act, BASE["gq"] + h)
            act.wait_ge(MX.copied, 4)
            for i, (src, width) in enumerate(((CQ, QL), (CKV, KVL))):
                for t in range(NT):
                    act.activation(LX[:, t, 0:width], src[:, t, :], ACT.Square,
                                   accum_out=CSQ[:, 2 * i + t:2 * i + t + 1]).then_inc(MX.c_squares, 1)
                act.wait_ge(MX.c_squares, 2 * i + 2)
            act.wait_ge(MX.la_x, 1)
            act_link(act.activation(LT, LA, ACT.Abs))
            act_link(act.activation(LT, LT, ACT.Exp, scale=-1.0))
            act.activation(LT, LT, ACT.Ln, bias=ones[:, 0:1]).then_inc(MX.la_ln, 1)

            def chunk(c):
                name = CHUNKS[c]
                last = BASE[name[:-1]] + int(name[-1]) * 4 + 3
                for k in range(3, 0, -1):
                    refill(act, last - k)
                half = int(name[-1]) * 512
                dst, func = {"gk": (GK, ACT.Copy), "gv": (GV, ACT.Copy), "gg": (GG, ACT.Silu)}.get(name[:-1], (None, None))
                if dst is not None:
                    for t in range(NT):
                        copy(last, dst[:, t, half:half + 512], ps[c % 2 * 2 + t][:], func)
                refill(act, last)

            chunk(0)
            act.wait_ge(MX.suffix, 1)
            for t in range(NT):
                ins = act.activation(LX[:, t, :], ps[5 + t][:], ACT.Exp, scale=1.0 / 16.0)
            ins.then_inc(MX.decays, 1)
            act.activation(DC, ps[7][:, 0:16], ACT.Exp, scale=1.0 / 16.0).then_inc(MX.decays, 1)
            chunk(1)
            chunk(2)
            chunk(3)
            for n, (bank, name, ks, slot) in enumerate(((4, "q_norm", (0, 1), 8), (5, "q_norm", (2,), 10),
                                                        (6, "kv2_norm", (0, 1), 11))):
                act.wait_ge(MX.c_turned, n + 1)
                for i, k in enumerate(ks):
                    act.activation(xhi[:, slot + i, :], ps[bank][:, i * SEQ:i * SEQ + SEQ], ACT.Copy,
                                   scale=colv(name, k)).then_inc(MX.c_hi, 1)
            for c in range(4, 9):
                chunk(c)
            act.wait_ge(MX.gates_in, 8)
            for g in (GA, GB):
                act.activation(g, g, ACT.Sigmoid).then_inc(MX.sigmoid, 1)
            for h in range(NT * GH):
                if h % GH == 0:
                    act.wait_ge(MX.o, 2 * (h // GH) + 2)
                t, q = h // GH, h % GH
                act.activation(scr[:, t, q * GDV:q * GDV + GDV], ACC[t][q // 2][:, q % 2 * GDV:q % 2 * GDV + GDV],
                               ACT.Square, accum_out=OSQ[:, h:h + 1]).then_inc(MX.o_squares, 1)
            for i in range(6):
                dst = QN[:, 2 * i:2 * i + 2, :] if i < 4 else QP[:, 2 * i - 8:2 * i - 6, :]
                copy(BASE["uq"] + i, dst, ps[4 + i % 4][:].rearrange("p (a b) -> p a b", a=2), scale=192.0 ** -0.5, done=MX.up_copied)
                refill(act, BASE["uq"] + i)
            for i in range(4):
                copy(BASE["kn"] + i // 2, KN[:, 2 * i:2 * i + 2, :],
                     ps[(6, 7, 4, 5)[i]][:].rearrange("p (a b) -> p a b", a=2), done=MX.up_copied)
                if i % 2:
                    refill(act, BASE["kn"] + i // 2)
            refill(act, BASE["vm"])
            for i in range(4):
                copy(BASE["vm"] + 1, VM[:, i // 2, i % 2 * 512:i % 2 * 512 + 512], ACC[i // 2][i % 2], done=MX.up_copied)
            refill(act, BASE["vm"] + 1)
            turn_act(act, "gla")
            for k in range(KD):
                refill(act, BASE["ogla"] + k)
            act.wait_ge(MX.rope_made, 1)
            act.dma_start(row_post, rows["post_mix"].broadcast_to([P, D])).then_inc(MX.row_post, 16)
            act.dma_start(row_ffn, rows["post_ffn"].broadcast_to([P, D])).then_inc(MX.row_ffn, 16)
            attention_act(act, mla, lambda half: None)
            turn_act(act, "mla")
            for k in range(KD):
                refill(act, BASE["omla"] + k)
            turn_act(act, "mixed")
            for k in range(KD):
                refill(act, BASE["w2"] + k)
            norm_act(act, "post_mix", unit_done, lambda t, h: BASE["ffn2"], ACC)
            norm_act(act, "ffn2", rescaled, lambda t, h: 5 + 2 * t + h)
            turn_act(act, "ffn2")
            ffn_act(act, 2, False)
            norm_act(act, "post_ffn", unit_done, lambda t, h: UNITS, ACC)

        def block2_dve(dve):
            dve.wait_ge(SW.row_final, 16)
            norm_dve(dve, "final", row_final)
            norm_dve(dve, "mix")
            turn_dve(dve, "mix")
            dve.wait_ge(MX.la_made, 1)
            dve.wait_ge(SW.row_b, 16)
            for t in range(NT):
                ins = dve.tensor_tensor(LA[:, t, :], ps[5 + t][:], row_b_a2, ALU.add)
            ins.then_inc(MX.la_x, 1)
            dve.wait_ge(MX.la_ln, 1)
            dve.scalar_tensor_tensor(LA, LA, 0.0, LT, ALU.min, ALU.subtract).then_inc(MX.la, 1)
            dve.wait_ge(MX.c_squares, 4)
            for i, (src, width) in enumerate(((CQ, QL), (CKV, KVL))):
                ss, r = CSQ[:, 2 * i:2 * i + 2], CSQ[:, 4 + 2 * i:6 + 2 * i]
                inverse_root(dve, r, ss, width, EPS, root_tmp[:, 0:2])
                for t in range(NT):
                    ins = dve.tensor_scalar(src[:, t, :], src[:, t, :], r[:, t:t + 1], None, ALU.mult)
            ins.then_inc(MX.c_ready, 1)
            dve.wait_ge(MX.decays, 1)
            dve.wait_ge(MX.copied, 11)
            dve.tensor_tensor(GK, GK, LX, ALU.mult).then_inc(MX.kdec, 1)
            n = 0
            for bank, name, ks, slot in ((4, "q_norm", (0, 1), 8), (5, "q_norm", (2,), 10), (6, "kv2_norm", (0, 1), 11)):
                n += len(ks)
                dve.wait_ge(MX.c_hi, n)
                for i, k in enumerate(ks):
                    dve.scalar_tensor_tensor(xlo[:, slot + i, :], ps[bank][:, i * SEQ:i * SEQ + SEQ], colv(name, k),
                                             xhi[:, slot + i, :].bitcast(F32), ALU.mult, ALU.subtract).then_inc(MX.c_lo, 1)
            dve.wait_ge(MX.row_gate, 16)
            for c in range(4):
                dve.wait_ge(unit_done, BASE["gates"] + 4 * c + 4)
                for t in range(NT):
                    dve.tensor_tensor((GA, GB)[c // 2][:, t, c % 2 * 512:c % 2 * 512 + 512],
                                      ps[(c + 1) % 2 * 2 + t][:], scr[:, c // 2, c % 2 * 512:c % 2 * 512 + 512],
                                      ALU.add).then_inc(MX.gates_in, 1)
            dve.wait_ge(MX.decays, 2)
            for c in range(2 * NT):
                dve.wait_ge(MX.kv, c + 1)
                if c >= 2:
                    dve.wait_ge(MX.o, c - 1)
                if c:
                    dve.wait_ge(MX.state, c)
                for h in range(GH):
                    new, old = (ST[:, i % 2, h * GDV:h * GDV + GDV] for i in (c, c + 1))
                    kv = ps[4 + c % 2 * 2 + h // 2][:, h % 2 * GDV:h % 2 * GDV + GDV]
                    i = (c // 2 * GH + h) * 2 + c % 2
                    if c == 0:
                        ins = dve.tensor_copy(new, kv)
                    else:
                        ins = dve.scalar_tensor_tensor(new, old, DC[:, i:i + 1], kv, ALU.mult, ALU.add)
                ins.then_inc(MX.state, 1)
            dve.wait_ge(MX.o_squares, 8)
            inverse_root(dve, OSQ[:, 8:16], OSQ[:, 0:8], GDV, EPS, root_tmp[:, 0:8])
            for half in range(2):
                for t in range(NT):
                    i = 8 + t * GH + half * 2
                    o = OG[:, t, half * 512:half * 512 + 512]
                    dve_link(dve.tensor_tensor(o.rearrange("p (h c) -> p h c", h=2),
                                               ACC[t][half].rearrange("p (h c) -> p h c", h=2),
                                               OSQ[:, i:i + 2].unsqueeze(2).broadcast_to([P, 2, GDV]), ALU.mult))
                    dve.tensor_tensor(o, o, GG[:, t, half * 512:half * 512 + 512], ALU.mult).then_inc(TR.ready, 1)
            turn_dve(dve, "gla")
            dve.wait_ge(MX.rope_made, 1)
            dve.wait_ge(IN.rope, 1)
            dve.wait_ge(IN.sin, 2)
            part = scr[:, 0, :].rearrange("p (a b) -> p a b", a=4)
            kpart = scr[:, 1, 0:SEQ]
            for i in range(2):
                dve.tensor_tensor(part[:, 2 * i:2 * i + 2, :], ps[4 + i][:].rearrange("p (a b) -> p a b", a=2),
                                  sinT[:].unsqueeze(1).broadcast_to([P, 2, SEQ]), ALU.mult)
            dve.tensor_tensor(QP, QP, cosT[:].unsqueeze(1).broadcast_to([P, 4, SEQ]), ALU.mult)
            dve.tensor_tensor(kpart, ps[6][:, SEQ:512], sinT[:], ALU.mult)
            dve_link(dve.tensor_tensor(KP, ps[6][:, 0:SEQ], cosT[:], ALU.mult))
            dve.tensor_tensor(QP, QP, part, ALU.add)
            dve.tensor_tensor(KP, KP, kpart, ALU.add).then_inc(MX.roped, 1)
            dve.wait_ge(MX.sigmoid, 2)
            dve.wait_ge(unit_done, BASE["ogla"] + KD)
            for t in range(NT):
                for half in range(2):
                    g = GA[:, t, half * 512:half * 512 + 512]
                    dve.tensor_tensor(g, g, ACC[t][half], ALU.mult).then_inc(MX.ya_used, 1)
            mask = tabv("chunk_mask")
            attention_dve(dve, mla, lambda h, t: mask[:, PARTS[t]], lambda h: -BIG, lambda half: None)
            turn_dve(dve, "mla")
            dve.wait_ge(unit_done, BASE["omla"] + KD)
            dve.wait_ge(MX.ya_used, 4)
            for half in range(2):
                for t in range(NT):
                    a, b = (g[:, t, half * 512:half * 512 + 512] for g in (GA, GB))
                    dve_link(dve.tensor_tensor(b, b, ACC[t][half], ALU.mult))
                    dve.tensor_tensor(a, a, b, ALU.add).then_inc(TR.ready, 1)
            turn_dve(dve, "mixed")
            dve.wait_ge(MX.row_post, 16)
            norm_dve(dve, "post_mix", row_post, ACC)
            norm_dve(dve, "ffn2")
            turn_dve(dve, "ffn2")
            ffn_dve(dve, 2, False)
            dve.wait_ge(MX.row_ffn, 16)
            norm_dve(dve, "post_ffn", row_ffn, ACC)
        IN = sems("in", "tabs ident cols small pos rel x0 x1 band_ps band band_out sin scaled rope angle")
        rel = sb("rel", [P, 16])
        band = sb("band", [P, 384])
        ang, _o = carve(12288, SEQ)
        turns, _o = carve(_o, SEQ)
        posi = area[:, _o:_o + SEQ].bitcast(I32)

        def load_x(sp):
            sp.dma_start(resid[:, 0, :], x[0:P, :]).then_inc(IN.x0, 16)
            sp.dma_start(resid[:, 1, :], x[P:SEQ, :]).then_inc(IN.x1, 16)

        def load_parameters(act):
            act.dma_start(tab[:, 0:512], tabs[:, 0:512]).then_inc(IN.ident, 16)
            act.dma_start(col[:], cols).then_inc(IN.cols, 16)
            act.dma_start(rel[0:32, :], rel_table).then_inc(IN.rel, 16)
            act.dma_start(small[:], rows["small"].broadcast_to([P, 48])).then_inc(IN.small, 16)

        def band_out(act):
            act.wait_ge(IN.band, 1)
            act.dma_start(band_scratch, band[0:16, :].unsqueeze(1).broadcast_to([16, P, 384])).then_inc(IN.band_out, 16)

        def rope_act(act):
            for n, dst in enumerate((sinT, cosT)):
                act.wait_ge(IN.angle, n + 1)
                act.activation(dst[:], dst[:], ACT.Sin).then_inc(IN.sin, 1)

        def start_pe(pe):
            pe.wait_ge(IN.ident, 16)
            pe.wait_ge(IN.rel, 16)
            pe.wait_ge(IN.scaled, 1)
            pe.matmul(ps[1][0:16, 0:BANDX], rel[0:33, :], tabv("buckets")[0:33, 0:BANDX], start=True,
                      stop=True).then_inc(IN.band_ps, 1)

        def start_dve(dve):
            dve.memset(rel[32:33, :], -BIG).then_inc(IN.scaled, 1)
            dve_link(dve.memset(band[0:16, :], 0.0))
            dve.wait_ge(IN.band_ps, 1)
            dve.tensor_copy(band[0:16, 0:BANDX], ps[1][0:16, 0:BANDX]).then_inc(IN.band, 1)
            dve.wait_ge(IN.cols, 16)

        def rope_dve(dve):
            dve.wait_ge(IN.pos, 16)
            dve_link(dve.tensor_copy(ang, posi))
            dve_link(dve.tensor_scalar(ang, ang, colv("inv_freq"), None, ALU.mult))
            c1, c2 = 6.28125, float(np.float32(int((2 * np.pi - 6.28125) * 2 ** 20) / 2 ** 20))
            c3 = float(2 * np.pi - c1 - c2)
            magic = 1.5 * 2.0 ** 23
            for dst, quarter in ((sinT, 0.0), (cosT, 0.25)):
                dve_link(dve.tensor_scalar(turns, ang, float(0.5 / np.pi), quarter, ALU.mult, ALU.add))
                dve_link(dve.tensor_scalar(turns, turns, magic, -magic, ALU.add, ALU.add))
                dve_link(dve.scalar_tensor_tensor(dst[:], turns, -c1, ang, ALU.mult, ALU.add))
                dve_link(dve.scalar_tensor_tensor(dst[:], turns, -c2, dst[:], ALU.mult, ALU.add))
                dve_link(dve.scalar_tensor_tensor(dst[:], turns, -c3, dst[:], ALU.mult, ALU.add))
                dve_link(dve.tensor_scalar(dst[:], dst[:], quarter * 2 * np.pi, float(np.float32(3.1415925)), ALU.add, ALU.min))
                dve.tensor_scalar(dst[:], dst[:], -float(np.float32(3.1415925)), None, ALU.max).then_inc(IN.angle, 1)
            dve.wait_ge(IN.sin, 1)
            dve.tensor_scalar(sinT[:], sinT[:], colv("rope_sign"), None, ALU.mult).then_inc(IN.rope, 1)
        out_done = sem("out_done")
        block = ctx.enter_context(nc.Block())

        @block.sync
        def _(sp):
            load_x(sp)
            for k in range(RING):
                load_unit(sp, unit(k))
            with sp.Fori(1, UNITS // RING) as i:
                for k in range(RING):
                    load_unit(sp, unit(k, i))
            for k in range(UNITS // RING * RING, UNITS):
                load_unit(sp, unit(k))
            for t in range(NT):
                sp.wait_ge(rescaled, 4 * NT + 2 * t + 2)
                sp.dma_start(out[t * P:t * P + P, :], resid[:, t, :]).then_inc(out_done, 16)
            sp.wait_ge(out_done, 16 * NT)

        @block.gpsimd
        def _(pool):
            for k in range(RING):
                rest_of_unit(pool, unit(k))
            with pool.Fori(1, UNITS // RING) as i:
                for k in range(RING):
                    rest_of_unit(pool, unit(k, i))
            for k in range(UNITS // RING * RING, UNITS):
                rest_of_unit(pool, unit(k))

        @block.scalar
        def _(act):
            load_parameters(act)
            act.wait_ge(IN.x0, 16)
            norm_act(act, "a", IN.x1, lambda t, h: 16)
            round_unit(act, unit(0))
            round_unit(act, unit(1))
            act.dma_start(tab[:, 512:NTABS], tabs[:, 512:NTABS]).then_inc(IN.tabs, 16)
            act.wait_ge(IN.cols, 16)
            turn_act(act, "a")
            for k in range(2, RING):
                round_unit(act, unit(k))
            gates_copy(act)
            qkv_act(act)
            band_out(act)
            delta_act(act)
            act.wait_ge(DN.resid, 1)
            swa_load(act)
            norm_act(act, "ffn0", DN.resid, lambda t, h: 2 * t + h + 1)
            turn_act(act, "ffn0")
            rope_act(act)
            ffn_act(act, 0, True)
            norm_act(act, "b", FS[0].resid, lambda t, h: 2 * t + h + 1)
            turn_act(act, "b")
            swa_act(act)
            norm_act(act, "ffn1", SW.resid, lambda t, h: 2 * t + h + 1)
            turn_act(act, "ffn1")
            ffn_act(act, 1, True)
            block2_act(act)

        @block.tensor
        def _(pe):
            start_pe(pe)
            turn_pe(pe, "a", scr, 0, SHORT_WAIT, SHORT_WAIT)
            qkv_pe(pe)
            delta_pe(pe)
            turn_pe(pe, "ffn0", scr, NORM_WAIT, SHORT_WAIT, SHORT_WAIT)
            ffn_pe(pe, 0, True)
            turn_pe(pe, "b", scr, NORM_WAIT, SHORT_WAIT, SHORT_WAIT)
            swa_pe(pe)
            turn_pe(pe, "ffn1", scr, NORM_WAIT, SHORT_WAIT, SHORT_WAIT)
            ffn_pe(pe, 1, True)
            block2_pe(pe)

        @block.vector
        def _(dve):
            start_dve(dve)
            norm_dve(dve, "a")
            turn_dve(dve, "a")
            qkv_dve(dve)
            delta_dve(dve)
            norm_dve(dve, "ffn0")
            turn_dve(dve, "ffn0")
            rope_dve(dve)
            ffn_dve(dve, 0, True)
            swa_clear(dve)
            add_residual(dve, BASE["kv"] - 1, FS[0].resid)
            norm_dve(dve, "b")
            turn_dve(dve, "b")
            swa_dve(dve)
            norm_dve(dve, "ffn1")
            turn_dve(dve, "ffn1")
            ffn_dve(dve, 1, True)
            add_residual(dve, BASE["cq"] - 1, FS[1].resid)
            block2_dve(dve)




def t5_buckets(dist):
    n = np.maximum(dist, 0)
    nf = np.maximum(n, 1).astype(np.float32)
    scale = np.float32(np.log(128 / 16))
    large = 16 + (np.log(nf / np.float32(16)) / scale * np.float32(16)).astype(np.int32)
    return np.where(n < 16, n, np.minimum(large, 31))


def tables():
    i, j = np.arange(P)[:, None], np.arange(P)[None, :]
    t = {"ident": i == j, "ones": np.ones((P, P)), "tri": i <= j,
         "future": np.where(j >= i, 0.0, -BIG), "later": (i > j) & (i // 64 == j // 64),
         "swap": i == (j ^ 32), "dup": i == 64 + j % 64, "dup_swap": i == 64 + (j % 64 ^ 32)}
    levels = []
    for lv in range(LEVELS):
        s = 1 << lv
        left = np.array([c for c in range(P) if not c & s])[None, :]
        levels.append((i // (2 * s) == left // (2 * s)) & (i & s > 0))
    t["levels"] = np.concatenate(levels, 1)
    k = np.arange(SEQ)[None, :]
    t["chunk_mask"] = np.concatenate([np.where(j // 64 <= i // 64, 0.0, -BIG),
                                      np.where(k // 64 <= (P + i) // 64, 0.0, -BIG)], 1)
    off = np.arange(384)[None, :]
    dist = 255 - off
    inside = (dist >= 0) & (dist < 128)
    t["buckets"] = np.where(i < 32, inside & (t5_buckets(dist) == i), (i == 32) & ~inside)
    return np.concatenate([t[name].astype(np.float32) for name, _ in TABS], 1)


def still(w, blocks_per_unit=1, pad_to=UNIT):
    kt, nb = w.shape[0] // P, w.shape[1] // P
    u = w.reshape(kt, P, nb // blocks_per_unit, blocks_per_unit, P).transpose(2, 1, 3, 0, 4)
    u = u.reshape(u.shape[0], P, -1)
    return np.pad(u, ((0, 0), (0, 0), (0, pad_to - u.shape[2])))


def moving(w, kts, width):
    kt, nc_ = w.shape[0] // P, w.shape[1] // width
    u = w.reshape(kt // kts, kts, P, nc_, width).transpose(3, 0, 2, 1, 4).reshape(-1, P, kts * width)
    return np.pad(u, ((0, 0), (0, 0), (0, UNIT - u.shape[2])))


def ffn_units(up_gate, up_val, down):
    g, v, d = still(up_gate), still(up_val), moving(down, 1, D)
    order = [g[0], v[0], g[1], v[1], d[0]]
    for j in range(2, NF):
        order += [g[j], v[j], d[j - 1]]
    return np.stack(order + [d[NF - 1]])


def lay_out(a):
    f = {k: np.asarray(v) for k, v in a.items()}
    w_in = f["a_w_in"][0]
    k_first = np.concatenate([w_in[:, 1024:2048], w_in[:, 0:1024], w_in[:, 2048:4096]], 1)
    heads_ = [4 * (2 * gp + half) + r for gp in range(2) for r in range(4) for half in range(2)]
    perm = np.concatenate([np.arange(h * AHD, h * AHD + AHD) for h in heads_])
    w2 = f["w_in_2"][0]
    cut = np.cumsum([0, 512, 512, 1024, 1024, 16, QL, KVL, 64])
    gq, gk, gv, gg, ga, cq, ckv, kpe = (w2[:, cut[i]:cut[i + 1]] for i in range(8))
    wx = np.concatenate([ga, np.zeros((D, 48), np.float32), kpe], 1)
    uq = f["w_uq_2"][0].reshape(QL, MH, 192)
    uq = np.concatenate([uq[:, :, :128].reshape(QL, 1024), uq[:, :, 128:].reshape(QL, 512)], 1)
    ukv = f["w_ukv_2"][0].reshape(KVL, MH, 256)
    up, down = f["ffn_w_up"], f["ffn_w_down"]
    w_ba = np.pad(w_in[:, 6144:6176], ((0, 0), (0, P - 32)))
    parts = {
        "ba": still(w_ba),
        "qkv": still(k_first), "z": moving(w_in[:, 4096:6144], 2, 512), "wout": moving(f["a_w_out"][0], 1, D),
        "ffn0": ffn_units(up[0][:, :FF], up[0][:, FF:], down[0]),
        "kv": np.concatenate([still(f["w_kv"][:, :256]), moving(f["w_kv"][:, 256:], 4, 256)]),
        "wq": still(f["b_w_q"][0][:, perm]), "wo": moving(f["b_w_o"][0][perm], 1, D),
        "ffn1": ffn_units(up[1][:, :FF], up[1][:, FF:], down[1]),
        "cq": moving(cq, 2, QL), "ckv": moving(ckv, 4, KVL), "x": still(wx), "gq": still(gq),
        "gk": moving(gk, 2, 512), "gv": moving(gv, 2, 512), "gg": moving(gg, 2, 512),
        "gates": moving(f["w_gate_2"][0], 2, 512), "uq": still(uq, 2),
        "kn": still(ukv[:, :, :128].reshape(KVL, 1024), 4), "vm": moving(ukv[:, :, 128:].reshape(KVL, 1024), 1, D),
        "ogla": moving(f["w_o_gla_2"][0], 1, D), "omla": moving(f["w_o_mla_2"][0], 1, D),
        "w2": moving(f["w_out_2"][0], 1, D),
        "ffn2": ffn_units(f["w_ffn_gate_2"][0], f["w_ffn_up_2"][0], f["w_ffn_down_2"][0]),
    }
    for name, n in PLAN:
        assert parts[name].shape == (n, P, UNIT), (name, parts[name].shape)
    stream = np.concatenate([parts[name] for name, _ in PLAN])

    def by_partition(v):
        return v.reshape(-1, P).T

    cw = f["a_conv_w"][0]
    cw = np.concatenate([cw[:, 1024:2048], cw[:, 0:1024], cw[:, 2048:]], 1)
    i = np.arange(P)
    inv_freq = (1.0 / (10000.0 ** (np.arange(0, 64, 2, dtype=np.float32) / np.float32(64)))).astype(np.float32)
    c = {
        "a_norm": by_partition(f["a_norm_w"][0]), "ffn0_norm": by_partition(f["ffn_norm_w"][0]),
        "kv_norm": by_partition(f["kv_norm_w"]), "b_norm": by_partition(f["b_norm_w"][0]),
        "ffn1_norm": by_partition(f["ffn_norm_w"][1]), "pre_mix": by_partition(f["pre_mix_norm_2"][0]),
        "pre_ffn": by_partition(f["pre_ffn_norm_2"][0]), "out_norm": by_partition(f["a_out_norm_w"][0]),
        "gla_norm": by_partition(f["gla_norm_2"][0]), "q_norm": by_partition(f["q_norm_2"][0]),
        "kv2_norm": by_partition(f["kv_norm_2"][0]), "conv_a": by_partition(cw),
        "conv0": by_partition(f["ffn_conv_w"][0]), "bias0": by_partition(f["ffn_conv_b"][0]),
        "conv1": by_partition(f["ffn_conv_w"][1]), "bias1": by_partition(f["ffn_conv_b"][1]),
        "left": np.stack([np.where(i & (1 << lv), 0.0, -1.0) for lv in range(LEVELS)], 1),
        "inv_freq": inv_freq[i % 32][:, None], "rope_sign": np.where(i % 64 < 32, -1.0, 1.0)[:, None],
        "chunk_of": np.stack([i // 64 == 0, i // 64 == 1], 1),
    }
    cols = np.concatenate([c[name].astype(np.float32) for name, _ in COLS], 1)
    r = {"small": np.concatenate([f["a_dt_bias"], f["a_a_log"], f["b_sinks"][:, heads_]], 1),
         "final": f["final_norm_w"][None], "b_gate": f["b_gate_2"], "b_a2": f["b_a2_2"],
         "post_mix": f["post_mix_norm_2"], "post_ffn": f["post_ffn_norm_2"]}
    arrays = {"x": f["x"][0], "stream": stream, "cols": cols, "tabs": tables(),
              "w_a2": f["w_a2_2"][0], "rel_table": f["rel_bias_table"][:, heads_], "positions": f["positions_2"]}
    arrays.update({"row_" + k: v for k, v in r.items()})
    return {k: np.ascontiguousarray(v) for k, v in arrays.items()}


def kernel(**inputs):
    import concourse.bacc as _bacc
    from concourse.bass_utils import run_bass_kernel_spmd as _run

    nc = _bacc.Bacc("TRN2", target_bir_lowering=False, num_devices=1, dynamic_dma_scratch_size=1024)
    arrays = {f"in_{k}": v for k, v in lay_out(inputs).items()}
    ap = {k: nc.dram_tensor(k, v.shape, mybir.dt.from_np(v.dtype), kind="ExternalInput").ap()
          for k, v in arrays.items()}
    out = nc.dram_tensor("out_0", (SEQ, D), F32, kind="ExternalOutput").ap()
    band_scratch = nc.dram_tensor("band_scratch", (AH, P, 384), F32).ap()
    rows = {k[7:]: v for k, v in ap.items() if k.startswith("in_row_")}
    build(nc, ap["in_x"], ap["in_stream"], ap["in_cols"], ap["in_tabs"], rows, ap["in_w_a2"],
          ap["in_rel_table"], ap["in_positions"], out, band_scratch)
    r = _run(nc, [arrays], core_ids=[0])
    return r.results[0]["out_0"].reshape(1, SEQ, D)
```
